# Optimizing a Trainium2 kernel written in Bass

```python
import math
import jax, jax.numpy as jnp
from jax import lax
import numpy as np
import jax
import jax.numpy as jnp

D_MODEL = 2048
BATCH = 1
SEQ = 256
DEPTH = 2

HEAD_DIM = 128
MIX_WIDTH = 2048
Q_BLOCK = 128
ROPE_THETA = 10000.0
EPS = 1e-6
MASKED = -1e30
FORCED = 1e9
NSA_HEADS = 8
NSA_KV_GROUPS = 2
NSA_CMP_LEN = 32
NSA_CMP_STRIDE = 16
NSA_CMP_HIDDEN = 256
NSA_SEL_LEN = 64
NSA_SEL_TOPN = 16
NSA_WINDOW = 512
DIFF_HEADS = 4
DIFF_QK_DIM = 64
DIFF_V_DIM = 128
DSA_HEADS = 12
DSA_KV_HEADS = 4
IDX_HEADS = 16
IDX_DIM = 64
DSA_TOPK_MAX = 256
MEM_HEADS = 4
MEM_LEN = 256

EVEN_SPLITS = (
    NSA_HEADS * HEAD_DIM,
    6 * NSA_KV_GROUPS * HEAD_DIM,
    NSA_HEADS * 3,
    NSA_HEADS * HEAD_DIM,
    DIFF_HEADS * 2 * DIFF_QK_DIM,
    DIFF_HEADS * 2 * DIFF_QK_DIM,
    DIFF_HEADS * DIFF_V_DIM,
    DIFF_HEADS * DIFF_V_DIM,
    MEM_HEADS * HEAD_DIM,
    MEM_HEADS * HEAD_DIM,
)
ODD_SPLITS = (
    DSA_HEADS * HEAD_DIM,
    DSA_KV_HEADS * HEAD_DIM,
    DSA_KV_HEADS * HEAD_DIM,
    IDX_HEADS * IDX_DIM,
    IDX_DIM,
    IDX_HEADS,
    DSA_HEADS * HEAD_DIM,
    MEM_HEADS * HEAD_DIM,
    MEM_HEADS * HEAD_DIM,
)
EVEN_IN = sum(EVEN_SPLITS)
ODD_IN = sum(ODD_SPLITS)


def rms_norm(x, gain):
    xf = x.astype(jnp.float32)
    y = xf * lax.rsqrt(jnp.mean(xf * xf, axis=-1, keepdims=True) + EPS)
    return (y * gain.astype(jnp.float32)).astype(x.dtype)

def rope(x, pos):
    half = x.shape[-1] // 2
    inv = ROPE_THETA ** (-jnp.arange(half, dtype=jnp.float32) / half)
    ang = pos.astype(jnp.float32)[:, None] * inv[None, :]
    cos = jnp.cos(ang)[:, None, :]
    sin = jnp.sin(ang)[:, None, :]
    xf = x.astype(jnp.float32)
    x1, x2 = xf[..., :half], xf[..., half:]
    return jnp.concatenate([x1 * cos - x2 * sin, x2 * cos + x1 * sin], axis=-1).astype(x.dtype)

def masked_softmax(scores, mask):
    s = jnp.where(mask, scores.astype(jnp.float32), MASKED)
    m = jnp.max(s, axis=-1, keepdims=True)
    e = jnp.exp(s - m) * mask
    return e / jnp.maximum(jnp.sum(e, axis=-1, keepdims=True), 1e-30)

def split_cols(h, sizes):
    return jnp.split(h, np.cumsum(sizes)[:-1].tolist(), axis=-1)

def unblock(y):
    y = jnp.moveaxis(y, 0, 1)
    return y.reshape((y.shape[0], y.shape[1] * y.shape[2]) + y.shape[3:])

def nsa_attention(q, kv, gate_logits, pos, cmp_pos, cmp_w1, cmp_w2, qk_gain):
    B, S, H, Dh = q.shape
    G = NSA_KV_GROUPS
    R = H // G
    scale = Dh ** -0.5
    n_cmp = (S - NSA_CMP_LEN) // NSA_CMP_STRIDE + 1
    n_sel = S // NSA_SEL_LEN
    top_n = min(NSA_SEL_TOPN, n_sel)
    cmp_start = np.arange(n_cmp) * NSA_CMP_STRIDE
    cmp_last = jnp.asarray(cmp_start + NSA_CMP_LEN - 1, dtype=jnp.int32)
    cmp_gather = cmp_start[:, None] + np.arange(NSA_CMP_LEN)[None, :]
    sel_start = np.arange(n_sel) * NSA_SEL_LEN
    ov = np.clip(np.minimum(cmp_start[:, None] + NSA_CMP_LEN, sel_start[None, :] + NSA_SEL_LEN)
                 - np.maximum(cmp_start[:, None], sel_start[None, :]), 0, None) / NSA_CMP_LEN
    overlap = jnp.asarray(ov, dtype=jnp.float32)

    qg = rope(rms_norm(q, qk_gain[0]), pos).reshape(B, S, G, R, Dh)
    k_c_raw, v_c_raw, k_s, v_s, k_w, v_w = [kv[:, :, j] for j in range(6)]

    def compress(t, pe, w1, w2):
        blk = t[:, cmp_gather] + pe[:, None, :]
        blk = blk.transpose(0, 1, 3, 2, 4).reshape(B, n_cmp, G, NSA_CMP_LEN * Dh)
        hid = jax.nn.silu(jnp.einsum('bcgf,fh->bcgh', blk, w1))
        return jnp.einsum('bcgh,hd->bcgd', hid, w2)

    k_c = rope(rms_norm(compress(k_c_raw, cmp_pos[0], cmp_w1[0], cmp_w2[0]), qk_gain[1]), cmp_last)
    v_c = compress(v_c_raw, cmp_pos[1], cmp_w1[1], cmp_w2[1])
    k_s = rope(rms_norm(k_s, qk_gain[2]), pos)
    k_w = rope(rms_norm(k_w, qk_gain[3]), pos)

    def to_blocks(t):
        return t.reshape(B, n_sel, NSA_SEL_LEN, G, Dh).transpose(0, 3, 1, 2, 4)

    k_s_blk, v_s_blk = to_blocks(k_s), to_blocks(v_s)
    pad = ((0, 0), (NSA_WINDOW, 0), (0, 0), (0, 0))
    k_w_pad, v_w_pad = jnp.pad(k_w, pad), jnp.pad(v_w, pad)
    gather_blocks = jax.vmap(jax.vmap(lambda tb, ii: tb[ii]))
    sel_ids = jnp.arange(n_sel)
    sel_off = jnp.arange(NSA_SEL_LEN)
    win_off = jnp.arange(NSA_WINDOW + Q_BLOCK)
    vdt = v_c.dtype

    def block(bi):
        q0 = bi * Q_BLOCK
        t = q0 + jnp.arange(Q_BLOCK)
        qb = lax.dynamic_slice_in_dim(qg, q0, Q_BLOCK, 1)
        p_c = masked_softmax(jnp.einsum('btgrd,bcgd->bgrtc', qb, k_c) * scale,
                             cmp_last[None, :] <= t[:, None])
        o_c = jnp.einsum('bgrtc,bcgd->btgrd', p_c.astype(vdt), v_c)
        imp = jnp.einsum('bgrtc,cj->bgtj', p_c, overlap)
        cur = t // NSA_SEL_LEN
        visible = sel_ids[None, :] <= cur[:, None]
        forced = (sel_ids[None, :] == 0) | (sel_ids[None, :] >= cur[:, None] - 1)
        imp = jnp.where(visible, jnp.where(forced, FORCED, imp), MASKED)
        _, idx = lax.top_k(imp, top_n)
        k_sel = gather_blocks(k_s_blk, idx).reshape(B, G, Q_BLOCK, top_n * NSA_SEL_LEN, Dh)
        v_sel = gather_blocks(v_s_blk, idx).reshape(B, G, Q_BLOCK, top_n * NSA_SEL_LEN, Dh)
        tok = (idx[..., None] * NSA_SEL_LEN + sel_off).reshape(B, G, Q_BLOCK, top_n * NSA_SEL_LEN)
        mask_s = (tok <= t[None, None, :, None])[:, :, None]
        p_s = masked_softmax(jnp.einsum('btgrd,bgtkd->bgrtk', qb, k_sel) * scale, mask_s)
        o_s = jnp.einsum('bgrtk,bgtkd->btgrd', p_s.astype(vdt), v_sel)
        kw = lax.dynamic_slice_in_dim(k_w_pad, q0, NSA_WINDOW + Q_BLOCK, 1)
        vw = lax.dynamic_slice_in_dim(v_w_pad, q0, NSA_WINDOW + Q_BLOCK, 1)
        s_pos = q0 - NSA_WINDOW + win_off
        mask_w = ((s_pos[None, :] <= t[:, None]) & (s_pos[None, :] > t[:, None] - NSA_WINDOW)
                  & (s_pos[None, :] >= 0))
        p_w = masked_softmax(jnp.einsum('btgrd,bkgd->bgrtk', qb, kw) * scale, mask_w)
        o_w = jnp.einsum('bgrtk,bkgd->btgrd', p_w.astype(vdt), vw)
        g = jax.nn.sigmoid(lax.dynamic_slice_in_dim(gate_logits, q0, Q_BLOCK, 1).astype(jnp.float32))
        g = g.astype(vdt).reshape(B, Q_BLOCK, G, R, 3)
        return g[..., 0:1] * o_c + g[..., 1:2] * o_s + g[..., 2:3] * o_w

    out = unblock(lax.map(block, jnp.arange(S // Q_BLOCK)))
    return out.reshape(B, S, H * Dh)

def diff_attention(q, k, v, pos, qk_gain, lam_vecs, subln_gain, lambda_init):
    B, S, H, _, dq = q.shape
    q = rope(rms_norm(q, qk_gain[0]).reshape(B, S, 2 * H, dq), pos).reshape(B, S, H, 2, dq)
    k = rope(rms_norm(k, qk_gain[1]).reshape(B, S, 2 * H, dq), pos).reshape(B, S, H, 2, dq)
    lv = lam_vecs.astype(jnp.float32)
    lam = jnp.exp(jnp.sum(lv[0] * lv[1])) - jnp.exp(jnp.sum(lv[2] * lv[3])) + lambda_init
    key_pos = jnp.arange(S)

    def block(bi):
        q0 = bi * Q_BLOCK
        t = q0 + jnp.arange(Q_BLOCK)
        qb = lax.dynamic_slice_in_dim(q, q0, Q_BLOCK, 1)
        p = masked_softmax(jnp.einsum('bthcd,bshcd->bhcts', qb, k) * dq ** -0.5,
                           key_pos[None, :] <= t[:, None])
        a = p[:, :, 0] - lam * p[:, :, 1]
        return jnp.einsum('bhts,bshd->bthd', a.astype(v.dtype), v)

    o = unblock(lax.map(block, jnp.arange(S // Q_BLOCK)))
    o = rms_norm(o, subln_gain) * (1.0 - lambda_init)
    return o.reshape(B, S, H * v.shape[-1])

def dsa_attention(q, k, v, q_idx, k_idx, w_idx, pos, qk_gain):
    B, S, H, Dh = q.shape
    G = DSA_KV_HEADS
    R = H // G
    top_k = min(DSA_TOPK_MAX, S // 4)
    scale = Dh ** -0.5
    qg = rope(rms_norm(q, qk_gain[0]), pos).reshape(B, S, G, R, Dh)
    k = rope(rms_norm(k, qk_gain[1]), pos)
    q_idx = rope(q_idx, pos)
    k_idx = rope(k_idx[:, :, None, :], pos)[:, :, 0]
    w_idx = w_idx * (IDX_HEADS ** -0.5 * IDX_DIM ** -0.5)
    key_pos = jnp.arange(S)
    gather = jax.vmap(lambda tt, ii: tt[ii])

    def block(bi):
        q0 = bi * Q_BLOCK
        t = q0 + jnp.arange(Q_BLOCK)
        qb = lax.dynamic_slice_in_dim(qg, q0, Q_BLOCK, 1)
        qi = lax.dynamic_slice_in_dim(q_idx, q0, Q_BLOCK, 1)
        wi = lax.dynamic_slice_in_dim(w_idx, q0, Q_BLOCK, 1)
        rel = jax.nn.relu(jnp.einsum('bthd,bsd->bths', qi, k_idx)).astype(jnp.float32)
        score = jnp.einsum('bths,bth->bts', rel, wi.astype(jnp.float32))
        causal = key_pos[None, :] <= t[:, None]
        _, idx = lax.top_k(jnp.where(causal, score, MASKED), top_k)
        kg = gather(k, idx)
        vg = gather(v, idx)
        ok = (idx <= t[None, :, None])[:, None, None]
        p = masked_softmax(jnp.einsum('btgrd,btkgd->bgrtk', qb, kg) * scale, ok)
        return jnp.einsum('bgrtk,btkgd->btgrd', p.astype(v.dtype), vg)

    out = unblock(lax.map(block, jnp.arange(S // Q_BLOCK)))
    return out.reshape(B, S, H * Dh)

def memory_attention(q, mem_n, w_kv, qk_gain):
    B, S, H, Dh = q.shape
    kv = jnp.einsum('bmd,dc->bmc', mem_n, w_kv).reshape(B, mem_n.shape[1], 2, H, Dh)
    k = rms_norm(kv[:, :, 0], qk_gain[1])
    v = kv[:, :, 1]
    q = rms_norm(q, qk_gain[0])
    p = jax.nn.softmax((jnp.einsum('bshd,bmhd->bhsm', q, k) * Dh ** -0.5).astype(jnp.float32), axis=-1)
    return jnp.einsum('bhsm,bmhd->bshd', p.astype(v.dtype), v).reshape(B, S, H * Dh)

def first_inputs(seed: int = 0) -> dict:
    key = jax.random.key(seed)
    ks = jax.random.split(key, 17)
    n_even = (DEPTH + 1) // 2
    n_odd = DEPTH // 2

    def nrm(k, shape, scale):
        return jax.random.normal(k, shape, jnp.float32) * scale

    def gain(k, shape):
        return 1.0 + 0.02 * jax.random.normal(k, shape, jnp.float32)

    return {
        "x": nrm(ks[0], (BATCH, SEQ, D_MODEL), 1.0),
        "mem": nrm(ks[1], (BATCH, MEM_LEN, D_MODEL), 1.0),
        "norm_gain": gain(ks[2], (DEPTH, D_MODEL)),
        "mem_norm_gain": gain(ks[3], (D_MODEL,)),
        "mem_w_kv": nrm(ks[4], (DEPTH, D_MODEL, 2 * MEM_HEADS * HEAD_DIM), D_MODEL ** -0.5),
        "mem_qk_gain": gain(ks[5], (DEPTH, 2, HEAD_DIM)),
        "w_out": nrm(ks[6], (DEPTH, MIX_WIDTH, D_MODEL), MIX_WIDTH ** -0.5),
        "even_w_in": nrm(ks[7], (n_even, D_MODEL, EVEN_IN), D_MODEL ** -0.5),
        "nsa_qk_gain": gain(ks[8], (n_even, 4, HEAD_DIM)),
        "nsa_cmp_pos": nrm(ks[9], (n_even, 2, NSA_CMP_LEN, HEAD_DIM), 0.3),
        "nsa_cmp_w1": nrm(ks[10], (n_even, 2, NSA_CMP_LEN * HEAD_DIM, NSA_CMP_HIDDEN), (NSA_CMP_LEN * HEAD_DIM) ** -0.5),
        "nsa_cmp_w2": nrm(ks[11], (n_even, 2, NSA_CMP_HIDDEN, HEAD_DIM), NSA_CMP_HIDDEN ** -0.5),
        "diff_qk_gain": gain(ks[12], (n_even, 2, DIFF_QK_DIM)),
        "diff_lambda": nrm(ks[13], (n_even, 4, DIFF_QK_DIM), 0.1),
        "diff_subln_gain": gain(ks[14], (n_even, DIFF_V_DIM)),
        "odd_w_in": nrm(ks[15], (n_odd, D_MODEL, ODD_IN), D_MODEL ** -0.5),
        "dsa_qk_gain": gain(ks[16], (n_odd, 2, HEAD_DIM)),
    }

def first_block(x, mem, norm_gain, mem_norm_gain, mem_w_kv, mem_qk_gain, w_out, even_w_in,
              nsa_qk_gain, nsa_cmp_pos, nsa_cmp_w1, nsa_cmp_w2, diff_qk_gain, diff_lambda,
              diff_subln_gain, odd_w_in, dsa_qk_gain):
    B, S, _ = x.shape
    pos = jnp.arange(S)
    mem_n = rms_norm(mem, mem_norm_gain)
    for i in range(DEPTH):
        h = rms_norm(x, norm_gain[i])
        if i % 2 == 0:
            e = i // 2
            proj = jnp.einsum('bsd,dc->bsc', h, even_w_in[e])
            a_q, a_kv, a_g, a_z, b_q, b_k, b_v, b_z, m_q, m_z = split_cols(proj, EVEN_SPLITS)
            y_a = nsa_attention(a_q.reshape(B, S, NSA_HEADS, HEAD_DIM),
                                a_kv.reshape(B, S, 6, NSA_KV_GROUPS, HEAD_DIM),
                                a_g.reshape(B, S, NSA_HEADS, 3), pos,
                                nsa_cmp_pos[e], nsa_cmp_w1[e], nsa_cmp_w2[e], nsa_qk_gain[e])
            lambda_init = 0.8 - 0.6 * math.exp(-0.3 * i)
            y_b = diff_attention(b_q.reshape(B, S, DIFF_HEADS, 2, DIFF_QK_DIM),
                                 b_k.reshape(B, S, DIFF_HEADS, 2, DIFF_QK_DIM),
                                 b_v.reshape(B, S, DIFF_HEADS, DIFF_V_DIM), pos,
                                 diff_qk_gain[e], diff_lambda[e], diff_subln_gain[e], lambda_init)
            y_m = memory_attention(m_q.reshape(B, S, MEM_HEADS, HEAD_DIM), mem_n, mem_w_kv[i], mem_qk_gain[i])
            y = jnp.concatenate([y_a * jax.nn.silu(a_z), y_b * jax.nn.silu(b_z),
                                 y_m * jax.nn.silu(m_z)], axis=-1)
        else:
            o = i // 2
            proj = jnp.einsum('bsd,dc->bsc', h, odd_w_in[o])
            c_q, c_k, c_v, i_q, i_k, i_w, c_z, m_q, m_z = split_cols(proj, ODD_SPLITS)
            y_c = dsa_attention(c_q.reshape(B, S, DSA_HEADS, HEAD_DIM),
                                c_k.reshape(B, S, DSA_KV_HEADS, HEAD_DIM),
                                c_v.reshape(B, S, DSA_KV_HEADS, HEAD_DIM),
                                i_q.reshape(B, S, IDX_HEADS, IDX_DIM), i_k, i_w, pos, dsa_qk_gain[o])
            y_m = memory_attention(m_q.reshape(B, S, MEM_HEADS, HEAD_DIM), mem_n, mem_w_kv[i], mem_qk_gain[i])
            y = jnp.concatenate([y_c * jax.nn.silu(c_z), y_m * jax.nn.silu(m_z)], axis=-1)
        x = x + jnp.einsum('bsc,cd->bsd', y, w_out[i])
    return x


N_GROUPS = 4
GROUP_WIDTH = D_MODEL // N_GROUPS
HEAD_DIM_2 = 64
N_HEADS = GROUP_WIDTH // HEAD_DIM_2
D_FF = ((8 * D_MODEL + 3 * 256 - 1) // (3 * 256)) * 256

RET_CHUNK = 128
HGRN_CHUNK = 32
MLSTM_CHUNK = 64
CONV_WIDTH = 4
ROPE_BASE = 10000.0
RWKV_W_LORA = 64
RWKV_A_LORA = 64
RWKV_V_LORA = 32
RWKV_G_LORA = 128
RWKV_DECAY_SCALE = 0.6065306597126334
RWKV_LN_EPS = 64e-5
NORM_EPS = 1e-6

RET_SPLIT = (GROUP_WIDTH,) * 4
HGRN_SPLIT = (GROUP_WIDTH,) * 4
MLSTM_SPLIT = (GROUP_WIDTH,) * 4 + (N_HEADS, N_HEADS)
RWKV_SPLIT = (GROUP_WIDTH,) * 3 + (RWKV_W_LORA, RWKV_A_LORA, RWKV_G_LORA)
GROUP_COLS = (sum(RET_SPLIT), sum(HGRN_SPLIT), sum(MLSTM_SPLIT), sum(RWKV_SPLIT))
N_IN = sum(GROUP_COLS)


def split_cols_2(t, sizes):
    return jnp.split(t, [int(i) for i in np.cumsum(sizes)[:-1]], axis=-1)

def rms_norm_2(x, w):
    xf = x.astype(jnp.float32)
    y = xf * lax.rsqrt(jnp.mean(xf * xf, axis=-1, keepdims=True) + NORM_EPS)
    return (y * w.astype(jnp.float32)).astype(x.dtype)

def to_heads(t):
    return t.reshape(t.shape[0], t.shape[1], N_HEADS, HEAD_DIM_2).transpose(0, 2, 1, 3)

def from_heads(t):
    return t.transpose(0, 2, 1, 3)

def head_rms(t, w=None):
    y = t * lax.rsqrt(jnp.mean(t * t, axis=-1, keepdims=True) + NORM_EPS)
    if w is not None:
        y = y * w.reshape(N_HEADS, HEAD_DIM_2)
    return y.reshape(t.shape[0], t.shape[1], -1)

def to_chunks(t, c):
    b, h, s = t.shape[:3]
    return jnp.moveaxis(t.reshape(b, h, s // c, c, *t.shape[3:]), 2, 0)

def from_chunks(t):
    t = jnp.moveaxis(t, 0, 2)
    return t.reshape(t.shape[0], t.shape[1], -1, t.shape[-1])

def rotary(t, pos):
    half = HEAD_DIM_2 // 2
    inv_freq = ROPE_BASE ** (-jnp.arange(half, dtype=jnp.float32) / half)
    ang = pos[:, None] * inv_freq[None, :]
    cos, sin = jnp.cos(ang), jnp.sin(ang)
    t1, t2 = t[..., :half], t[..., half:]
    return jnp.concatenate([t1 * cos - t2 * sin, t1 * sin + t2 * cos], axis=-1)

def token_shift(t):
    return jnp.pad(t, ((0, 0), (1, 0), (0, 0)))[:, :-1]

def causal_dwconv(t, w, b):
    seq = t.shape[1]
    tp = jnp.pad(t, ((0, 0), (CONV_WIDTH - 1, 0), (0, 0)))
    out = b + tp[:, 0:seq] * w[0]
    for j in range(1, CONV_WIDTH):
        out = out + tp[:, j:j + seq] * w[j]
    return out

def chunked_retention(q, k, v):
    c = RET_CHUNK
    b, h, s, d = q.shape
    log_gamma = jnp.log1p(-jnp.exp2(-5.0 - jnp.arange(h, dtype=jnp.float32)))
    idx = jnp.arange(c, dtype=jnp.float32)
    rel = idx[:, None] - idx[None, :]
    intra = jnp.where(rel >= 0, jnp.exp(log_gamma[:, None, None] * jnp.maximum(rel, 0.0)), 0.0)
    q_dec = jnp.exp(log_gamma[:, None] * (idx + 1.0))[:, :, None]
    k_dec = jnp.exp(log_gamma[:, None] * (c - 1.0 - idx))[:, :, None]
    chunk_dec = jnp.exp(log_gamma * c)[:, None, None]

    def step(state, inp):
        qc, kc, vc = inp
        scores = jnp.einsum('bhtd,bhsd->bhts', qc, kc) * intra
        out = (jnp.einsum('bhts,bhse->bhte', scores, vc)
               + jnp.einsum('bhtd,bhde->bhte', qc * q_dec, state))
        state = chunk_dec * state + jnp.einsum('bhsd,bhse->bhde', kc * k_dec, vc)
        return state, out

    _, o = lax.scan(step, jnp.zeros((b, h, d, d), q.dtype),
                    (to_chunks(q, c), to_chunks(k, c), to_chunks(v, c)))
    return from_chunks(o)

def retention_group(p):
    q, k, v, g = split_cols_2(p, RET_SPLIT)
    pos = jnp.arange(p.shape[1], dtype=jnp.float32)
    qh = rotary(to_heads(q), pos)
    kh = rotary(to_heads(k), pos) * HEAD_DIM_2 ** -0.5
    o = chunked_retention(qh, kh, to_heads(v))
    return head_rms(from_heads(o)) * jax.nn.silu(g)

def chunked_hgrn2(q, k, v, log_f):
    c = HGRN_CHUNK
    b, h, s, dk = q.shape
    dv = v.shape[-1]
    causal = jnp.tril(jnp.ones((c, c), dtype=bool))[:, :, None]

    def step(state, inp):
        qc, kc, vc, gc = inp
        cum = jnp.cumsum(gc, axis=2)
        pair = jnp.where(causal,
                         jnp.exp(jnp.minimum(cum[:, :, :, None, :] - cum[:, :, None, :, :], 0.0)), 0.0)
        scores = jnp.einsum('bhtd,bhsd,bhtsd->bhts', qc, kc, pair)
        out = (jnp.einsum('bhts,bhse->bhte', scores, vc)
               + jnp.einsum('bhtd,bhde->bhte', qc * jnp.exp(cum), state))
        cum_end = cum[:, :, -1:, :]
        state = (jnp.exp(cum_end)[:, :, 0, :, None] * state
                 + jnp.einsum('bhsd,bhse->bhde', kc * jnp.exp(cum_end - cum), vc))
        return state, out

    _, o = lax.scan(step, jnp.zeros((b, h, dk, dv), q.dtype),
                    (to_chunks(q, c), to_chunks(k, c), to_chunks(v, c), to_chunks(log_f, c)))
    return from_chunks(o)

def hgrn2_group(p, lb, norm_w):
    q, f, i, g = split_cols_2(p, HGRN_SPLIT)
    log_f = jnp.logaddexp(jnp.log(lb), jnp.log1p(-lb) + jax.nn.log_sigmoid(f))
    k = (1.0 - lb) * jax.nn.sigmoid(-f)
    o = chunked_hgrn2(to_heads(jax.nn.silu(q)) * HEAD_DIM_2 ** -0.5, to_heads(k), to_heads(i), to_heads(log_f))
    return head_rms(from_heads(o), norm_w) * jax.nn.sigmoid(g)

def chunked_mlstm(q, k, v, log_i, log_f):
    c = MLSTM_CHUNK
    b, h, s, dk = q.shape
    dv = v.shape[-1]
    causal = jnp.tril(jnp.ones((c, c), dtype=bool))

    def step(carry, inp):
        cmem, nvec, m = carry
        qc, kc, vc, ic, fc = inp
        cum = jnp.cumsum(fc, axis=-1)
        logd = jnp.where(causal, cum[..., :, None] - cum[..., None, :] + ic[..., None, :], -jnp.inf)
        log_inter = cum + m[..., None]
        m_t = jnp.maximum(jnp.max(logd, axis=-1), log_inter)
        scores = jnp.einsum('bhtd,bhsd->bhts', qc, kc) * jnp.exp(logd - m_t[..., None])
        w_inter = jnp.exp(log_inter - m_t)
        num = (jnp.einsum('bhts,bhse->bhte', scores, vc)
               + w_inter[..., None] * jnp.einsum('bhtd,bhde->bhte', qc, cmem))
        den = jnp.sum(scores, axis=-1) + w_inter * jnp.einsum('bhtd,bhd->bht', qc, nvec)
        h_out = num / jnp.maximum(jnp.abs(den), jnp.exp(-m_t))[..., None]
        cum_end = cum[..., -1]
        log_w = cum_end[..., None] - cum + ic
        m_new = jnp.maximum(cum_end + m, jnp.max(log_w, axis=-1))
        decay = jnp.exp(cum_end + m - m_new)
        kw = kc * jnp.exp(log_w - m_new[..., None])[..., None]
        cmem = decay[..., None, None] * cmem + jnp.einsum('bhsd,bhse->bhde', kw, vc)
        nvec = decay[..., None] * nvec + jnp.sum(kw, axis=2)
        return (cmem, nvec, m_new), h_out

    init = (jnp.zeros((b, h, dk, dv), q.dtype), jnp.zeros((b, h, dk), q.dtype), jnp.zeros((b, h), q.dtype))
    _, o = lax.scan(step, init, (to_chunks(q, c), to_chunks(k, c), to_chunks(v, c),
                                 to_chunks(log_i, c), to_chunks(log_f, c)))
    return from_chunks(o)

def mlstm_group(p, conv_w, conv_b, i_bias, f_bias, norm_w):
    q, k, v, o, ig, fg = split_cols_2(p, MLSTM_SPLIT)
    qk = jax.nn.silu(causal_dwconv(jnp.concatenate([q, k], axis=-1), conv_w, conv_b))
    q, k = jnp.split(qk, 2, axis=-1)
    log_i = jnp.swapaxes(ig + i_bias, 1, 2)
    log_f = jnp.swapaxes(jax.nn.log_sigmoid(fg + f_bias), 1, 2)
    hm = chunked_mlstm(to_heads(q), to_heads(k) * HEAD_DIM_2 ** -0.5, to_heads(v), log_i, log_f)
    return jax.nn.sigmoid(o) * head_rms(from_heads(hm), norm_w)

def rwkv7_scan(r, log_w, k, v, kk, a):
    b, s, h, d = r.shape
    xs = tuple(jnp.swapaxes(t, 0, 1) for t in (r, log_w, k, v, kk, a))

    def step(state, inp):
        rt, lwt, kt, vt, kkt, at = inp
        state = (state * jnp.exp(lwt)[:, :, None, :]
                 - jnp.einsum('bhvk,bhk->bhv', state, kkt)[..., None] * (at * kkt)[:, :, None, :]
                 + vt[..., None] * kt[:, :, None, :])
        return state, jnp.einsum('bhvk,bhk->bhv', state, rt)

    _, y = lax.scan(step, jnp.zeros((b, h, d, d), r.dtype), xs)
    return jnp.swapaxes(y, 0, 1)

def rwkv7_group(p, v_first, mu, w0, w_up, a0, a_up, g_up, k_k, k_a, r_k, ln_w, ln_b, vmix):
    b, s, _ = p.shape
    p = p + (token_shift(p) - p) * mu
    r, k, v, wd, ad, gd = split_cols_2(p, RWKV_SPLIT)
    log_w = -RWKV_DECAY_SCALE * jax.nn.sigmoid(w0 + jnp.tanh(wd) @ w_up)
    a = jax.nn.sigmoid(a0 + ad @ a_up)
    g = jax.nn.sigmoid(gd) @ g_up
    if vmix is None:
        v_first = v
    else:
        v0, v_down, v_up = vmix
        v = v + (v_first - v) * jax.nn.sigmoid(v0 + (v @ v_down) @ v_up)

    def hs(t):
        return t.reshape(b, s, N_HEADS, HEAD_DIM_2)

    kk = hs(k * k_k)
    kk = kk / jnp.maximum(jnp.sqrt(jnp.sum(kk * kk, axis=-1, keepdims=True)), 1e-12)
    k = k * (1.0 + (a - 1.0) * k_a)
    y = rwkv7_scan(hs(r), hs(log_w), hs(k), hs(v), kk, hs(a))
    mean = jnp.mean(y, axis=-1, keepdims=True)
    var = jnp.mean(jnp.square(y - mean), axis=-1, keepdims=True)
    y = ((y - mean) * lax.rsqrt(var + RWKV_LN_EPS)).reshape(b, s, -1) * ln_w + ln_b
    bonus = (jnp.sum(hs(r * k * r_k), axis=-1, keepdims=True) * hs(v)).reshape(b, s, -1)
    return (y + bonus) * g, v_first

def second_inputs(seed: int = 0) -> dict:
    key = jax.random.key(seed)
    keys = jax.random.split(key, 31)
    counter = iter(range(31))
    G, H, L = GROUP_WIDTH, N_HEADS, DEPTH

    def nrm(shape, scale):
        return scale * jax.random.normal(keys[next(counter)], shape, jnp.float32)

    def gain(shape):
        return 1.0 + nrm(shape, 0.05)

    return {
        'x': nrm((BATCH, SEQ, D_MODEL), 1.0),
        'w_in': nrm((L, D_MODEL, N_IN), D_MODEL ** -0.5),
        'w_out': nrm((L, D_MODEL, D_MODEL), D_MODEL ** -0.5),
        'norm_pre_mix': gain((L, D_MODEL)),
        'norm_post_mix': gain((L, D_MODEL)),
        'norm_pre_ffn': gain((L, D_MODEL)),
        'norm_post_ffn': gain((L, D_MODEL)),
        'w_ffn_gate': nrm((L, D_MODEL, D_FF), D_MODEL ** -0.5),
        'w_ffn_up': nrm((L, D_MODEL, D_FF), D_MODEL ** -0.5),
        'w_ffn_down': nrm((L, D_FF, D_MODEL), D_FF ** -0.5),
        'hgrn_lb_logits': nrm((L, G), 0.5),
        'hgrn_norm_w': gain((L, G)),
        'mlstm_conv_w': nrm((L, CONV_WIDTH, 2 * G), CONV_WIDTH ** -0.5),
        'mlstm_conv_b': nrm((L, 2 * G), 0.02),
        'mlstm_i_bias': nrm((L, H), 0.1) - 1.0,
        'mlstm_f_bias': nrm((L, H), 0.5) + 3.0,
        'mlstm_norm_w': gain((L, G)),
        'rwkv_mu': jax.random.uniform(keys[next(counter)], (L, GROUP_COLS[3]), jnp.float32),
        'rwkv_w0': nrm((L, G), 0.5),
        'rwkv_w_up': nrm((L, RWKV_W_LORA, G), 0.5 * RWKV_W_LORA ** -0.5),
        'rwkv_a0': nrm((L, G), 0.5),
        'rwkv_a_up': nrm((L, RWKV_A_LORA, G), 0.5 * RWKV_A_LORA ** -0.5),
        'rwkv_g_up': nrm((L, RWKV_G_LORA, G), RWKV_G_LORA ** -0.5),
        'rwkv_k_k': gain((L, G)),
        'rwkv_k_a': gain((L, G)),
        'rwkv_r_k': nrm((L, G), 0.1),
        'rwkv_ln_w': gain((L, G)),
        'rwkv_ln_b': nrm((L, G), 0.02),
        'rwkv_v0': nrm((L - 1, G), 0.5),
        'rwkv_v_down': nrm((L - 1, G, RWKV_V_LORA), G ** -0.5),
        'rwkv_v_up': nrm((L - 1, RWKV_V_LORA, G), 0.5 * RWKV_V_LORA ** -0.5),
    }

def second_block(x, w_in, w_out, norm_pre_mix, norm_post_mix, norm_pre_ffn, norm_post_ffn,
              w_ffn_gate, w_ffn_up, w_ffn_down, hgrn_lb_logits, hgrn_norm_w,
              mlstm_conv_w, mlstm_conv_b, mlstm_i_bias, mlstm_f_bias, mlstm_norm_w,
              rwkv_mu, rwkv_w0, rwkv_w_up, rwkv_a0, rwkv_a_up, rwkv_g_up,
              rwkv_k_k, rwkv_k_a, rwkv_r_k, rwkv_ln_w, rwkv_ln_b,
              rwkv_v0, rwkv_v_down, rwkv_v_up):
    lb_cum = jnp.cumsum(jax.nn.softmax(hgrn_lb_logits.astype(jnp.float32), axis=0), axis=0)
    lower_bounds = lb_cum - lb_cum[0]
    v_first = None
    h = x
    for l in range(DEPTH):
        u = rms_norm_2(h, norm_pre_mix[l])
        p = (u @ w_in[l]).astype(jnp.float32)
        p_ret, p_hgrn, p_ml, p_rw = split_cols_2(p, GROUP_COLS)
        o_ret = retention_group(p_ret)
        o_hgrn = hgrn2_group(p_hgrn, lower_bounds[l], hgrn_norm_w[l])
        o_ml = mlstm_group(p_ml, mlstm_conv_w[l], mlstm_conv_b[l], mlstm_i_bias[l],
                           mlstm_f_bias[l], mlstm_norm_w[l])
        vmix = None if l == 0 else (rwkv_v0[l - 1], rwkv_v_down[l - 1], rwkv_v_up[l - 1])
        o_rw, v_first = rwkv7_group(p_rw, v_first, rwkv_mu[l], rwkv_w0[l], rwkv_w_up[l],
                                    rwkv_a0[l], rwkv_a_up[l], rwkv_g_up[l], rwkv_k_k[l],
                                    rwkv_k_a[l], rwkv_r_k[l], rwkv_ln_w[l], rwkv_ln_b[l], vmix)
        mixed = jnp.concatenate([o_ret, o_hgrn, o_ml, o_rw], axis=-1).astype(h.dtype) @ w_out[l]
        h = h + rms_norm_2(mixed, norm_post_mix[l])
        u = rms_norm_2(h, norm_pre_ffn[l])
        ffn = (jax.nn.silu(u @ w_ffn_gate[l]) * (u @ w_ffn_up[l])) @ w_ffn_down[l]
        h = h + rms_norm_2(ffn, norm_post_ffn[l])
    return h


def setup_inputs(seed=0):
    out = dict(first_inputs(seed))
    for name, value in second_inputs(seed + 1).items():
        if name != "x":
            out[name + "_2"] = value
    return out


def reference(
    x, mem, norm_gain, mem_norm_gain, mem_w_kv, mem_qk_gain, w_out, even_w_in, nsa_qk_gain,
    nsa_cmp_pos, nsa_cmp_w1, nsa_cmp_w2, diff_qk_gain, diff_lambda, diff_subln_gain, odd_w_in,
    dsa_qk_gain, w_in_2, w_out_2, norm_pre_mix_2, norm_post_mix_2, norm_pre_ffn_2,
    norm_post_ffn_2, w_ffn_gate_2, w_ffn_up_2, w_ffn_down_2, hgrn_lb_logits_2, hgrn_norm_w_2,
    mlstm_conv_w_2, mlstm_conv_b_2, mlstm_i_bias_2, mlstm_f_bias_2, mlstm_norm_w_2, rwkv_mu_2,
    rwkv_w0_2, rwkv_w_up_2, rwkv_a0_2, rwkv_a_up_2, rwkv_g_up_2, rwkv_k_k_2, rwkv_k_a_2,
    rwkv_r_k_2, rwkv_ln_w_2, rwkv_ln_b_2, rwkv_v0_2, rwkv_v_down_2, rwkv_v_up_2,
):
    x = first_block(
        x, mem, norm_gain, mem_norm_gain, mem_w_kv, mem_qk_gain, w_out, even_w_in, nsa_qk_gain,
        nsa_cmp_pos, nsa_cmp_w1, nsa_cmp_w2, diff_qk_gain, diff_lambda, diff_subln_gain,
        odd_w_in, dsa_qk_gain,
    )
    return second_block(
        x, w_in_2, w_out_2, norm_pre_mix_2, norm_post_mix_2, norm_pre_ffn_2, norm_post_ffn_2,
        w_ffn_gate_2, w_ffn_up_2, w_ffn_down_2, hgrn_lb_logits_2, hgrn_norm_w_2, mlstm_conv_w_2,
        mlstm_conv_b_2, mlstm_i_bias_2, mlstm_f_bias_2, mlstm_norm_w_2, rwkv_mu_2, rwkv_w0_2,
        rwkv_w_up_2, rwkv_a0_2, rwkv_a_up_2, rwkv_g_up_2, rwkv_k_k_2, rwkv_k_a_2, rwkv_r_k_2,
        rwkv_ln_w_2, rwkv_ln_b_2, rwkv_v0_2, rwkv_v_down_2, rwkv_v_up_2,
    )


_drawn_inputs = setup_inputs


def setup_inputs(seed=0):
    import zlib

    import numpy as np

    out = dict(_drawn_inputs(seed))
    spreads = {}
    factors = {'mem_norm_gain': 8.0,
     'mem_qk_gain': 6.76,
     'nsa_qk_gain': 4.892,
     'diff_qk_gain': 2.739,
     'diff_lambda': 3.585,
     'diff_subln_gain': 3.161,
     'dsa_qk_gain': 7.308,
     'mlstm_conv_b_2': 17.848,
     'mlstm_i_bias_2': 8.0,
     'rwkv_k_k_2': 64.0,
     'rwkv_ln_b_2': 13.369,
     'norm_post_mix_2': 2.727,
     'norm_post_ffn_2': 3.017,
     'hgrn_lb_logits_2': 4.503,
     'hgrn_norm_w_2': 4.988,
     'mlstm_norm_w_2': 7.411,
     'rwkv_w_up_2': 4.309,
     'rwkv_k_a_2': 4.41,
     'rwkv_ln_w_2': 5.288}
    for name, (base, spread) in spreads.items():
        noise = np.random.default_rng([zlib.crc32(name.encode()), seed]).standard_normal(out[name].shape)
        drawn = base * np.exp(spread * noise) if base else spread * noise
        out[name] = jnp.asarray(drawn.astype(out[name].dtype))
    for name, factor in factors.items():
        out[name] = (out[name] * factor).astype(out[name].dtype)
    return out
```

```python
import concourse.bass as bass
from concourse import mybir
from contextlib import ExitStack, contextmanager
import math
import numpy as np

F32 = mybir.dt.float32
ALU = mybir.AluOpType
ACT = mybir.ActivationFunctionType
AX = mybir.AxisListType
ds = bass.ds

P = 128
S = 256
T = S // P
D = 2048
KC = D // P
TILE = 512
UNIT = 4
SLOTS = 4
EPS = 1e-6
BIG = 1e30

EVEN = dict(a_q=0, a_kv=1024, a_g=2560, a_z=2584, b_q=3608, b_k=4120, b_v=4632, b_z=5144, m_q=5656, m_z=6168)
EVEN_IN = 6680
ODD = dict(c_q=0, c_k=1536, c_v=2048, i_q=2560, i_k=3584, i_w=3648, c_z=3664, m_q=5200, m_z=5712)
ODD_IN = 6224
HD = 128
CMP_LEN, CMP_STRIDE, CMP_HID = 32, 16, 256
NCMP = (S - CMP_LEN) // CMP_STRIDE + 1
TOPK = S // 4
LAMBDA_INIT = 0.8 - 0.6 * math.exp(0.0)

GW, H2, HD2 = 512, 8, 64
N_IN = 7952
D_FF = 5632
LEVELS = 7
DECAY_SCALE = 0.6065306597126334
LN_EPS = 64e-5
WORK = 12150


def shape_constants():
    t = np.arange(S)
    p = np.arange(P)
    parts = {}

    def put(name, a):
        full = np.zeros((P, a.shape[1]), np.float32)
        full[:a.shape[0]] = a
        parts[name] = full

    def rope_tables(pos, half):
        inv = (np.float32(10000.0) ** (-np.arange(half, dtype=np.float32) / np.float32(half))).astype(np.float32)
        ang = pos.astype(np.float32)[:, None] * inv[None, :]
        return np.cos(ang).astype(np.float32), np.sin(ang).astype(np.float32)

    def by_tile(a):
        return a.reshape(T, P, -1).transpose(1, 0, 2).reshape(P, -1)

    put("ident", np.eye(P, dtype=np.float32))
    future = (p[None, :] > p[:, None]).astype(np.float32)
    put("causal", np.concatenate([np.zeros((P, P)), future * BIG], 1))
    put("zeros", np.zeros((P, S)))
    put("ones", np.ones((P, P)))
    put("pair_ones", np.kron(np.eye(2), np.ones((HD2, HD2))))
    put("pair_pick", np.kron(np.eye(2), np.ones((HD2, 1))))
    for d in (HD, HD2):
        c, s = rope_tables(t, d // 2)
        put(f"cos{d}", by_tile(c))
        put(f"sin{d}", by_tile(s))
    last = np.arange(NCMP) * CMP_STRIDE + CMP_LEN - 1
    c, s = rope_tables(np.tile(last, 2), HD // 2)
    put("cos_cmp", c)
    put("sin_cmp", s)
    for g in range(2):
        for tt in range(T):
            ok = np.zeros((P, 2 * NCMP), np.float32)
            ok[:, g * NCMP:(g + 1) * NCMP] = last[None, :] <= (tt * P + p)[:, None]
            put(f"cmp_keep{g}{tt}", ok)
            put(f"cmp_drop{g}{tt}", (1 - ok) * BIG)
    put("upto_T", (p[:, None] <= p[None, :]).astype(np.float32))
    put("before_T", (p[:, None] < p[None, :]).astype(np.float32))
    offs, at = {}, 0
    for n, a in parts.items():
        offs[n] = (at, a.shape[1])
        at += a.shape[1]
    small = np.concatenate(list(parts.values()), 1).astype(np.float32)

    half = [((p[:, None] // (2 * b) == p[None, :] // (2 * b)) & (p[:, None] % (2 * b) < b) & (p[None, :] % (2 * b) >= b))
            .astype(np.float32) for b in (1 << np.arange(LEVELS))]
    halves_T = np.concatenate(half, 1)
    halves = np.concatenate([h.T for h in half], 1)
    lg = np.log1p(-np.exp2(-5.0 - np.arange(H2)))
    rel = p[None, :] - p[:, None]
    dec = [[np.exp(lg[h] * np.maximum(rel + off, 0)) * (rel + off >= 0) * HD2 ** -0.5 for off in (0, P)] for h in range(H2)]
    decay = np.concatenate([np.concatenate(d2, 1) for d2 in dec], 1).astype(np.float32)
    return small, offs, halves_T.astype(np.float32), halves.astype(np.float32), decay


class Counter:

    def __init__(self, sem, step=1):
        self.sem, self.step, self.base, self.k = sem, step, 0, 0

    def count(self, ins):
        ins.then_inc(self.sem, self.step)
        self.k += 1
        return self.now()

    def now(self, back=0):
        return (self.sem, self.base + (self.k - back) * self.step)


class Queue(Counter):

    def __init__(self, eng, sem):
        super().__init__(sem)
        self.eng = eng

    def wait(self, *marks):
        for sem, value in marks:
            self.eng.wait_ge(sem, value)

    def did(self, ins):
        return self.count(ins)

    def hold(self, passed):
        self.eng.sem_inc(passed, 1)

    def seq(self, ins):
        m = self.count(ins)
        self.wait(m)
        return m


class Program:
    def __init__(self, nc, A, consts, out):
        self.nc, self.A, self.C, self.out_dram = nc, A, consts, out

    def build(self):
        nc = self.nc
        with ExitStack() as ctx:
            def sem(name):
                return ctx.enter_context(nc.semaphore(name))

            def sb(name, shape):
                return ctx.enter_context(nc.sbuf_tensor(name, shape, F32))

            self.pe = Queue(nc.tensor, sem("pe_done"))
            self.act = Queue(nc.scalar, sem("act_done"))
            self.dve = Queue(nc.vector, sem("dve_done"))
            self.pool = Queue(nc.gpsimd, sem("pool_done"))
            self.full = [Counter(sem(f"slot_full{i}"), 16) for i in range(SLOTS)]
            self.freed = [Counter(sem(f"slot_freed{i}")) for i in range(SLOTS)]
            self.small = Counter(sem("small_loads"), 16)
            self.work_ld = Counter(sem("work_loads"), 16)
            self.passed = sem("passed")
            self.outs = Counter(sem("out_stores"), 16)
            self.counters = dict(pe=self.pe, act=self.act, dve=self.dve, pool=self.pool)
            for i in range(SLOTS):
                self.counters[f"full{i}"] = self.full[i]
                self.counters[f"freed{i}"] = self.freed[i]

            self.x = sb("x_residual", [P, T, D])
            self.hT = sb("h_transposed", [P, KC, S])
            self.mixed = sb("mixed", [P, T, D])
            self.proj = sb("proj", [P, 16384])
            self.ring = [sb(f"weights{i}", [P, UNIT, TILE]) for i in range(SLOTS)]
            self.const = sb("const", [P, self.C["small"].shape[1]])
            self.work = sb("work", [P, WORK])
            self.work_at = 0
            self.params = sb("params", [P, 2250])
            self.params_at = 0
            self.ps = [ctx.enter_context(nc.psum_tensor(f"bank{b}", [P, 512], F32)) for b in range(8)]

            for i in range(SLOTS):
                nc.sync.sem_inc(self.freed[i].sem, 1)
                self.freed[i].base = 1
            self.load_params()
            self.main()
            self.finish()

    def c(self, name):
        at, w = self.C["offs"][name]
        return self.const[:, at:at + w]

    def take(self, cols):
        a = self.work[:, self.work_at:self.work_at + cols]
        self.work_at += cols
        assert self.work_at <= WORK, self.work_at
        return a

    @contextmanager
    def loop(self, n, engines, **per):
        nc = self.nc
        kinds = dict(pe=mybir.EngineType.PE, act=mybir.EngineType.Activation, dve=mybir.EngineType.DVE,
                     pool=mybir.EngineType.Pool, sp=mybir.EngineType.SP)
        old = {k: (c.base, c.k) for k, c in self.counters.items()}
        with nc.Fori(0, n, engines=[kinds[e] for e in engines]) as i:
            for k, c in self.counters.items():
                if per.get(k):
                    c.base, c.k = c.base + c.k * c.step + i * (per[k] * c.step), 0
                else:
                    c.base, c.k = c.base + c.k * c.step, 0
            yield i
            made = {k: c.k for k, c in self.counters.items() if c.k}
            assert made == {k: v for k, v in per.items() if v}, f"a turn makes {made}"
        for k, c in self.counters.items():
            c.base, c.k = old[k][0], old[k][1] + n * per.get(k, 0)

    def meet(self, names=("pe", "act", "dve", "pool")):
        qs = [self.counters[n] for n in names]
        marks = [q.now() for q in qs]
        for q in qs:
            q.wait(*marks)

    def param(self, dram_row, width):
        dst = self.params[:, self.params_at:self.params_at + width]
        self.params_at += width
        self.small.count(self.nc.scalar.dma_start(dst, dram_row.partition_broadcast(P)))
        return dst

    def param_cols(self, dram_vec, chunks):
        dst = self.params[:, self.params_at:self.params_at + chunks]
        self.params_at += chunks
        with self.nc.allow_non_contiguous_dma(reason="a few thousand parameters"):
            self.small.count(self.nc.scalar.dma_start(dst, dram_vec.rearrange("(c p) -> p c", p=P)))
        return dst

    def load_unit(self, slot, W, u, col, width, chunks=UNIT):
        nc = self.nc
        full, freed = self.full[slot], self.freed[slot]
        nc.sync.wait_ge(freed.sem, freed.base + freed.k)
        dst = self.ring[slot][:, 0:chunks, 0:width]
        full.count(nc.sync.dma_start(dst, W[u, :, :, ds(col, width)]))

    def tile_tokens(self, AT, W, units, col, width, dst, before):
        nc, pe, act = self.nc, self.pe, self.act
        marks = []
        for u in range(units):
            slot = u % SLOTS
            self.load_unit(slot, W, u, col, width)
            pe.wait(self.full[slot].now())
            for t in range(T):
                if u == 0:
                    pe.wait(before[t])
                for c in range(UNIT):
                    k = u * UNIT + c
                    ins = nc.tensor.matmul(self.ps[t][:, 0:width], AT[:, k, t * P:(t + 1) * P],
                                           self.ring[slot][:, c, 0:width], start=(k == 0), stop=(k == units * UNIT - 1))
                if u == units - 1 and t < T - 1:
                    marks.append(pe.did(ins))
            released = self.freed[slot].count(ins)
        marks.append(released)
        done = []
        for t in range(T):
            act.wait(marks[t])
            done.append(act.did(nc.scalar.activation(dst(t), self.ps[t][:, 0:width], ACT.Copy)))
        return done

    def tile_features(self, AT, W, units, col, chunks, dst, before, bank0=0, evac=None):
        nc, pe, act = self.nc, self.pe, self.act
        marks = []
        for u in range(units):
            slot = u % SLOTS
            self.load_unit(slot, W, u, col, chunks * P)
            pe.wait(self.full[slot].now())
            for j in range(chunks):
                if u == 0:
                    pe.wait(before[j])
                for c in range(UNIT):
                    k = u * UNIT + c
                    ins = nc.tensor.matmul(self.ps[bank0 + j][:, 0:S], self.ring[slot][:, c, j * P:(j + 1) * P],
                                           AT[:, k, :], start=(k == 0), stop=(k == units * UNIT - 1))
                if u == units - 1 and j < chunks - 1:
                    marks.append(pe.did(ins))
            released = self.freed[slot].count(ins)
        marks.append(released)
        done = []
        for j in range(chunks):
            if evac:
                done.append(evac(j, marks[j]))
                continue
            act.wait(marks[j])
            done.append(act.did(nc.scalar.activation(dst(j), self.ps[bank0 + j][:, 0:S], ACT.Copy)))
        return done

    def units_of(self, W):
        return W.rearrange("(u c p) n -> u p c n", c=UNIT, p=P)

    def per_slot(self, units):
        n = {}
        for u in range(units):
            n[f"full{u % SLOTS}"] = n[f"freed{u % SLOTS}"] = n.get(f"full{u % SLOTS}", 0) + 1
        return n

    def project_tokens(self, AT, W, rows, col0, n, dst):
        nc, act = self.nc, self.act
        units = rows // (UNIT * P)
        Wu = self.units_of(W)
        whole, rest = n // TILE, n % TILE
        start = act.k
        if whole:
            with self.loop(whole, ("pe", "act", "sp"), pe=T - 1, act=T, **self.per_slot(units)) as i:
                before = [act.now(1), act.now()]
                self.tile_tokens(AT, Wu, units, col0 + i * TILE, TILE,
                                 lambda t: dst[:, t, ds(i * TILE, TILE)], before)
        if rest:
            before = [act.now(1), act.now()]
            self.tile_tokens(AT, Wu, units, col0 + whole * TILE, rest,
                             lambda t: dst[:, t, whole * TILE:n], before)
        base = act.base

        def ready(col):
            return (act.sem, base + start + T * (-(-col // TILE)))
        return ready

    def transpose_tokens(self, src, dst, gain=None):
        nc, pe, act, dve = self.nc, self.pe, self.act, self.dve
        n = src.shape[2] // P
        free = {}
        ident = self.c("ident")
        done = []
        for k, c in enumerate(range(0, n, 2)):
            b = 2 + k % 4
            cc = min(2, n - c)
            if b in free:
                pe.wait(free[b])
            for j in range(cc):
                for t in range(T):
                    ins = nc.tensor.transpose(self.ps[b][:, (j * T + t) * P:(j * T + t + 1) * P],
                                              src[:, t, (c + j) * P:(c + j + 1) * P], ident)
            m = pe.did(ins)
            q = act if k % 2 else dve
            q.wait(m)
            if gain is None:
                o, i_ = dst[:, c:c + cc, :], self.ps[b][:, 0:cc * S].rearrange("p (c s) -> p c s", c=cc)
                ins = nc.scalar.activation(o, i_, ACT.Copy) if q is act else nc.vector.tensor_copy(o, i_)
                free[b] = q.did(ins)
            else:
                for j in range(cc):
                    o, i_, g = dst[:, c + j, :], self.ps[b][:, j * S:(j + 1) * S], gain[:, c + j:c + j + 1]
                    ins = (nc.scalar.activation(o, i_, ACT.Copy, scale=g) if q is act
                           else nc.vector.tensor_scalar(o, i_, g, None, ALU.mult))
                    free[b] = q.did(ins)
            done.append(free[b])
        return done

    def inv_rms(self, ss, width, n, eps=EPS):
        nc, dve, pool = self.nc, self.dve, self.pool
        m = dve.did(nc.vector.tensor_scalar(ss, ss, 1.0 / n, eps, ALU.mult, ALU.add))
        pool.wait(m)
        mh = self.minus_half.broadcast_to([ss.shape[0], ss.shape[1]]) if False else self.minus_half[0:ss.shape[0], 0:ss.shape[1]]
        m = pool.did(nc.gpsimd.tensor_tensor(ss, ss, mh, ALU.pow))
        dve.wait(m)

    def norm_to_hT(self, src, gain):
        nc, act, dve = self.nc, self.act, self.dve
        ss = self.rowstat[:, 0:T]
        for t in range(T):
            m = act.did(nc.scalar.activation(self.mixed[:, t, :], src[:, t, :], ACT.Square, accum_out=ss[:, t:t + 1]))
        dve.wait(m)
        self.inv_rms(ss, T, D)
        for t in range(T):
            m = dve.did(nc.vector.tensor_scalar(self.mixed[:, t, :], src[:, t, :], ss[:, t:t + 1], None, ALU.mult))
        self.pe.wait(m)
        self.transpose_tokens(self.mixed, self.hT, gain)
        self.meet()

    def head_norm(self, src, tmp, heads, d, gain, rows=P):
        nc, dve = self.nc, self.dve
        ss = self.rowstat[0:rows, 4:4 + heads]
        dve.seq(nc.vector.tensor_tensor(tmp, src, src, ALU.mult))
        dve.seq(nc.vector.tensor_reduce(ss, tmp, AX.X, ALU.add))
        self.inv_rms(ss, heads, d)
        dve.seq(nc.vector.tensor_tensor(tmp, src, ss.unsqueeze(2).broadcast_to([rows, heads, d]), ALU.mult))
        if gain is not None:
            dve.seq(nc.vector.tensor_tensor(tmp, tmp, gain[0:rows].unsqueeze(1).broadcast_to([rows, heads, d]), ALU.mult))

    def rope(self, src, dst, heads, d, cos, sin, rows=P):
        nc, dve = self.nc, self.dve
        h = d // 2
        cb = cos.unsqueeze(1).broadcast_to([rows, heads, h])
        sb_ = sin.unsqueeze(1).broadcast_to([rows, heads, h])
        x1, x2, o1, o2 = src[:, :, 0:h], src[:, :, h:d], dst[:, :, 0:h], dst[:, :, h:d]
        tmp = self.rope_tmp[0:rows, 0:heads * h].rearrange("p (n d) -> p n d", n=heads)
        dve.did(nc.vector.tensor_tensor(o1, x1, cb, ALU.mult))
        dve.seq(nc.vector.tensor_tensor(tmp, x2, sb_, ALU.mult))
        dve.did(nc.vector.tensor_tensor(o1, o1, tmp, ALU.subtract))
        dve.seq(nc.vector.tensor_tensor(o2, x2, cb, ALU.mult))
        dve.seq(nc.vector.tensor_tensor(tmp, x1, sb_, ALU.mult))
        return dve.seq(nc.vector.tensor_tensor(o2, o2, tmp, ALU.add))

    def prep(self, view, heads, d, gain, rope, norm=True):
        nc, dve = self.nc, self.dve
        for t in range(T):
            src = view(t)
            tmp = self.prep_tmp[:, 0:heads * d].rearrange("p (n d) -> p n d", n=heads)
            if norm:
                self.head_norm(src, tmp, heads, d, gain)
            else:
                dve.seq(nc.vector.tensor_copy(tmp, src))
            if rope:
                half = d // 2
                m = self.rope(tmp, src, heads, d, self.c(f"cos{d}")[:, t * half:(t + 1) * half],
                              self.c(f"sin{d}")[:, t * half:(t + 1) * half])
            else:
                m = dve.seq(nc.vector.tensor_copy(src, tmp))
        return m

    def attention(self, units):
        nc, pe, act, dve = self.nc, self.pe, self.act, self.dve
        R = 2
        n = len(units)
        st = [dict() for _ in units]

        def scores(i):
            u, s = units[i], st[i]
            s["ps"] = self.ps[2 + i % R][:, 0:u["keys"]]
            if i >= R:
                pe.wait(st[i - R]["masked"])
            s["scored"] = pe.did(nc.tensor.matmul(s["ps"], u["qT"], u["kT"], start=True, stop=True))
            if u.get("mlstm"):
                for c, g in enumerate(u["gates"]):
                    s["scored"] = pe.did(nc.tensor.matmul(self.ps[2 + i % R][:, S + c * P:S + (c + 1) * P],
                                                          g.broadcast_to([P, P]), self.c("ident"), start=True, stop=True))

        def soften(i):
            u, s = units[i], st[i]
            k, j = u["keys"], i % 3
            s["e"] = self.sm_e[:, j * S:j * S + k]
            stat = self.sm_stat[:, 4 * j:4 * j + 4]
            dve.wait(s["scored"])
            if i >= 3:
                dve.wait(st[i - 3]["exp"], st[i - 3]["out"])
            if u.get("mlstm"):
                return soften_mlstm(i, u, s, k, j)
            dve.hold(self.passed)
            s["masked"] = dve.did(nc.vector.tensor_tensor_reduce(
                out=self.sm_s[:, j * S:j * S + k], in0=s["ps"], in1=u["mask"], scale=1.0, scalar=3e38,
                op0=ALU.add, op1=ALU.min, accum_out=stat[:, 0:1]))
            act.wait(s["masked"])
            if i >= 3:
                act.wait(st[i - 3]["flipped"])
            s["exp"] = act.did(nc.scalar.activation(s["e"], self.sm_s[:, j * S:j * S + k], ACT.Exp,
                                                    bias=stat[:, 0:1], scale=-1.0, accum_out=stat[:, 1:2]))
            dve.wait(s["exp"])
            if u.get("keep") is not None:
                dve.hold(self.passed)
                s["exp"] = dve.seq(nc.vector.tensor_tensor_reduce(
                    out=s["e"], in0=s["e"], in1=u["keep"], scale=1.0, scalar=0.0,
                    op0=ALU.mult, op1=ALU.add, accum_out=stat[:, 1:2]))
            dve.seq(nc.vector.tensor_scalar(stat[:, 2:3], stat[:, 1:2], 1e-30, None, ALU.max))
            s["recip"] = dve.did(nc.vector.reciprocal(stat[:, 3:4], stat[:, 2:3]))
            s["r"] = stat[:, 3:4]

        def soften_mlstm(i, u, s, k, j):
            G = self.ps[2 + i % R][:, S:S + k]
            stat = self.sm_stat[:, 8 * j:8 * j + 8]
            M, neg, m, floor, den, recip = [stat[:, c:c + 1] for c in range(6)]
            buf = self.sm_s[:, j * S:j * S + k]
            dve.hold(self.passed)
            dve.seq(nc.vector.tensor_tensor_reduce(out=buf, in0=G, in1=u["mask"], scale=1.0, scalar=0.0,
                                                   op0=ALU.subtract, op1=ALU.max, accum_out=M))
            dve.did(nc.vector.tensor_scalar(neg, M, -1.0, None, ALU.mult))
            act.wait(dve.did(nc.vector.tensor_tensor(m, M, u["F"], ALU.add)))
            act.did(nc.scalar.activation(buf, buf, ACT.Exp, bias=neg))
            dve.wait(act.did(nc.scalar.activation(floor, m, ACT.Exp, scale=-1.0)))
            if i >= 3:
                dve.wait(st[i - 3]["flipped"])
            dve.hold(self.passed)
            s["masked"] = s["exp"] = dve.seq(nc.vector.tensor_tensor_reduce(
                out=s["e"], in0=s["ps"], in1=buf, scale=HD2 ** -0.5, scalar=0.0, op0=ALU.mult, op1=ALU.add, accum_out=den))
            dve.seq(nc.vector.scalar_tensor_tensor(floor, den, -1.0, floor, ALU.mult, ALU.max))
            dve.seq(nc.vector.tensor_tensor(den, den, floor, ALU.max))
            s["recip"] = dve.did(nc.vector.reciprocal(recip, den))
            s["r"] = recip

        def flip(i):
            u, s = units[i], st[i]
            k = u["keys"]
            kt = -(-k // P)
            bank = self.ps[4 + i % R]
            pe.wait(s["exp"])
            if i >= R:
                pe.wait(st[i - R]["eT"])
            for c in range(kt):
                w = min(P, k - c * P)
                ins = nc.tensor.transpose(bank[0:w, c * P:(c + 1) * P], s["e"][:, c * P:c * P + w], self.c("ident"))
            s["flipped"] = pe.did(ins)
            q = act if i % 2 else dve
            q.wait(s["flipped"])
            if i >= R:
                q.wait(st[i - R]["mixed"])
            w = min(P, k)
            s["eT_buf"] = self.sm_eT[0:w, (i % R) * S:(i % R) * S + kt * P]
            ins = (nc.scalar.activation(s["eT_buf"], bank[0:w, 0:kt * P], ACT.Copy) if q is act
                   else nc.vector.tensor_copy(s["eT_buf"], bank[0:w, 0:kt * P]))
            s["eT"] = q.did(ins)

        def mix(i):
            u, s = units[i], st[i]
            kt = -(-u["keys"] // P)
            o = self.ps[6 + i % R][:, 0:u["dv"]]
            pe.wait(s["eT"])
            if i >= R:
                pe.wait(st[i - R]["out"])
            for c in range(kt):
                ins = nc.tensor.matmul(o, s["eT_buf"][:, c * P:(c + 1) * P], u["v"][c], start=(c == 0), stop=(c == kt - 1))
            s["mixed"] = pe.did(ins)
            dve.wait(s["mixed"], s["recip"])
            s["out"] = u["out"](o, s["r"])

        for w in range(n + 2):
            if w < n:
                scores(w)
                soften(w)
            if 0 <= w - 1 < n:
                flip(w - 1)
            if 0 <= w - 2 < n:
                mix(w - 2)

    def stage_q(self, src, dst):
        nc, pe, act = self.nc, self.pe, self.act
        d = src.shape[2]
        q = self.q_stage[:, 0:T * d].rearrange("p (t d) -> p t d", t=T)
        m = act.did(nc.scalar.activation(q, src, ACT.Copy))
        pe.wait(m)
        pe.hold(self.passed)
        for t in range(T):
            ins = nc.tensor.transpose(self.ps[0][0:d, t * P:(t + 1) * P], q[:, t, :], self.c("ident"))
        m = pe.did(ins)
        act.wait(m)
        m = act.did(nc.scalar.activation(dst, self.ps[0][0:d, 0:S], ACT.Copy))
        pe.wait(m)

    def causal(self, t):
        return self.c("causal")[:, P:2 * P] if t == 0 else self.c("causal")

    def scaled(self, out, O, r):
        return self.dve.did(self.nc.vector.tensor_scalar(out, O, r, None, ALU.mult))

    def gate_with_silu(self, z, out):
        nc, act, dve = self.nc, self.act, self.dve
        for t in range(T):
            m = act.did(nc.scalar.activation(z[:, t, :], z[:, t, :], ACT.Silu))
            dve.wait(m)
            m = dve.did(nc.vector.tensor_tensor(out[:, t, :], out[:, t, :], z[:, t, :], ALU.mult))

    def project_out(self, W):
        nc, dve, pe = self.nc, self.dve, self.pe
        self.meet()
        self.transpose_tokens(self.mixed, self.hT)
        self.meet()
        ready = self.project_tokens(self.hT, W, D, 0, D, self.mixed)
        for t in range(T):
            dve.wait(ready(D))
            m = dve.did(nc.vector.tensor_tensor(self.x[:, t, :], self.x[:, t, :], self.mixed[:, t, :], ALU.add))
        self.meet()

    def load_params(self):
        nc, A = self.nc, self.A
        self.rowstat = self.take_fixed("rowstat", 64)
        self.minus_half = self.take_fixed("minus_half", 32)
        self.small.count(nc.scalar.dma_start(self.const[:, :], A["const_small"]))
        for t in range(T):
            self.small.count(nc.scalar.dma_start(self.x[:, t, :], A["x"][0, t * P:(t + 1) * P, :]))
        self.g_norm = [self.param_cols(A["norm_gain"][i], KC) for i in range(2)]
        self.g_mem = self.param_cols(A["mem_norm_gain"], KC)
        self.g_memqk = [[self.param(A["mem_qk_gain"][i, j], HD) for j in range(2)] for i in range(2)]
        self.g_nsa = [self.param(A["nsa_qk_gain"][0, j], HD) for j in range(4)]
        self.g_diff = [self.param(A["diff_qk_gain"][0, j], HD2) for j in range(2)]
        self.g_subln = self.param(A["diff_subln_gain"][0], HD)
        self.g_dsa = [self.param(A["dsa_qk_gain"][0, j], HD) for j in range(2)]
        self.lam = self.param(A["diff_lambda"][0].rearrange("a b -> (a b)"), 4 * HD2)
        self.second_params()
        nc.gpsimd.memset(self.minus_half[:, :], -0.5).then_inc(self.pool.sem, 1)
        self.pool.k += 1
        self.params_landed = self.small.now()
        for q in (self.pe, self.act, self.dve, self.pool):
            q.wait(self.params_landed)
        dve = self.dve
        for g, d in ((self.g_nsa[0], HD), (self.g_dsa[0], HD), (self.g_diff[0], HD2),
                     (self.g_memqk[0][0], HD), (self.g_memqk[1][0], HD)):
            dve.seq(nc.vector.tensor_scalar(g, g, -float(d) ** -0.5, None, ALU.mult))
        self.meet()

    def take_fixed(self, name, cols):
        t = self.work[:, self.work_at:self.work_at + cols]
        self.work_at += cols
        self.work_fixed = self.work_at
        return t

    def fresh_work(self):
        self.meet()
        self.work_at = self.work_fixed

    def attention_buffers(self):
        self.sm_s = self.take(3 * S)
        self.sm_e = self.take(3 * S)
        self.sm_eT = self.take(2 * S)
        self.sm_stat = self.take(12)
        self.q_stage = self.take(T * P)
        self.qT = self.take(S)
        self.prep_tmp = self.take(12 * HD)
        self.rope_tmp = self.take(12 * HD // 2)

    def memory_kv(self, i):
        ready = self.project_tokens(self.hT, self.A["mem_w_kv"][i], D, 0, 1024, self.mkv)
        return ready

    def first_block(self):
        nc, A, pe, act, dve, pool = self.nc, self.A, self.pe, self.act, self.dve, self.pool
        self.mkv = [self.proj[:, 8192 * i:8192 * i + 2048].rearrange("p (t n) -> p t n", t=T) for i in range(2)]
        self.memkT = [self.proj[:, 14336 + i * 4 * S:14336 + (i + 1) * 4 * S] for i in range(2)]
        self.memv = [self.take_fixed(f"memv{i}", T * 512) for i in range(2)]
        for t in range(T):
            m = self.work_ld.count(nc.scalar.dma_start(self.proj[:, t * D:(t + 1) * D], A["mem"][0, t * P:(t + 1) * P, :]))
        act.wait(m)
        dve.wait(m)
        self.norm_to_hT(self.proj[:, 0:T * D].rearrange("p (t n) -> p t n", t=T), self.g_mem)
        self.attention_buffers()
        for i in range(2):
            kv = self.mkv[i]
            ready = self.project_tokens(self.hT, A["mem_w_kv"][i], D, 0, 1024, kv)
            dve.wait(ready(1024))
            self.prep(lambda t: kv[:, t, 0:512].rearrange("p (n d) -> p n d", d=HD), 4, HD, self.g_memqk[i][1], False)
            for t in range(T):
                m = dve.did(nc.vector.tensor_copy(self.memv[i][:, t * 512:(t + 1) * 512], kv[:, t, 512:1024]))
            self.meet()
            self.transpose_tokens(kv[:, :, 0:512], self.memkT[i].rearrange("p (c s) -> p c s", c=4))
            self.meet()
        self.even_layer()
        self.odd_layer()
        self.meet()

    def memory_heads(self, i, pr, q_col, out_col):
        nc = self.nc
        mv = self.memv[i].rearrange("p (t n) -> p t n", t=T)
        kT = self.memkT[i].rearrange("p (h s) -> p h s", h=4)
        with self.loop(4, ("pe", "act", "dve", "pool"), **self.per["mem"]) as h:
            self.meet()
            self.stage_q(pr[:, :, ds(h * HD + q_col, HD)], self.qT)
            self.attention([dict(qT=self.qT[:, t * P:(t + 1) * P], kT=kT[:, ds(h, 1), :].rearrange("p a s -> p (a s)"), keys=S,
                                 mask=self.c("zeros"), v=[mv[:, c, ds(h * HD, HD)] for c in range(T)], dv=HD,
                                 out=lambda O, r, t=t: self.scaled(self.mixed[:, t, ds(h * HD + out_col, HD)], O, r))
                            for t in range(T)])
        self.meet()

    per = dict(mem=dict(pe=7, act=5, dve=9),
               nsa=dict(pe=19, act=11, dve=35), diff=dict(pe=16, act=14, dve=20), dsa=dict(pe=7, act=5, dve=9),
               idx=dict(pe=3, act=4, dve=2), ret=dict(pe=4, act=4, dve=4), mlstm=dict(pe=18, act=12, dve=36), rwkv=dict(pe=71, act=32, dve=84))

    def even_layer(self):
        nc, A, pe, act, dve, pool = self.nc, self.A, self.pe, self.act, self.dve, self.pool
        E = EVEN
        self.fresh_work()
        self.attention_buffers()
        self.norm_to_hT(self.x, self.g_norm[0])
        pr = self.proj[:, 0:T * EVEN_IN].rearrange("p (t n) -> p t n", t=T)
        kvT = self.take(4 * S).rearrange("p (c s) -> p c s", c=4)
        rawT = self.take(S)
        blkT = self.take(CMP_LEN * 2 * NCMP).rearrange("p (l g c) -> p l g c", l=CMP_LEN, g=2)
        peT = self.take(CMP_LEN)
        pe_rows = self.take(HD)
        hid = self.take(CMP_HID)
        hidT = self.take(2 * 2 * NCMP)
        kc = self.take(HD)
        kcT = self.take(2 * NCMP)
        vc = self.take(HD)
        w2 = [self.take(2 * HD).rearrange("p (c n) -> p c n", c=2) for _ in range(2)]
        pos = [pe_rows, self.take(HD)]
        for j in range(2):
            m = self.work_ld.count(nc.scalar.dma_start(w2[j], A["nsa_cmp_w2"][0, j].rearrange("(c p) n -> p c n", p=P)))
            m = self.work_ld.count(nc.scalar.dma_start(pos[j][0:CMP_LEN, :], A["nsa_cmp_pos"][0, j]))
        pe.wait(m)

        ready = self.project_tokens(self.hT, A["even_w_in"][0], D, 0, EVEN_IN, pr)
        heads = lambda col, n, d: (lambda t: pr[:, t, col:col + n * d].rearrange("p (n d) -> p n d", d=d))
        dve.wait(ready(1024))
        self.prep(heads(E["a_q"], 8, HD), 8, HD, self.g_nsa[0], True)
        dve.wait(ready(2560))
        self.prep(heads(E["a_kv"] + 2 * 256, 2, HD), 2, HD, self.g_nsa[2], True)
        self.prep(heads(E["a_kv"] + 4 * 256, 2, HD), 2, HD, self.g_nsa[3], True)
        dve.wait(ready(4632))
        self.prep(heads(E["b_q"], 8, HD2), 8, HD2, self.g_diff[0], True)
        self.prep(heads(E["b_k"], 8, HD2), 8, HD2, self.g_diff[1], True)
        dve.wait(ready(EVEN_IN))
        self.prep(heads(E["m_q"], 4, HD), 4, HD, self.g_memqk[0][0], False)
        self.meet()
        act.seq(nc.scalar.activation(pr[:, :, E["a_g"]:E["a_z"]], pr[:, :, E["a_g"]:E["a_z"]], ACT.Sigmoid))

        w1 = [A["nsa_cmp_w1"][0, j].rearrange("(u l p) n -> u p l n", l=8, p=P) for j in range(2)]
        for j in range(2):
            pe.seq(nc.tensor.transpose(self.ps[2][:, 0:CMP_LEN], pos[j][0:CMP_LEN, :], self.c("ident")[0:CMP_LEN, 0:CMP_LEN]))
            dve.wait(pe.now())
            dve.seq(nc.vector.tensor_copy(peT, self.ps[2][:, 0:CMP_LEN]))
            for g in range(2):
                col = E["a_kv"] + j * 256 + g * HD
                if g:
                    pe.wait(dve.now())
                for t in range(T):
                    ins = nc.tensor.transpose(self.ps[3][:, t * P:(t + 1) * P], pr[:, t, col:col + HD], self.c("ident"))
                dve.wait(pe.did(ins))
                dve.seq(nc.vector.tensor_copy(rawT, self.ps[3][:, 0:S]))
                win = bass.AP(rawT.tensor, rawT.offset, [rawT.ap[0], [1, CMP_LEN], [CMP_STRIDE, NCMP]])
                dve.seq(nc.vector.tensor_tensor(blkT[:, :, g, :], win, peT.unsqueeze(2).broadcast_to([P, CMP_LEN, NCMP]), ALU.add))
            pe.wait(dve.now())
            for u in range(4):
                slot = u % SLOTS
                full, freed = self.full[slot], self.freed[slot]
                nc.sync.wait_ge(freed.sem, freed.base + freed.k)
                wv = self.ring[slot][:, :, :].rearrange("p c n -> p (c n)").rearrange("p (l n) -> p l n", l=8)
                full.count(nc.sync.dma_start(wv, w1[j][u]))
                pe.wait(full.now())
                for l in range(8):
                    k = u * 8 + l
                    ins = nc.tensor.matmul(self.ps[4][0:2 * NCMP, 0:CMP_HID], blkT[:, k, :, :].rearrange("p g c -> p (g c)"), wv[:, l, :],
                                           start=(k == 0), stop=(k == CMP_LEN - 1))
                released = freed.count(ins)
            act.wait(released)
            act.seq(nc.scalar.activation(hid[0:2 * NCMP, :], self.ps[4][0:2 * NCMP, 0:CMP_HID], ACT.Silu))
            pe.wait(act.now())
            for c in range(2):
                ins = nc.tensor.transpose(self.ps[5][:, c * 2 * NCMP:(c + 1) * 2 * NCMP], hid[0:2 * NCMP, c * P:(c + 1) * P],
                                          self.c("ident")[0:2 * NCMP, 0:2 * NCMP])
            dve.wait(pe.did(ins))
            dve.seq(nc.vector.tensor_copy(hidT, self.ps[5][:, 0:4 * NCMP]))
            pe.wait(dve.now())
            for c in range(2):
                ins = nc.tensor.matmul(self.ps[6][0:2 * NCMP, 0:HD], hidT[:, c * 2 * NCMP:(c + 1) * 2 * NCMP], w2[j][:, c, :],
                                       start=(c == 0), stop=(c == 1))
            dve.wait(pe.did(ins))
            if j == 1:
                dve.seq(nc.vector.tensor_copy(vc[0:2 * NCMP, :], self.ps[6][0:2 * NCMP, 0:HD]))
            else:
                R2 = 2 * NCMP
                three = lambda a: a[0:R2, :].rearrange("p (n d) -> p n d", n=1)
                dve.seq(nc.vector.tensor_copy(kc[0:R2, :], self.ps[6][0:R2, 0:HD]))
                tmp = self.prep_tmp[:, 0:HD]
                self.head_norm(three(kc), three(tmp), 1, HD, self.g_nsa[1], rows=R2)
                self.rope(three(tmp), three(kc), 1, HD, self.c("cos_cmp")[0:R2], self.c("sin_cmp")[0:R2], rows=R2)
                pe.wait(dve.now())
                pe.seq(nc.tensor.transpose(self.ps[7][:, 0:R2], kc[0:R2, :], self.c("ident")[0:R2, 0:R2]))
                dve.wait(pe.now())
                dve.seq(nc.vector.tensor_copy(kcT, self.ps[7][:, 0:R2]))
            self.meet()

        self.transpose_tokens(pr[:, :, E["a_kv"] + 512:E["a_kv"] + 768], kvT[:, 0:2, :])
        self.meet()
        self.transpose_tokens(pr[:, :, E["a_kv"] + 1024:E["a_kv"] + 1280], kvT[:, 2:4, :])
        self.meet()
        gates = pr[:, :, E["a_g"]:E["a_z"]]
        for g in range(2):
            with self.loop(4, ("pe", "act", "dve", "pool"), **self.per["nsa"]) as r:
                self.meet()
                self.stage_q(pr[:, :, ds(r * HD + g * 4 * HD, HD)], self.qT)
                units = []
                for t in range(T):
                    for b in range(3):
                        def out(O, rc, t=t, b=b):
                            dst = self.mixed[:, t, ds(r * HD + g * 4 * HD, HD)]
                            dve.seq(nc.vector.tensor_tensor(self.coef, rc, gates[:, t, ds(r * 3 + (g * 12 + b), 1)], ALU.mult))
                            if b == 0:
                                return dve.seq(nc.vector.tensor_scalar(dst, O, self.coef, None, ALU.mult))
                            return dve.seq(nc.vector.scalar_tensor_tensor(dst, O, self.coef, dst, ALU.mult, ALU.add))
                        u = dict(qT=self.qT[:, t * P:(t + 1) * P], dv=HD, out=out)
                        if b == 0:
                            u.update(kT=kcT, keys=2 * NCMP, mask=self.c(f"cmp_drop{g}{t}"), keep=self.c(f"cmp_keep{g}{t}"),
                                     v=[vc[0:2 * NCMP, :]])
                        else:
                            vcol = E["a_kv"] + (3 if b == 1 else 5) * 256 + g * HD
                            u.update(kT=kvT[:, 2 * (b - 1) + g, 0:(t + 1) * P], keys=(t + 1) * P, mask=self.causal(t),
                                     v=[pr[:, c, vcol:vcol + HD] for c in range(t + 1)])
                        units.append(u)
                self.attention(units)
            self.meet()

        lam, lt = self.rowstat[:, 20:24], self.prep_tmp
        for j in range(2):
            dve.seq(nc.vector.tensor_tensor(lt[:, 0:HD2], self.lam[:, 2 * j * HD2:(2 * j + 1) * HD2],
                                            self.lam[:, (2 * j + 1) * HD2:(2 * j + 2) * HD2], ALU.mult))
            dve.seq(nc.vector.tensor_reduce(lam[:, j:j + 1], lt[:, 0:HD2], AX.X, ALU.add))
        act.wait(dve.now())
        act.seq(nc.scalar.activation(lam[:, 0:2], lam[:, 0:2], ACT.Exp))
        dve.wait(act.now())
        dve.seq(nc.vector.tensor_tensor(lam[:, 2:3], lam[:, 1:2], lam[:, 0:1], ALU.subtract))
        dve.seq(nc.vector.tensor_scalar(lam[:, 2:3], lam[:, 2:3], LAMBDA_INIT, None, ALU.subtract))
        kT2 = self.take(2 * S)
        self.meet()
        with self.loop(4, ("pe", "act", "dve", "pool"), **self.per["diff"]) as h:
            self.meet()
            units = []
            for c in range(2):
                self.stage_q(pr[:, :, ds(h * HD + (E["b_q"] + c * HD2), HD2)], self.q2[0:HD2, c * S:(c + 1) * S])
                self.stage_q(pr[:, :, ds(h * HD + (E["b_k"] + c * HD2), HD2)], kT2[0:HD2, c * S:(c + 1) * S])
            for t in range(T):
                for c in range(2):
                    def out(O, rc, t=t, c=c):
                        dst = self.mixed[:, t, ds(h * HD + 1024, HD)]
                        if c == 0:
                            return dve.seq(nc.vector.tensor_scalar(dst, O, rc, None, ALU.mult))
                        dve.seq(nc.vector.tensor_tensor(self.coef, rc, lam[:, 2:3], ALU.mult))
                        return dve.seq(nc.vector.scalar_tensor_tensor(dst, O, self.coef, dst, ALU.mult, ALU.add))
                    units.append(dict(qT=self.q2[0:HD2, c * S + t * P:c * S + (t + 1) * P], dv=HD, out=out,
                                      kT=kT2[0:HD2, c * S:c * S + (t + 1) * P], keys=(t + 1) * P, mask=self.causal(t),
                                      v=[pr[:, k, ds(h * HD + E["b_v"], HD)] for k in range(t + 1)]))
            self.attention(units)
        self.meet()
        for t in range(T):
            o = self.mixed[:, t, 1024:1536].rearrange("p (n d) -> p n d", d=HD)
            tmp = self.prep_tmp[:, 0:512].rearrange("p (n d) -> p n d", d=HD)
            self.head_norm(o, tmp, 4, HD, self.g_subln)
            dve.seq(nc.vector.tensor_scalar(o, tmp, 1.0 - LAMBDA_INIT, None, ALU.mult))
        self.meet()
        self.memory_heads(0, pr, E["m_q"], 1536)
        self.gate_with_silu(pr[:, :, E["a_z"]:E["a_z"] + 1024], self.mixed[:, :, 0:1024])
        self.gate_with_silu(pr[:, :, E["b_z"]:E["b_z"] + 512], self.mixed[:, :, 1024:1536])
        self.gate_with_silu(pr[:, :, E["m_z"]:E["m_z"] + 512], self.mixed[:, :, 1536:2048])
        self.project_out(A["w_out"][0])

    def odd_layer(self):
        nc, A, pe, act, dve, pool = self.nc, self.A, self.pe, self.act, self.dve, self.pool
        O_ = ODD
        self.fresh_work()
        self.attention_buffers()
        self.norm_to_hT(self.x, self.g_norm[1])
        pr = self.proj[:, 0:T * ODD_IN].rearrange("p (t n) -> p t n", t=T)
        kT = self.take(4 * S).rearrange("p (c s) -> p c s", c=4)
        kiT = self.take(S)
        score = self.take(T * S).rearrange("p (t s) -> p t s", t=T)
        drop = self.take(T * S).rearrange("p (t s) -> p t s", t=T)
        rel = self.take(T * S).rearrange("p (t s) -> p t s", t=T)
        best = self.take(8 * T)
        ready = self.project_tokens(self.hT, A["odd_w_in"][0], D, 0, ODD_IN, pr)
        heads = lambda col, n, d: (lambda t: pr[:, t, col:col + n * d].rearrange("p (n d) -> p n d", d=d))
        dve.wait(ready(1536))
        self.prep(heads(O_["c_q"], 12, HD), 12, HD, self.g_dsa[0], True)
        dve.wait(ready(2048))
        self.prep(heads(O_["c_k"], 4, HD), 4, HD, self.g_dsa[1], True)
        dve.wait(ready(3664))
        self.prep(heads(O_["i_q"], 16, HD2), 16, HD2, None, True, norm=False)
        self.prep(heads(O_["i_k"], 1, HD2), 1, HD2, None, True, norm=False)
        wi = pr[:, :, O_["i_w"]:O_["c_z"]]
        dve.seq(nc.vector.tensor_scalar(wi, wi, 16.0 ** -0.5 * 64.0 ** -0.5, None, ALU.mult))
        dve.wait(ready(ODD_IN))
        self.prep(heads(O_["m_q"], 4, HD), 4, HD, self.g_memqk[1][0], False)
        dve.seq(nc.vector.memset(score, 0.0))
        self.meet()
        self.transpose_tokens(pr[:, :, O_["c_k"]:O_["c_v"]], kT)
        self.meet()
        self.stage_q(pr[:, :, O_["i_k"]:O_["i_w"]], kiT[0:HD2, :])
        self.meet()
        with self.loop(16, ("pe", "act", "dve", "pool"), **self.per["idx"]) as h:
            self.meet()
            self.stage_q(pr[:, :, ds(h * HD2 + O_["i_q"], HD2)], self.q2[0:HD2, 0:S])
            for t in range(T):
                k = (t + 1) * P
                m = pe.did(nc.tensor.matmul(self.ps[2 + t][:, 0:k], self.q2[0:HD2, t * P:(t + 1) * P], kiT[0:HD2, 0:k],
                                            start=True, stop=True))
                act.wait(m)
                m = act.did(nc.scalar.activation(rel[:, t, 0:k], self.ps[2 + t][:, 0:k], ACT.Relu))
                dve.wait(m)
                dve.did(nc.vector.scalar_tensor_tensor(score[:, t, 0:k], rel[:, t, 0:k], pr[:, t, ds(h + O_["i_w"], 1)],
                                                       score[:, t, 0:k], ALU.mult, ALU.add))
        self.meet()
        TAKEN = -3e38
        for t in range(T):
            k = (t + 1) * P
            s_, m_ = score[:, t, 0:k], self.causal(t)
            dve.seq(nc.vector.tensor_tensor(s_, s_, m_, ALU.subtract))
        for rnd in range(TOPK // 8):
            for t in range(T):
                s_ = score[:, t, 0:(t + 1) * P]
                dve.did(nc.vector.max(best[:, 8 * t:8 * t + 8], s_))
            dve.wait(dve.now())
            for t in range(T):
                s_ = score[:, t, 0:(t + 1) * P]
                dve.did(nc.vector.match_replace(s_, best[:, 8 * t:8 * t + 8], s_, TAKEN))
            dve.wait(dve.now())
        for t in range(T):
            k = (t + 1) * P
            dve.seq(nc.vector.tensor_scalar(drop[:, t, 0:k], score[:, t, 0:k], -2e38, BIG, ALU.is_gt, ALU.mult))
            dve.seq(nc.vector.tensor_tensor(drop[:, t, 0:k], drop[:, t, 0:k], self.causal(t), ALU.add))
        for g in range(4):
            with self.loop(3, ("pe", "act", "dve", "pool"), **self.per["dsa"]) as r:
                self.meet()
                self.stage_q(pr[:, :, ds(r * HD + g * 3 * HD, HD)], self.qT)
                vcol = O_["c_v"] + g * HD
                self.attention([dict(qT=self.qT[:, t * P:(t + 1) * P], dv=HD, kT=kT[:, g, 0:(t + 1) * P], keys=(t + 1) * P,
                                     mask=drop[:, t, 0:(t + 1) * P], v=[pr[:, c, vcol:vcol + HD] for c in range(t + 1)],
                                     out=lambda O, rc, t=t: self.scaled(self.mixed[:, t, ds(r * HD + g * 3 * HD, HD)], O, rc))
                                for t in range(T)])
            self.meet()
        self.memory_heads(1, pr, O_["m_q"], 1536)
        self.gate_with_silu(pr[:, :, O_["c_z"]:O_["c_z"] + 1536], self.mixed[:, :, 0:1536])
        self.gate_with_silu(pr[:, :, O_["m_z"]:O_["m_z"] + 512], self.mixed[:, :, 1536:2048])
        self.project_out(A["w_out"][1])

    def main(self):
        self.coef = self.take_fixed("coef", 1)
        self.q2 = self.take_fixed("q2", 2 * S)
        self.work_second = self.work_fixed
        self.first_block()
        self.second_block()

    def second_params(self):
        A = self.A
        self.b2 = []
        for l in range(2):
            q = {}
            for name, n in (("norm_pre_mix_2", KC), ("norm_pre_ffn_2", KC), ("rwkv_mu_2", 14), ("rwkv_w0_2", 4),
                            ("rwkv_a0_2", 4), ("rwkv_k_k_2", 4), ("rwkv_k_a_2", 4), ("rwkv_r_k_2", 4),
                            ("mlstm_conv_b_2", 8)):
                q[name] = self.param_cols(A[name][l], n)
            q["conv"] = [self.param_cols(A["mlstm_conv_w_2"][l, j], 8) for j in range(4)]
            q["lb"] = self.param_cols(A["hgrn_lb_logits_2"][l], 4)
            q["ib"] = self.param(A["mlstm_i_bias_2"][l], H2)
            q["fb"] = self.param(A["mlstm_f_bias_2"][l], H2)
            self.b2.append(q)
        self.b2[1]["v0"] = self.param_cols(A["rwkv_v0_2"][0], 4)

    def load_row(self, dram_row, width):
        dst = self.take(width)
        self.work_ld.count(self.nc.scalar.dma_start(dst, dram_row.partition_broadcast(P)))
        return dst

    def load_work(self, dst, src):
        self.work_ld.count(self.nc.scalar.dma_start(dst, src))

    def work_landed(self):
        for q in (self.pe, self.act, self.dve, self.pool):
            q.wait(self.work_ld.now())

    def before(self, last):
        a = self.act
        return [a.now(3), a.now(2), a.now(1), a.now()] if last == "features" else [a.now(1), a.now(), a.now(2), a.now(2)]

    def second_block(self):
        self.work_at = self.work_second
        self.v_first = self.take(4 * S)
        self.work_second = self.work_at
        for l in range(2):
            self.second_layer(l)

    def second_layer(self, l):
        nc, A, pe, act, dve, pool = self.nc, self.A, self.pe, self.act, self.dve, self.pool
        self.meet()
        self.work_at = self.work_fixed = self.work_second
        q = self.b2[l]
        self.norm_to_hT(self.x, q["norm_pre_mix_2"])
        NT = 8 * GW + 2 * H2
        pt = self.proj[:, 0:T * NT].rearrange("p (t n) -> p t n", t=T)
        pf = self.proj[:, T * NT:T * NT + 30 * S].rearrange("p (c s) -> p c s", c=30)
        W = A["w_in_2"][l]
        Wu = self.units_of(W)
        self.project_tokens(self.hT, W, D, 0, 4 * GW, pt)
        slots = {k: 4 * v for k, v in self.per_slot(4).items()}
        fm = lambda c0, i, w: (lambda j: pf[:, ds(i * w + (c0 + j), 1), :].rearrange("p a s -> p (a s)"))
        with self.loop(2, ("pe", "act", "sp"), pe=2 * 3 + 2 * (T - 1), act=8 + 2 * T, **slots) as i:
            c0 = 4 * GW
            self.tile_features(self.hT, Wu, 4, i * 4 * GW + c0, 4, fm(0, i, 8), self.before("tokens"))
            self.tile_features(self.hT, Wu, 4, i * 4 * GW + (c0 + GW), 4, fm(4, i, 8), self.before("features"))
            self.tile_tokens(self.hT, Wu, 4, i * 4 * GW + (c0 + 2 * GW), TILE,
                             lambda t: pt[:, t, ds(i * 2 * GW + 4 * GW, GW)], self.before("features"))
            self.tile_tokens(self.hT, Wu, 4, i * 4 * GW + (c0 + 3 * GW), TILE,
                             lambda t: pt[:, t, ds(i * 2 * GW + 5 * GW, GW)], self.before("tokens"))
        self.tile_tokens(self.hT, Wu, 4, 12 * GW, 2 * H2, lambda t: pt[:, t, 8 * GW:NT], self.before("tokens"))
        rw = 12 * GW + 2 * H2
        self.tile_features(self.hT, Wu, 4, rw + 3 * GW, 2, lambda j: pf[:, 28 + j, :], self.before("tokens"))
        with self.loop(3, ("pe", "act", "sp"), pe=3, act=4, **self.per_slot(4)) as i:
            b = act.now()
            self.tile_features(self.hT, Wu, 4, i * GW + rw, 4, fm(16, i, 4), [b, b, b, b])
        self.meet()
        self.retention(l, pt)
        self.hgrn(l, pt, pf)
        self.mlstm(l, pt, pf)
        self.rwkv(l, pt, pf)
        self.work_at = self.work_fixed
        self.meet()
        self.transpose_tokens(self.mixed, self.hT)
        self.meet()
        gain = self.load_row(A["norm_post_mix_2"][l], D)
        ready = self.project_tokens(self.hT, A["w_out_2"][l], D, 0, D, self.mixed)
        self.add_normed(gain, ready(D))
        self.norm_to_hT(self.x, q["norm_pre_ffn_2"])
        self.work_at = self.work_fixed
        gain = self.load_row(A["norm_post_ffn_2"][l], D)
        actT = self.proj[:, 0:D_FF // P * S].rearrange("p (c s) -> p c s", c=D_FF // P)
        gate = self.take(4 * S).rearrange("p (c s) -> p c s", c=4)
        Gu, Uu = self.units_of(A["w_ffn_gate_2"][l]), self.units_of(A["w_ffn_up_2"][l])
        slots = {k: 2 * v for k, v in self.per_slot(4).items()}
        with self.loop(D_FF // TILE, ("pe", "act", "dve", "sp"), pe=6, act=4, dve=4, **slots) as i:
            gated = [act.now(3), act.now(2), act.now(1), act.now()]
            multiplied = [dve.now(3), dve.now(2), dve.now(1), dve.now()]

            def silu(j, mark):
                act.wait(mark, multiplied[j])
                return act.did(nc.scalar.activation(gate[:, j, :], self.ps[j][:, 0:S], ACT.Silu))
            silus = self.tile_features(self.hT, Gu, 4, i * TILE, 4, None, gated, 0, silu)

            def times(j, mark):
                dve.wait(mark, silus[j])
                return dve.did(nc.vector.tensor_tensor(actT[:, ds(i * 4 + j, 1), :].rearrange("p a s -> p (a s)"),
                                                       gate[:, j, :], self.ps[4 + j][:, 0:S], ALU.mult))
            self.tile_features(self.hT, Uu, 4, i * TILE, 4, None, multiplied, 4, times)
        self.meet()
        ready = self.project_tokens(actT, A["w_ffn_down_2"][l], D_FF, 0, D, self.mixed)
        self.add_normed(gain, ready(D))

    def add_normed(self, gain, ready):
        nc, act, dve = self.nc, self.act, self.dve
        ss = self.rowstat[:, 0:T]
        tmp = self.hT[:, :, :].rearrange("p c s -> p (c s)")
        self.pe.wait(ready)
        self.meet()
        for t in range(T):
            m = act.did(nc.scalar.activation(tmp[:, t * D:(t + 1) * D], self.mixed[:, t, :], ACT.Square, accum_out=ss[:, t:t + 1]))
        dve.wait(m)
        self.inv_rms(ss, T, D)
        dve.wait(self.work_ld.now())
        for t in range(T):
            dve.seq(nc.vector.scalar_tensor_tensor(self.mixed[:, t, :], self.mixed[:, t, :], ss[:, t:t + 1], gain, ALU.mult, ALU.mult))
            dve.seq(nc.vector.tensor_tensor(self.x[:, t, :], self.x[:, t, :], self.mixed[:, t, :], ALU.add))
        self.meet()

    def head_rms_gate(self, col, z, func, gain):
        nc, act, dve = self.nc, self.act, self.dve
        for t in range(T):
            o = self.mixed[:, t, col:col + GW].rearrange("p (n d) -> p n d", d=HD2)
            tmp = self.hT[:, 2 * t:2 * t + 2, :].rearrange("p c s -> p (c s)")
            self.head_norm(o, tmp.rearrange("p (n d) -> p n d", d=HD2), H2, HD2, None)
            if gain is not None:
                dve.seq(nc.vector.tensor_tensor(tmp, tmp, gain, ALU.mult))
            m = act.did(nc.scalar.activation(z[:, t, :], z[:, t, :], func))
            dve.wait(m)
            dve.seq(nc.vector.tensor_tensor(self.mixed[:, t, col:col + GW], tmp, z[:, t, :], ALU.mult))

    def pair(self, fm, j):
        return fm[:, ds(j, 1), :].rearrange("p a s -> p (a s)")

    def retention(self, l, pt):
        nc, pe, act, dve, pool = self.nc, self.pe, self.act, self.dve, self.pool
        self.fresh_work()
        self.prep_tmp, self.rope_tmp = self.take(GW), self.take(GW // 2)
        decay = self.take(H2 * 2 * P)
        self.load_work(decay, self.A["const_decay"])
        qT, kT = [self.take(4 * S).rearrange("p (c s) -> p c s", c=4) for _ in range(2)]
        qs, ks = self.take(S), self.take(S)
        sT = [self.take(3 * P) for _ in range(2)]
        for c in range(2):
            self.prep(lambda t: pt[:, t, c * GW:(c + 1) * GW].rearrange("p (n d) -> p n d", d=HD2), H2, HD2, None, True, norm=False)
        self.meet()
        self.transpose_tokens(pt[:, :, 0:GW], qT)
        self.meet()
        self.transpose_tokens(pt[:, :, GW:2 * GW], kT)
        self.meet()
        self.work_landed()
        dv = decay.rearrange("p (h n) -> p h n", h=H2)
        with self.loop(4, ("pe", "act", "dve", "pool"), **self.per["ret"]) as j:
            self.meet()
            act.did(nc.scalar.activation(qs, self.pair(qT, j), ACT.Copy))
            pe.wait(act.did(nc.scalar.activation(ks, self.pair(kT, j), ACT.Copy)))
            scored = []
            for e in range(2):
                h = slice(e * HD2, (e + 1) * HD2)
                b = self.ps[2 + e]
                nc.tensor.matmul(b[:, 0:S], ks[h, 0:P], qs[h, 0:S], start=True, stop=True)
                scored.append(pe.did(nc.tensor.matmul(b[:, S:S + P], ks[h, P:S], qs[h, P:S], start=True, stop=True)))
            for e in range(2):
                dve.wait(scored[e])
                dve.did(nc.vector.tensor_tensor(sT[e][:, 0:S], self.ps[2 + e][:, 0:S],
                                                dv[:, ds(j * 2 + e, 1), :].rearrange("p a n -> p (a n)"), ALU.mult))
                pe.wait(dve.did(nc.vector.tensor_tensor(sT[e][:, S:S + P], self.ps[2 + e][:, S:S + P],
                                                        dv[:, ds(j * 2 + e, 1), 0:P].rearrange("p a n -> p (a n)"), ALU.mult)))
                v = [pt[:, t, ds(j * 2 * HD2 + (2 * GW + e * HD2), HD2)] for t in range(T)]
                o = self.ps[4 + e]
                nc.tensor.matmul(o[:, 0:HD2], sT[e][:, 0:P], v[0], start=True, stop=True)
                nc.tensor.matmul(o[:, HD2:2 * HD2], sT[e][:, P:S], v[0], start=True, stop=False)
                act.wait(pe.did(nc.tensor.matmul(o[:, HD2:2 * HD2], sT[e][:, S:S + P], v[1], start=False, stop=True)))
                act.did(nc.scalar.activation(self.mixed[:, :, ds(j * 2 * HD2 + e * HD2, HD2)],
                                             o[:, 0:2 * HD2].rearrange("p (t d) -> p t d", t=T), ACT.Copy))
        self.meet()
        self.head_rms_gate(0, pt[:, :, 3 * GW:4 * GW], ACT.Silu, None)

    def cumulate(self, out, src, width):
        nc, dve = self.nc, self.dve
        n = src.shape[1]
        one = self.c("ones")[:, 0:1].broadcast_to([P, width])
        for k in range(0, n, width):
            dve.did(nc.vector.tensor_tensor_scan(out[:, k:k + width], one, src[:, k:k + width], 0.0, ALU.mult, ALU.add))
        dve.wait(dve.now())

    def hgrn(self, l, pt, pf):
        nc, pe, act, dve, pool = self.nc, self.pe, self.act, self.dve, self.pool
        self.fresh_work()
        flat = lambda a: a.rearrange("p c s -> p (c s)")
        q, f = flat(pf[:, 0:4, :]), flat(pf[:, 4:8, :])
        n = 4 * S
        masks = self.take(LEVELS * P)
        self.load_work(masks, self.A["const_halves_T"])
        gain = self.load_row(self.A["hgrn_norm_w_2"][l], GW)
        lb, keep = self.rowstat[:, 24:28], self.rowstat[:, 28:32]
        E, cum, k, qd, kd = [self.take(n) for _ in range(5)]
        acc = self.take(16 * P)
        cross = self.take(H2 * P)
        if l == 1:
            dve.seq(nc.vector.tensor_tensor(lb, self.b2[1]["lb"], self.b2[0]["lb"], ALU.subtract))
            act.wait(dve.now())
            act.seq(nc.scalar.activation(lb, lb, ACT.Sigmoid))
            dve.wait(act.now())
            dve.seq(nc.vector.tensor_scalar(keep, lb, -1.0, 1.0, ALU.mult, ALU.add))
        over = lambda a: a.unsqueeze(2).broadcast_to([P, 4, S])
        v3 = lambda a: a.rearrange("p (c s) -> p c s", c=4)
        act.did(nc.scalar.activation(k, f, ACT.Sigmoid, scale=-1.0))
        act.seq(nc.scalar.activation(q, q, ACT.Silu))
        act.seq(nc.scalar.activation(E, f, ACT.Abs))
        act.seq(nc.scalar.activation(E, E, ACT.Exp, scale=-1.0))
        act.seq(nc.scalar.activation(E, E, ACT.Ln, bias=1.0))
        dve.wait(act.now())
        dve.did(nc.vector.tensor_scalar(q, q, HD2 ** -0.5, None, ALU.mult))
        if l == 0:
            dve.seq(nc.vector.scalar_tensor_tensor(f, f, 0.0, E, ALU.min, ALU.subtract))
        else:
            dve.did(nc.vector.tensor_scalar(qd, f, 0.0, None, ALU.min))
            dve.did(nc.vector.tensor_scalar(kd, f, 0.0, None, ALU.max))
            dve.seq(nc.vector.tensor_tensor(v3(k), v3(k), over(keep), ALU.mult))
            act.wait(dve.now())
            act.did(nc.scalar.activation(qd, qd, ACT.Exp))
            act.did(nc.scalar.activation(kd, kd, ACT.Exp, scale=-1.0))
            dve.wait(act.now())
            dve.seq(nc.vector.tensor_tensor(v3(kd), v3(kd), over(lb), ALU.mult))
            dve.seq(nc.vector.tensor_tensor(qd, qd, kd, ALU.add))
            dve.seq(nc.vector.tensor_scalar(qd, qd, 2.0 ** -60, None, ALU.max))
            act.wait(dve.now())
            act.seq(nc.scalar.activation(qd, qd, ACT.Ln))
            dve.wait(act.now())
            dve.seq(nc.vector.tensor_tensor(f, qd, E, ALU.subtract))
        self.cumulate(cum, f, P)
        dve.seq(nc.vector.memset(acc, 0.0))
        self.work_landed()
        self.meet()
        heads = [(h // 2, slice((h % 2) * HD2, (h % 2 + 1) * HD2)) for h in range(H2)]

        def products(kk, qq, mask, first):
            k3, q3 = v3(kk), v3(qq)
            for g in range(4):
                b = self.ps[2 + g]
                if not first:
                    pe.wait(self.level_read[g])
                for i in range(4):
                    c, h = heads[4 * (g // 2) + g % 2 + 2 * (i // 2)]
                    t = i % 2
                    ins = nc.tensor.matmul(b[:, i * P:(i + 1) * P], k3[h, c, t * P:(t + 1) * P], q3[h, c, t * P:(t + 1) * P],
                                           start=True, stop=True)
                dve.wait(pe.did(ins))
                m = mask.bitcast(mybir.dt.uint32).unsqueeze(1).broadcast_to([P, 4, P])
                self.level_read[g] = dve.did(nc.vector.copy_predicated(
                    acc[:, g * 512:(g + 1) * 512].rearrange("p (i s) -> p i s", i=4), m,
                    b[:, :].rearrange("p (i s) -> p i s", i=4)))
        self.level_read = {}
        products(k, q, self.c("ident"), True)
        for lev in range(LEVELS):
            B = 1 << lev
            blk = lambda a: a.rearrange("p (n b) -> p n b", b=2 * B)
            c3 = blk(cum)
            if lev:
                dve.wait(self.exp_done)
            dve.seq(nc.vector.tensor_tensor(blk(E), c3, c3[:, :, B - 1:B].broadcast_to([P, n // (2 * B), 2 * B]), ALU.subtract))
            act.wait(dve.now())
            act.seq(nc.scalar.activation(E, E, ACT.Abs))
            self.exp_done = act.seq(nc.scalar.activation(E, E, ACT.Exp, scale=-1.0))
            dve.wait(act.now(), pe.now())
            dve.did(nc.vector.tensor_tensor(qd, q, E, ALU.mult))
            dve.seq(nc.vector.tensor_tensor(kd, k, E, ALU.mult))
            pe.wait(dve.now())
            products(kd, qd, masks[:, lev * P:(lev + 1) * P], False)
        c3, E3, qd3, kd3 = v3(cum), v3(E), v3(qd), v3(kd)
        dve.seq(nc.vector.tensor_tensor(E3[:, :, 0:P], c3[:, :, P - 1:P].broadcast_to([P, 4, P]), c3[:, :, 0:P], ALU.subtract))
        dve.seq(nc.vector.tensor_copy(E3[:, :, P:S], c3[:, :, P:S]))
        act.wait(dve.now())
        act.seq(nc.scalar.activation(E, E, ACT.Exp))
        dve.wait(act.now(), pe.now())
        dve.did(nc.vector.tensor_tensor(kd3[:, :, 0:P], v3(k)[:, :, 0:P], E3[:, :, 0:P], ALU.mult))
        dve.seq(nc.vector.tensor_tensor(qd3[:, :, P:S], v3(q)[:, :, P:S], E3[:, :, P:S], ALU.mult))
        pe.wait(dve.now())
        for g in range(2):
            for i in range(4):
                c, h = heads[g + 2 * i]
                ins = nc.tensor.matmul(self.ps[6 + g][:, i * P:(i + 1) * P], kd3[h, c, 0:P], qd3[h, c, P:S], start=True, stop=True)
            act.wait(pe.did(ins))
            pe.wait(act.did(nc.scalar.activation(cross[:, g * 512:(g + 1) * 512], self.ps[6 + g][:, :], ACT.Copy)))
        i0 = 4 * GW
        for t in range(T):
            o = self.ps[t]
            for h in range(H2):
                v = [pt[:, c, i0 + h * HD2:i0 + (h + 1) * HD2] for c in range(T)]
                at = 4 * (2 * (h // 4) + h % 2) + 2 * ((h % 4) // 2) + t
                a = acc[:, at * P:(at + 1) * P]
                x = cross[:, (4 * (h % 2) + h // 2) * P:(4 * (h % 2) + h // 2 + 1) * P]
                ins = nc.tensor.matmul(o[:, h * HD2:(h + 1) * HD2], a, v[t], start=True, stop=(t == 0))
                if t:
                    ins = nc.tensor.matmul(o[:, h * HD2:(h + 1) * HD2], x, v[0], start=False, stop=True)
            act.wait(pe.did(ins))
            act.did(nc.scalar.activation(self.mixed[:, t, GW:2 * GW], o[:, :], ACT.Copy))
        self.meet()
        self.head_rms_gate(GW, pt[:, :, 5 * GW:6 * GW], ACT.Sigmoid, gain)

    def mlstm(self, l, pt, pf):
        nc, pe, act, dve, pool = self.nc, self.pe, self.act, self.dve, self.pool
        q_ = self.b2[l]
        self.fresh_work()
        gain = self.load_row(self.A["mlstm_norm_w_2"][l], GW)
        self.sm_s, self.sm_e, self.sm_eT, self.sm_stat = self.take(3 * S), self.take(3 * S), self.take(2 * S), self.take(24)
        gates = self.take(4 * T * H2).rearrange("p (k t h) -> p k t h", k=4, t=T)
        li, lf, cum, G = [gates[:, k, :, :] for k in range(4)]
        qs, ks, gs, fs = self.take(S), self.take(S), self.take(T * 2), self.take(T * 2)
        for c in range(8):
            src, dst = pf[:, 8 + c, :], pf[:, c, :]
            w = [x[:, c:c + 1] for x in q_["conv"]]
            dve.seq(nc.vector.tensor_scalar(dst, src, w[3], q_["mlstm_conv_b_2"][:, c:c + 1], ALU.mult, ALU.add))
            for d in range(1, 4):
                dve.seq(nc.vector.scalar_tensor_tensor(dst[:, d:S], src[:, 0:S - d], w[3 - d], dst[:, d:S], ALU.mult, ALU.add))
        act.wait(dve.now())
        qk = pf[:, 0:8, :].rearrange("p c s -> p (c s)")
        act.seq(nc.scalar.activation(qk, qk, ACT.Silu))
        raw = pt[:, :, 8 * GW:8 * GW + 2 * H2]
        row = lambda a: a.unsqueeze(1).broadcast_to([P, T, H2])
        dve.did(nc.vector.tensor_tensor(li, raw[:, :, 0:H2], row(q_["ib"]), ALU.add))
        dve.seq(nc.vector.tensor_tensor(lf, raw[:, :, H2:2 * H2], row(q_["fb"]), ALU.add))
        act.wait(dve.now())
        act.seq(nc.scalar.activation(G, lf, ACT.Abs))
        act.seq(nc.scalar.activation(G, G, ACT.Exp, scale=-1.0))
        act.seq(nc.scalar.activation(G, G, ACT.Ln, bias=1.0))
        dve.wait(act.now())
        dve.seq(nc.vector.scalar_tensor_tensor(lf, lf, 0.0, G, ALU.min, ALU.subtract))
        pe.wait(dve.now())
        nc.tensor.matmul(self.ps[2][:, 0:H2], self.c("upto_T"), lf[:, 0, :], start=True, stop=True)
        nc.tensor.matmul(self.ps[2][:, H2:2 * H2], self.c("ones"), lf[:, 0, :], start=True, stop=False)
        dve.wait(pe.did(nc.tensor.matmul(self.ps[2][:, H2:2 * H2], self.c("upto_T"), lf[:, 1, :], start=False, stop=True)))
        dve.seq(nc.vector.tensor_copy(cum, self.ps[2][:, 0:2 * H2].rearrange("p (t h) -> p t h", t=T)))
        dve.seq(nc.vector.tensor_tensor(G, li, cum, ALU.subtract))
        self.meet()
        st3 = lambda a: a.rearrange("p (t e) -> p t e", t=T)
        with self.loop(4, ("pe", "act", "dve", "pool"), **self.per["mlstm"]) as j:
            self.meet()
            act.did(nc.scalar.activation(qs, self.pair(pf[:, 0:4, :], j), ACT.Copy))
            act.did(nc.scalar.activation(ks, self.pair(pf[:, 4:8, :], j), ACT.Copy))
            dve.did(nc.vector.tensor_copy(st3(gs), G[:, :, ds(j * 2, 2)]))
            dve.seq(nc.vector.tensor_copy(st3(fs), cum[:, :, ds(j * 2, 2)]))
            pe.wait(act.now(), dve.now())
            units = []
            for e in range(2):
                h = slice(e * HD2, (e + 1) * HD2)
                for t in range(T):
                    units.append(dict(
                        mlstm=True, qT=qs[h, t * P:(t + 1) * P], kT=ks[h, 0:(t + 1) * P], keys=(t + 1) * P, mask=self.causal(t),
                        gates=[st3(gs)[:, c, e:e + 1] for c in range(t + 1)], F=st3(fs)[:, t, e:e + 1], dv=HD2,
                        v=[pt[:, c, ds(j * 2 * HD2 + (6 * GW + e * HD2), HD2)] for c in range(t + 1)],
                        out=lambda O, r, t=t, e=e: self.scaled(self.mixed[:, t, ds(j * 2 * HD2 + (2 * GW + e * HD2), HD2)], O, r)))
            self.attention(units)
        self.meet()
        self.work_landed()
        self.head_rms_gate(2 * GW, pt[:, :, 7 * GW:8 * GW], ACT.Sigmoid, gain)

    def rwkv(self, l, pt, pf):
        nc, pe, act, dve, pool = self.nc, self.pe, self.act, self.dve, self.pool
        q_, A = self.b2[l], self.A
        self.fresh_work()
        lora, g_up = self.take(GW), self.take(GW)
        self.load_work(lora[0:64, :], A["rwkv_w_up_2"][l])
        self.load_work(lora[64:128, :], A["rwkv_a_up_2"][l])
        self.load_work(g_up, A["rwkv_g_up_2"][l])
        masks_T, low = self.take(LEVELS * P), self.take(P)
        self.load_work(masks_T, A["const_halves_T"])
        self.load_work(low, A["const_halves"][:, 0:P])
        vt = self.take(T * GW).rearrange("p (t n) -> p t n", t=T)
        gt = self.take(T * GW).rearrange("p (t n) -> p t n", t=T)
        col = lambda a, c: a[:, c:c + 1]
        over = lambda a: a.unsqueeze(2).broadcast_to([P, 4, S])
        p, d = pf[:, 16:30, :], pf[:, 0:14, :]
        dve.did(nc.vector.tensor_tensor(d[:, :, 1:S], p[:, :, 0:S - 1], p[:, :, 1:S], ALU.subtract))
        dve.seq(nc.vector.tensor_scalar(d[:, :, 0:1], p[:, :, 0:1], -1.0, None, ALU.mult))
        for c in range(14):
            dve.did(nc.vector.scalar_tensor_tensor(p[:, c, :], d[:, c, :], col(q_["rwkv_mu_2"], c), p[:, c, :], ALU.mult, ALU.add))
        dve.wait(dve.now())
        r, k, v, wa, gd = pf[:, 16:20, :], pf[:, 20:24, :], pf[:, 24:28, :], pf[:, 28, :], pf[:, 29, :]
        lw, a, kk, L = pf[:, 0:4, :], pf[:, 4:8, :], pf[:, 8:12, :], pf[:, 12:16, :]
        act.wait(dve.now())
        act.did(nc.scalar.activation(wa[0:64, :], wa[0:64, :], ACT.Tanh))
        act.seq(nc.scalar.activation(gd, gd, ACT.Sigmoid))
        self.work_landed()
        self.meet()
        if l == 1:
            vd = self.take(4 * 32).rearrange("p (c n) -> p c n", c=4)
            vu, low_v, mix = self.take(GW), self.take(S), self.take(S)
            self.load_work(vd, A["rwkv_v_down_2"][0].rearrange("(c p) n -> p c n", p=P))
            self.load_work(vu[0:32, :], A["rwkv_v_up_2"][0])
            self.work_landed()
            for c in range(4):
                ins = nc.tensor.matmul(self.ps[2][0:32, 0:S], vd[:, c, :], v[:, c, :], start=(c == 0), stop=(c == 3))
            act.wait(pe.did(ins))
            pe.wait(act.did(nc.scalar.activation(low_v[0:32, :], self.ps[2][0:32, 0:S], ACT.Copy)))
            for c in range(4):
                pe.wait(act.now())
                act.wait(pe.did(nc.tensor.matmul(self.ps[3][:, 0:S], vu[0:32, c * P:(c + 1) * P], low_v[0:32, :], start=True, stop=True)))
                act.wait(dve.now())
                dve.wait(act.did(nc.scalar.activation(mix, self.ps[3][:, 0:S], ACT.Sigmoid, bias=col(q_["v0"], c))))
                vf = self.v_first[:, c * S:(c + 1) * S]
                dve.seq(nc.vector.tensor_tensor(vf, vf, v[:, c, :], ALU.subtract))
                dve.seq(nc.vector.tensor_tensor(vf, vf, mix, ALU.mult))
                dve.seq(nc.vector.tensor_tensor(v[:, c, :], v[:, c, :], vf, ALU.add))
        else:
            dve.seq(nc.vector.tensor_copy(self.v_first, v.rearrange("p c s -> p (c s)")))
        pe.wait(act.now())
        for c in range(4):
            b = self.ps[4 + c]
            b2 = self.ps[c]
            nc.tensor.matmul(b[:, 0:S], lora[0:64, c * P:(c + 1) * P], wa[0:64, :], start=True, stop=True)
            act.wait(pe.did(nc.tensor.matmul(b2[:, 0:S], lora[64:128, c * P:(c + 1) * P], wa[64:128, :], start=True, stop=True)))
            act.did(nc.scalar.activation(lw[:, c, :], b[:, 0:S], ACT.Sigmoid, bias=col(q_["rwkv_w0_2"], c)))
            act.did(nc.scalar.activation(a[:, c, :], b2[:, 0:S], ACT.Sigmoid, bias=col(q_["rwkv_a0_2"], c)))
            dve.did(nc.vector.tensor_scalar(kk[:, c, :], k[:, c, :], col(q_["rwkv_k_k_2"], c), None, ALU.mult))
        pe.wait(act.now())
        for t in range(T):
            act.wait(pe.did(nc.tensor.matmul(self.ps[t][:, :], gd[:, t * P:(t + 1) * P], g_up, start=True, stop=True)))
            act.did(nc.scalar.activation(gt[:, t, :], self.ps[t][:, :], ACT.Copy))
        self.meet()
        f3 = lambda x: x.rearrange("p c s -> p (c s)")
        dve.did(nc.vector.tensor_scalar(lw, lw, -DECAY_SCALE, None, ALU.mult))
        sq = self.take(4 * S)
        act.seq(nc.scalar.activation(sq, f3(kk), ACT.Square))
        pe.wait(act.now())
        for g in range(2):
            m = pe.did(nc.tensor.matmul(self.ps[2 + g][:, :], self.c("pair_ones"), sq[:, g * 512:(g + 1) * 512], start=True, stop=True))
            act.wait(m)
        for g in range(2):
            act.did(nc.scalar.activation(sq[:, g * 512:(g + 1) * 512], self.ps[2 + g][:, :], ACT.Sqrt))
        dve.wait(act.now())
        dve.seq(nc.vector.tensor_scalar(sq, sq, 1e-12, None, ALU.max))
        dve.seq(nc.vector.reciprocal(sq, sq))
        dve.seq(nc.vector.tensor_tensor(f3(kk), f3(kk), sq, ALU.mult))
        for c in range(4):
            dve.did(nc.vector.tensor_scalar(sq[:, c * S:(c + 1) * S], a[:, c, :], 1.0, col(q_["rwkv_k_a_2"], c), ALU.subtract, ALU.mult))
        dve.wait(dve.now())
        dve.seq(nc.vector.scalar_tensor_tensor(f3(k), sq, 1.0, f3(k), ALU.add, ALU.mult))
        dve.seq(nc.vector.tensor_tensor(sq, f3(r), f3(k), ALU.mult))
        for c in range(4):
            dve.did(nc.vector.tensor_scalar(sq[:, c * S:(c + 1) * S], sq[:, c * S:(c + 1) * S], col(q_["rwkv_r_k_2"], c), None, ALU.mult))
        bonus = self.take(T * H2).rearrange("p (t h) -> p t h", t=T)
        pe.wait(dve.now())
        for t in range(T):
            for c in range(4):
                ins = nc.tensor.matmul(self.ps[2][:, t * H2 + 2 * c:t * H2 + 2 * c + 2], sq[:, c * S + t * P:c * S + (t + 1) * P],
                                       self.c("pair_pick"), start=True, stop=True)
        dve.wait(pe.did(ins))
        dve.seq(nc.vector.tensor_copy(bonus, self.ps[2][:, 0:T * H2].rearrange("p (t h) -> p t h", t=T)))
        dve.seq(nc.vector.tensor_tensor(f3(a), f3(a), f3(kk), ALU.mult))
        self.cumulate(f3(L), f3(lw), P)
        L4 = f3(L).rearrange("p (n s) -> p n s", s=P)
        ends = self.rowstat[:, 32:64].rearrange("p (k n) -> p k n", k=4)
        dve.did(nc.vector.tensor_copy(ends[:, 0, :].unsqueeze(2), L4[:, :, P // 2 - 1:P // 2]))
        dve.seq(nc.vector.tensor_copy(ends[:, 1, :].unsqueeze(2), L4[:, :, P - 1:P]))
        dve.seq(nc.vector.tensor_tensor(L4, L4, ends[:, 0, :].unsqueeze(2).broadcast_to([P, 8, P]), ALU.subtract))
        mid = ends[:, 0, :].rearrange("p (c t) -> p c t", t=T)
        end = ends[:, 1, :].rearrange("p (c t) -> p c t", t=T)
        fac = ends[:, 2, 0:4].unsqueeze(2)
        dve.seq(nc.vector.tensor_tensor(fac, end[:, :, 0:1], mid[:, :, 0:1], ALU.subtract))
        dve.seq(nc.vector.tensor_tensor(fac, fac, mid[:, :, 1:2], ALU.add))
        act.wait(dve.now())
        act.seq(nc.scalar.activation(ends[:, 2, 0:4], ends[:, 2, 0:4], ACT.Exp))
        self.meet()
        for t in range(T):
            for c in range(4):
                ins = nc.tensor.transpose(self.ps[2 + t][:, c * P:(c + 1) * P], v[:, c, t * P:(t + 1) * P], self.c("ident"))
            act.wait(pe.did(ins))
            act.did(nc.scalar.activation(vt[:, t, :], self.ps[2 + t][:, :], ACT.Copy))
        self.meet()
        self.work_at -= T * H2 + 4 * S
        bonus2 = self.take(T * H2).rearrange("p (t h) -> p t h", t=T)
        dve.seq(nc.vector.tensor_copy(bonus2, bonus))
        eP, eN = self.take(S), self.take(S)
        kr = self.take(2 * S).rearrange("p (t k s) -> p t k s", t=T, k=2)
        bt, kt = self.take(S), self.take(S)
        units = [(e, t) for t in range(T) for e in range(2)]
        M4 = [self.hT[:, 2 * n:2 * n + 2, :].rearrange("p c s -> p (c s)") for n in range(4)]
        TT = [self.take(2 * P) for _ in units]
        AmT = self.take(4 * P)
        Y = [self.take(P) for _ in units]
        RU = [self.take(2 * HD2) for _ in units]
        bk = self.take(2 * P)
        S1 = self.take(HD2)
        vs = self.take(T * P).rearrange("p (t n) -> p t n", t=T)
        with self.loop(4, ("pe", "act", "dve", "pool"), **self.per["rwkv"]) as j:
            self.meet()
            Lj = self.pair(L, j)
            act.did(nc.scalar.activation(eP, Lj, ACT.Exp))
            act.did(nc.scalar.activation(eN, Lj, ACT.Exp, scale=-1.0))
            act.did(nc.scalar.activation(vs, vt[:, :, ds(j * P, P)], ACT.Copy))
            tmp = AmT[:, 0:S]
            dve.seq(nc.vector.tensor_tensor(tmp, Lj, self.pair(lw, j), ALU.subtract))
            act.wait(dve.now())
            act.seq(nc.scalar.activation(tmp, tmp, ACT.Exp))
            dve.wait(act.now())
            t3 = lambda x: x.rearrange("p (t s) -> p t s", t=T)
            dve.did(nc.vector.tensor_tensor(kr[:, :, 0, :], t3(tmp), t3(self.pair(kk, j)), ALU.mult))
            dve.did(nc.vector.tensor_tensor(kr[:, :, 1, :], t3(eP), t3(self.pair(r, j)), ALU.mult))
            dve.did(nc.vector.tensor_tensor(bt, eN, self.pair(a, j), ALU.mult))
            dve.did(nc.vector.tensor_tensor(kt, eN, self.pair(k, j), ALU.mult))
            pe.wait(dve.now(), act.now())
            dve.wait(dve.now())
            for n, (e, t) in enumerate(units):
                h, tok = slice(e * HD2, (e + 1) * HD2), slice(t * P, (t + 1) * P)
                b = self.ps[4 + n]
                rhs = kr[h, t, :, :].rearrange("p k s -> p (k s)")
                nc.tensor.matmul(b[:, 0:S], bt[h, tok], rhs, start=True, stop=True)
                m = pe.did(nc.tensor.matmul(b[:, S:2 * S], kt[h, tok], rhs, start=True, stop=True))
                m2 = pe.did(nc.tensor.matmul(self.ps[n][:, 0:P], kr[h, t, 0, :], bt[h, tok], start=True, stop=True))
                dve.wait(m)
                v4 = lambda x: x.rearrange("p (g k s) -> p g k s", g=2, k=2)
                dve.did(nc.vector.tensor_tensor(v4(M4[n])[:, :, 0, :], v4(b[:, :])[:, :, 0, :],
                                                self.c("before_T").unsqueeze(1).broadcast_to([P, 2, P]), ALU.mult))
                dve.did(nc.vector.tensor_tensor(v4(M4[n])[:, :, 1, :], v4(b[:, :])[:, :, 1, :],
                                                self.c("upto_T").unsqueeze(1).broadcast_to([P, 2, P]), ALU.mult))
                dve.wait(m2)
                dve.did(nc.vector.tensor_tensor(TT[n][:, 0:P], self.ps[n][:, 0:P], low, ALU.mult))
                dve.wait(dve.now())
                dve.did(nc.vector.tensor_tensor(TT[n][:, P:2 * P], M4[n][:, 0:P], masks_T[:, 0:P], ALU.mult))
                dve.wait(dve.now())
                dve.did(nc.vector.tensor_tensor(TT[n][:, :].rearrange("p (k s) -> p k s", k=2),
                                                self.c("ident").unsqueeze(1).broadcast_to([P, 2, P]),
                                                TT[n][:, :].rearrange("p (k s) -> p k s", k=2), ALU.subtract))
            pe.wait(dve.now())
            nc.tensor.transpose(self.ps[0][:, P:2 * P], bt[:, 0:P], self.c("ident"))
            m = pe.did(nc.tensor.transpose(self.ps[0][:, 2 * P:3 * P], kt[:, 0:P], self.c("ident")))
            dve.wait(m)
            dve.did(nc.vector.tensor_copy(bk, self.ps[0][:, P:3 * P]))
            dve.wait(dve.now())
            for lev in range(1, LEVELS):
                marks, ys = [], []
                for n in range(4):
                    am = AmT[:, n * P:(n + 1) * P]
                    if lev > 1:
                        dve.wait(am_read[n])
                    marks.append(dve.did(nc.vector.tensor_tensor(am, M4[n][:, 0:P], masks_T[:, lev * P:(lev + 1) * P], ALU.mult)))
                am_read = []
                for n in range(4):
                    pe.wait(marks[n])
                    am_read.append(pe.did(nc.tensor.matmul(self.ps[n][:, 0:P], AmT[:, n * P:(n + 1) * P], TT[n][:, 0:P], start=True, stop=True)))
                    act.wait(am_read[n])
                    ys.append(act.did(nc.scalar.activation(Y[n], self.ps[n][:, 0:P], ACT.Copy)))
                last = lev == LEVELS - 1
                for n in range(4):
                    b = self.ps[4 + n]
                    pe.wait(ys[n])
                    if not last:
                        nc.tensor.matmul(b[:, 0:P], TT[n][:, P:2 * P], Y[n], start=True, stop=True)
                    dve.wait(pe.did(nc.tensor.matmul(b[:, P:2 * P], Y[n], TT[n][:, P:2 * P], start=True, stop=True)))
                    lo = P if last else 0
                    dve.did(nc.vector.tensor_tensor(TT[n][:, lo:2 * P], TT[n][:, lo:2 * P], b[:, lo:2 * P], ALU.subtract))
                    pe.wait(dve.now())
                dve.wait(dve.now())
            for n, (e, t) in enumerate(units):
                h = slice(e * HD2, (e + 1) * HD2)
                vj = vs[:, t, e * HD2:(e + 1) * HD2]
                b = self.ps[n]
                nc.tensor.matmul(b[:, 0:HD2], M4[n][:, S:S + P], vj, start=True, stop=(t == 0))
                if t:
                    nc.tensor.matmul(b[:, 0:HD2], kr[h, 1, 0, :], S1[h, :], start=False, stop=True)
                dve.wait(pe.did(nc.tensor.matmul(self.ps[4 + n][:, 0:HD2], M4[n][:, S + P:2 * S], vj, start=True, stop=False)))
                pe.wait(dve.did(nc.vector.tensor_scalar(RU[n][:, 0:HD2], b[:, 0:HD2], -1.0, None, ALU.mult)))
                dve.wait(pe.did(nc.tensor.matmul(b[:, HD2:2 * HD2], TT[n][:, P:2 * P], RU[n][:, 0:HD2], start=True, stop=True)))
                pe.wait(dve.did(nc.vector.tensor_copy(RU[n][:, HD2:2 * HD2], b[:, HD2:2 * HD2])))
                U = RU[n][:, HD2:2 * HD2]
                y = self.ps[4 + n][:, 0:HD2]
                if t:
                    nc.tensor.matmul(y, kr[h, 1, 1, :], S1[h, :], start=False, stop=False)
                act.wait(pe.did(nc.tensor.matmul(y, M4[n][:, P:2 * P], U, start=False, stop=True)))
                act.did(nc.scalar.activation(self.mixed[:, t, ds(j * 2 * HD2 + (3 * GW + e * HD2), HD2)], y, ACT.Copy))
                if t == 0:
                    s_ = b[h, 2 * HD2:3 * HD2]
                    nc.tensor.matmul(s_, bk[:, e * HD2:(e + 1) * HD2], U, start=True, stop=False)
                    dve.wait(pe.did(nc.tensor.matmul(s_, bk[:, P + e * HD2:P + (e + 1) * HD2], vj, start=False, stop=True)))
                    pe.wait(dve.did(nc.vector.tensor_scalar(S1[h, :], s_, ends[h, 2, ds(j, 1)], None, ALU.mult)))
        self.meet()
        row_w, row_b = M4[0], M4[1]
        self.work_ld.count(nc.scalar.dma_start(row_w, A["rwkv_ln_w_2"][l].partition_broadcast(P)))
        self.work_ld.count(nc.scalar.dma_start(row_b, A["rwkv_ln_b_2"][l].partition_broadcast(P)))
        self.work_landed()
        tmp = M4[2].rearrange("p (n d) -> p n d", d=HD2)
        st = self.rowstat[:, 4:4 + H2]
        over = lambda x: x.unsqueeze(2).broadcast_to([P, H2, HD2])
        for t in range(T):
            y2 = self.mixed[:, t, 3 * GW:4 * GW]
            y = y2.rearrange("p (n d) -> p n d", d=HD2)
            v8 = vt[:, t, :].rearrange("p (n d) -> p n d", d=HD2)
            dve.seq(nc.vector.tensor_reduce(st, y, AX.X, ALU.add))
            dve.seq(nc.vector.tensor_scalar(st, st, 1.0 / HD2, None, ALU.mult))
            dve.seq(nc.vector.tensor_tensor(y, y, over(st), ALU.subtract))
            dve.seq(nc.vector.tensor_tensor(tmp, y, y, ALU.mult))
            dve.seq(nc.vector.tensor_reduce(st, tmp, AX.X, ALU.add))
            self.inv_rms(st, H2, HD2, LN_EPS)
            dve.seq(nc.vector.tensor_tensor(y, y, over(st), ALU.mult))
            dve.seq(nc.vector.tensor_tensor(y2, y2, row_w, ALU.mult))
            dve.seq(nc.vector.tensor_tensor(y2, y2, row_b, ALU.add))
            dve.seq(nc.vector.tensor_tensor(tmp, v8, over(bonus2[:, t, :]), ALU.mult))
            dve.seq(nc.vector.tensor_tensor(y, y, tmp, ALU.add))
            dve.seq(nc.vector.tensor_tensor(y2, y2, gt[:, t, :], ALU.mult))
        self.meet()

    def finish(self):
        nc = self.nc
        for q in (self.pe, self.act, self.dve, self.pool):
            nc.sync.wait_ge(*q.now())
        for t in range(T):
            self.outs.count(nc.sync.dma_start(self.out_dram[0, t * P:(t + 1) * P, :], self.x[:, t, :]))
        nc.sync.wait_ge(*self.outs.now())


def build(nc, A, consts, out):
    Program(nc, A, consts, out).build()


_INS = ['x', 'mem', 'norm_gain', 'mem_norm_gain', 'mem_w_kv', 'mem_qk_gain', 'w_out', 'even_w_in', 'nsa_qk_gain',
        'nsa_cmp_pos', 'nsa_cmp_w1', 'nsa_cmp_w2', 'diff_qk_gain', 'diff_lambda', 'diff_subln_gain', 'odd_w_in',
        'dsa_qk_gain', 'w_in_2', 'w_out_2', 'norm_pre_mix_2', 'norm_post_mix_2', 'norm_pre_ffn_2', 'norm_post_ffn_2',
        'w_ffn_gate_2', 'w_ffn_up_2', 'w_ffn_down_2', 'hgrn_lb_logits_2', 'hgrn_norm_w_2', 'mlstm_conv_w_2',
        'mlstm_conv_b_2', 'mlstm_i_bias_2', 'mlstm_f_bias_2', 'mlstm_norm_w_2', 'rwkv_mu_2', 'rwkv_w0_2',
        'rwkv_w_up_2', 'rwkv_a0_2', 'rwkv_a_up_2', 'rwkv_g_up_2', 'rwkv_k_k_2', 'rwkv_k_a_2', 'rwkv_r_k_2',
        'rwkv_ln_w_2', 'rwkv_ln_b_2', 'rwkv_v0_2', 'rwkv_v_down_2', 'rwkv_v_up_2']


def kernel(**inputs):
    import numpy as _np
    import concourse.bacc as _bacc
    from concourse import mybir as _mybir
    from concourse.bass_utils import run_bass_kernel_spmd as _run

    nc = _bacc.Bacc("TRN2", target_bir_lowering=False, num_devices=1)
    small, offs, halves_T, halves, decay = shape_constants()
    arrays, A = {}, {}
    tables = dict(const_small=small, const_halves_T=halves_T, const_halves=halves, const_decay=decay)
    for name, a in [(n, inputs[n]) for n in _INS] + list(tables.items()):
        a = _np.ascontiguousarray(a)
        arrays[f"in_{name}_dram"] = a
        A[name] = nc.dram_tensor(f"in_{name}_dram", a.shape, _mybir.dt.from_np(a.dtype), kind="ExternalInput").ap()
    out = nc.dram_tensor("out_0_dram", (1, S, D), _mybir.dt.float32, kind="ExternalOutput").ap()
    build(nc, A, dict(small=small, offs=offs), out)
    r = _run(nc, [arrays], core_ids=[0])
    return r.results[0]["out_0_dram"]
```

```python
import concourse.bass as bass
from concourse import mybir
from contextlib import ExitStack, contextmanager
import math
import numpy as np

F32 = mybir.dt.float32
F32R = mybir.dt.float32r
ALU = mybir.AluOpType
ACT = mybir.ActivationFunctionType
AX = mybir.AxisListType
ds = bass.ds

P = 128
S = 256
T = S // P
D = 2048
KC = D // P
TILE = 512
UNIT = 2
SLOTS = 4
EPS = 1e-6
BIG = 1e30

EVEN = dict(a_q=0, a_kv=1024, a_g=2560, a_z=2584, b_q=3608, b_k=4120, b_v=4632, b_z=5144, m_q=5656, m_z=6168)
EVEN_IN = 6680
ODD = dict(c_q=0, c_k=1536, c_v=2048, i_q=2560, i_k=3584, i_w=3648, c_z=3664, m_q=5200, m_z=5712)
ODD_IN = 6224
HD = 128
CMP_LEN, CMP_STRIDE, CMP_HID = 32, 16, 256
NCMP = (S - CMP_LEN) // CMP_STRIDE + 1
TOPK = S // 4
LAMBDA_INIT = 0.8 - 0.6 * math.exp(0.0)

GW, H2, HD2 = 512, 8, 64
N_IN = 7952
D_FF = 5632
LEVELS = 7
DECAY_SCALE = 0.6065306597126334
LN_EPS = 64e-5
WORK = 6650
FIXED = 1128
SPARE = 2 * KC * S


def shape_constants():
    t = np.arange(S)
    p = np.arange(P)
    parts = {}

    def put(name, a):
        full = np.zeros((P, a.shape[1]), np.float32)
        full[:a.shape[0]] = a
        parts[name] = full

    def rope_tables(pos, half):
        inv = (np.float32(10000.0) ** (-np.arange(half, dtype=np.float32) / np.float32(half))).astype(np.float32)
        ang = pos.astype(np.float32)[:, None] * inv[None, :]
        return np.cos(ang).astype(np.float32), np.sin(ang).astype(np.float32)

    def by_tile(a):
        return a.reshape(T, P, -1).transpose(1, 0, 2).reshape(P, -1)

    put("ident", np.eye(P, dtype=np.float32))
    future = (p[None, :] > p[:, None]).astype(np.float32)
    put("causal", np.concatenate([np.zeros((P, P)), future * BIG], 1))
    put("zeros", np.zeros((P, S)))
    put("ones", np.ones((P, P)))
    put("pair_ones", np.kron(np.eye(2), np.ones((HD2, HD2))))
    put("pair_pick", np.kron(np.eye(2), np.ones((HD2, 1))))
    for d in (HD, HD2):
        c, s = rope_tables(t, d // 2)
        put(f"cos{d}", by_tile(c))
        put(f"sin{d}", by_tile(s))
    last = np.arange(NCMP) * CMP_STRIDE + CMP_LEN - 1
    c, s = rope_tables(np.tile(last, 2), HD // 2)
    put("cos_cmp", c)
    put("sin_cmp", s)
    for g in range(2):
        for tt in range(T):
            ok = np.zeros((P, 2 * NCMP), np.float32)
            ok[:, g * NCMP:(g + 1) * NCMP] = last[None, :] <= (tt * P + p)[:, None]
            put(f"cmp_keep{g}{tt}", ok)
            put(f"cmp_drop{g}{tt}", (1 - ok) * BIG)
    put("upto_T", (p[:, None] <= p[None, :]).astype(np.float32))
    put("before_T", (p[:, None] < p[None, :]).astype(np.float32))
    offs, at = {}, 0
    for n, a in parts.items():
        offs[n] = (at, a.shape[1])
        at += a.shape[1]
    small = np.concatenate(list(parts.values()), 1).astype(np.float32)

    half = [((p[:, None] // (2 * b) == p[None, :] // (2 * b)) & (p[:, None] % (2 * b) < b) & (p[None, :] % (2 * b) >= b))
            .astype(np.float32) for b in (1 << np.arange(LEVELS))]
    halves_T = np.concatenate(half, 1)
    halves = np.concatenate([h.T for h in half], 1)
    lg = np.log1p(-np.exp2(-5.0 - np.arange(H2)))
    rel = p[None, :] - p[:, None]
    dec = [[np.exp(lg[h] * np.maximum(rel + off, 0)) * (rel + off >= 0) * HD2 ** -0.5 for off in (0, P)] for h in range(H2)]
    decay = np.concatenate([np.concatenate(d2, 1) for d2 in dec], 1).astype(np.float32)
    return small, offs, halves_T.astype(np.float32), halves.astype(np.float32), decay


class Counter:

    def __init__(self, sem, step=1):
        self.sem, self.step, self.base, self.k = sem, step, 0, 0

    def count(self, ins):
        ins.then_inc(self.sem, self.step)
        self.k += 1
        return self.now()

    def now(self, back=0):
        return (self.sem, self.base + (self.k - back) * self.step)


class Queue(Counter):

    def __init__(self, eng, sem):
        super().__init__(sem)
        self.eng = eng

    def wait(self, *marks):
        for sem, value in marks:
            self.eng.wait_ge(sem, value)

    def did(self, ins):
        return self.count(ins)

    def hold(self, passed):
        self.eng.sem_inc(passed, 1)

    def seq(self, ins):
        m = self.count(ins)
        self.wait(m)
        return m


class Program:
    def __init__(self, nc, A, consts, out):
        self.nc, self.A, self.C, self.out_dram = nc, A, consts, out

    def build(self):
        nc = self.nc
        with ExitStack() as ctx:
            def sem(name):
                return ctx.enter_context(nc.semaphore(name))

            at = [(nc.sbuf_base + 31) // 32 * 32]

            def sb(name, shape, dtype=F32, offset=None):
                if offset is None:
                    offset = at[0]
                    at[0] += (int(np.prod(shape[1:])) * 4 + 31) // 32 * 32
                return nc.alloc_sbuf_tensor_at(name, shape, dtype, offset=offset)

            self.pe = Queue(nc.tensor, sem("pe_done"))
            self.act = Queue(nc.scalar, sem("act_done"))
            self.dve = Queue(nc.vector, sem("dve_done"))
            self.pool = Queue(nc.gpsimd, sem("pool_done"))
            self.full = [Counter(sem(f"slot_full{i}"), 16) for i in range(SLOTS)]
            self.ready = [Counter(sem(f"unit_split{i}")) for i in range(SLOTS)]
            self.used = [Counter(sem(f"unit_used{i}")) for i in range(SLOTS)]
            self.emptied = [Counter(sem(f"bank_emptied{b}")) for b in range(8)]
            self.open = []
            self.small = Counter(sem("small_loads"), 16)
            self.work_ld = Counter(sem("work_loads"), 16)
            self.passed = sem("passed")
            self.outs = Counter(sem("out_stores"), 16)
            self.counters = dict(pe=self.pe, act=self.act, dve=self.dve, pool=self.pool)
            for i in range(SLOTS):
                self.counters[f"full{i}"] = self.full[i]
                self.counters[f"ready{i}"] = self.ready[i]
                self.counters[f"used{i}"] = self.used[i]
            for b in range(8):
                self.counters[f"emptied{b}"] = self.emptied[b]

            self.x = sb("x_residual", [P, T, D])
            mixed_at = at[0]
            self.mixed = sb("mixed", [P, T, D])
            spare_at = at[0]
            self.hT = (sb("h_high", [P, KC, S], F32R), sb("h_low", [P, KC, S], F32R))
            self.raw = [sb(f"weights{i}", [P, UNIT, TILE]) for i in range(SLOTS)]
            self.w_high = [sb(f"weights_high{i}", [P, UNIT, TILE], F32R) for i in range(SLOTS)]
            self.w_low = [sb(f"weights_low{i}", [P, UNIT, TILE], F32R) for i in range(SLOTS)]
            self.const = sb("const", [P, self.C["small"].shape[1]])
            self.params = sb("params", [P, 2250])
            self.params_at = 0
            self.fixed = sb("fixed", [P, FIXED])
            self.fixed_at = 0
            proj_at = at[0]
            self.proj = sb("proj", [P, 16384])
            self.work = sb("work", [P, WORK])
            self.spare = sb("spare", [P, SPARE], offset=spare_at)
            ff = D_FF // P
            self.actT = (sb("act_high", [P, ff, S], F32R, offset=proj_at),
                         sb("act_low", [P, ff, S], F32R, offset=proj_at + ff * S * 4))
            assert proj_at + 2 * ff * S * 4 <= at[0] <= nc.sbuf_usable_end
            self.ff_small = sb("ff_small", [P, T * D], offset=mixed_at)
            self.work_at = self.spare_at = self.work_fixed = 0
            self.ps = [ctx.enter_context(nc.psum_tensor(f"bank{b}", [P, 512], F32)) for b in range(8)]

            for c in self.ready + self.used + self.emptied:
                nc.sync.sem_inc(c.sem, 1)
                c.base = 1
            self.load_params()
            self.main()
            self.finish()

    def c(self, name):
        at, w = self.C["offs"][name]
        return self.const[:, at:at + w]

    def take(self, cols):
        if self.work_at + cols <= WORK:
            self.work_at += cols
            return self.work[:, self.work_at - cols:self.work_at]
        return self.take_spare(cols)

    def take_spare(self, cols):
        self.spare_at += cols
        assert self.spare_at <= SPARE, self.spare_at
        return self.spare[:, self.spare_at - cols:self.spare_at]

    @contextmanager
    def loop(self, n, engines, **per):
        nc = self.nc
        kinds = dict(pe=mybir.EngineType.PE, act=mybir.EngineType.Activation, dve=mybir.EngineType.DVE,
                     pool=mybir.EngineType.Pool, sp=mybir.EngineType.SP)
        old = {k: (c.base, c.k) for k, c in self.counters.items()}
        with nc.Fori(0, n, engines=[kinds[e] for e in engines]) as i:
            for k, c in self.counters.items():
                if per.get(k):
                    c.base, c.k = c.base + c.k * c.step + i * (per[k] * c.step), 0
                else:
                    c.base, c.k = c.base + c.k * c.step, 0
            yield i
            made = {k: c.k for k, c in self.counters.items() if c.k}
            assert made == {k: v for k, v in per.items() if v}, f"a turn makes {made}"
        for k, c in self.counters.items():
            c.base, c.k = old[k][0], old[k][1] + n * per.get(k, 0)

    def meet(self, names=("pe", "act", "dve", "pool")):
        qs = [self.counters[n] for n in names]
        marks = [q.now() for q in qs] + self.open
        self.open = []
        for q in qs:
            q.wait(*marks)

    def param(self, dram_row, width):
        dst = self.params[:, self.params_at:self.params_at + width]
        self.params_at += width
        self.small.count(self.nc.scalar.dma_start(dst, dram_row.partition_broadcast(P)))
        return dst

    def param_cols(self, dram_vec, chunks):
        dst = self.params[:, self.params_at:self.params_at + chunks]
        self.params_at += chunks
        with self.nc.allow_non_contiguous_dma(reason="a few thousand parameters"):
            self.small.count(self.nc.scalar.dma_start(dst, dram_vec.rearrange("(c p) -> p c", p=P)))
        return dst

    def split_unit(self, st, u):
        nc, act, dve = self.nc, self.act, self.dve
        i, w = u % SLOTS, st["width"]
        raw, high, low = [a[i][:, :, 0:w] for a in (self.raw, self.w_high, self.w_low)]
        nc.sync.wait_ge(*self.ready[i].now())
        nc.sync.sem_inc(self.passed, 1)
        self.full[i].count(nc.sync.dma_start(raw, st["W"][u, :, :, ds(st["col"], w)]))
        act.wait(self.full[i].now(), self.used[i].now())
        dve.wait(act.did(nc.scalar.activation(high, raw, ACT.Copy)))
        self.ready[i].count(nc.vector.tensor_tensor(low, raw, high.bitcast(F32), ALU.subtract))

    def run_step(self, st, after=None):
        nc, pe, act = self.nc, self.pe, self.act
        AT, w, units, banks = st["AT"], st["width"], st["units"], st["banks"]
        marks = []
        for u in range(units):
            i = u % SLOTS
            if u:
                self.split_unit(st, u)
            pe.wait(self.ready[i].now())
            for n, b in enumerate(banks):
                if u == 0:
                    pe.wait(self.emptied[b].now())
                for c in range(UNIT):
                    k = u * UNIT + c
                    for x, y in ((0, 0), (1, 0), (0, 1)):
                        wt = (self.w_high, self.w_low)[y][i]
                        if st["kind"] == "tokens":
                            out, l, r = self.ps[b][:, 0:w], AT[x][:, k, n * P:(n + 1) * P], wt[:, c, 0:w]
                        else:
                            out, l, r = self.ps[b][:, 0:S], wt[:, c, n * P:(n + 1) * P], AT[x][:, k, :]
                        ins = nc.tensor.matmul(out, l, r, start=(k == 0 and x + y == 0),
                                               stop=(k == units * UNIT - 1 and y == 1))
                if u == units - 1 and n < len(banks) - 1:
                    marks.append(pe.did(ins))
            released = self.used[i].count(ins)
        marks.append(released)
        if after is not None:
            self.split_unit(after, 0)
        for n, b in enumerate(banks):
            st["evac"](n, b, marks[n])

    def copy_out(self, dst):
        def evac(n, b, mark):
            d = dst(n)
            w = d.shape[-1]
            self.act.wait(mark)
            self.emptied[b].count(self.nc.scalar.activation(d, self.ps[b][:, 0:w], ACT.Copy))
        return evac

    def tokens(self, AT, Wu, units, col, width, dst):
        return dict(kind="tokens", AT=AT, W=Wu, units=units, col=col, width=width, banks=range(T), evac=self.copy_out(dst))

    def features(self, AT, Wu, units, col, chunks, dst, bank0=0, evac=None):
        return dict(kind="features", AT=AT, W=Wu, units=units, col=col, width=chunks * P,
                    banks=range(bank0, bank0 + chunks), evac=evac or self.copy_out(dst))

    def units_of(self, W):
        return W.rearrange("(u c p) n -> u p c n", c=UNIT, p=P)

    def run_steps(self, make, n, rest=(), **more):
        first = make(0) if n else rest
        self.split_unit(first[0], 0)
        tail = list(rest)
        if n > 1:
            per = {k: v for k, v in more.items()}
            for s in first:
                for u in range(s["units"]):
                    for k in ("full", "ready", "used"):
                        per[f"{k}{u % SLOTS}"] = per.get(f"{k}{u % SLOTS}", 0) + 1
                per["act"] = per.get("act", 0) + s["units"]
                per["pe"] = per.get("pe", 0) + len(s["banks"]) - 1
                for b in s["banks"]:
                    per[f"emptied{b}"] = per.get(f"emptied{b}", 0) + 1
            with self.loop(n - 1, ("pe", "act", "dve", "sp"), **per) as i:
                steps = make(i)
                for s, after in zip(steps, steps[1:] + [make(i + 1)[0]]):
                    self.run_step(s, after)
        if n:
            tail = make(n - 1) + tail
        for s, after in zip(tail, tail[1:] + [None]):
            self.run_step(s, after)
        self.open += [self.emptied[b].now() for b in range(8)]

    def project_tokens(self, AT, W, rows, col0, n, dst):
        units, Wu = rows // (UNIT * P), self.units_of(W)
        whole, rest = n // TILE, n % TILE
        last = [self.tokens(AT, Wu, units, col0 + whole * TILE, rest, lambda t: dst[:, t, whole * TILE:n])] if rest else []
        self.run_steps(lambda i: [self.tokens(AT, Wu, units, col0 + i * TILE, TILE, lambda t: dst[:, t, ds(i * TILE, TILE)])],
                       whole, last)
        return [self.emptied[t].now() for t in range(T)]

    def transpose_split(self, src, gain=None):
        nc, pe, act, dve = self.nc, self.pe, self.act, self.dve
        ident = self.c("ident")
        high, low = self.hT
        free = {}
        for k, c in enumerate(range(0, KC, 2)):
            b = 2 + k % 4
            if b in free:
                pe.wait(free[b])
            for j in range(2):
                for t in range(T):
                    ins = nc.tensor.transpose(self.ps[b][:, (j * T + t) * P:(j * T + t + 1) * P],
                                              src[:, t, (c + j) * P:(c + j + 1) * P], ident)
            act.wait(pe.did(ins))
            if gain is None:
                o, v = [a[:, c:c + 2, :] for a in (high, low)], self.ps[b][:, :].rearrange("p (c s) -> p c s", c=2)
                dve.wait(act.did(nc.scalar.activation(o[0], v, ACT.Copy)))
                free[b] = dve.did(nc.vector.tensor_tensor(o[1], v, o[0].bitcast(F32), ALU.subtract))
                continue
            for j in range(2):
                m = act.did(nc.scalar.activation(high[:, c + j, :], self.ps[b][:, j * S:(j + 1) * S], ACT.Copy,
                                                 scale=gain[:, c + j:c + j + 1]))
            dve.wait(m)
            for j in range(2):
                free[b] = dve.did(nc.vector.scalar_tensor_tensor(
                    low[:, c + j, :], self.ps[b][:, j * S:(j + 1) * S], gain[:, c + j:c + j + 1],
                    high[:, c + j, :].bitcast(F32), ALU.mult, ALU.subtract))

    def transpose_tokens(self, src, dst, gain=None):
        nc, pe, act, dve = self.nc, self.pe, self.act, self.dve
        n = src.shape[2] // P
        free = {}
        ident = self.c("ident")
        done = []
        for k, c in enumerate(range(0, n, 2)):
            b = 2 + k % 4
            cc = min(2, n - c)
            if b in free:
                pe.wait(free[b])
            for j in range(cc):
                for t in range(T):
                    ins = nc.tensor.transpose(self.ps[b][:, (j * T + t) * P:(j * T + t + 1) * P],
                                              src[:, t, (c + j) * P:(c + j + 1) * P], ident)
            m = pe.did(ins)
            q = act if k % 2 else dve
            q.wait(m)
            if gain is None:
                o, i_ = dst[:, c:c + cc, :], self.ps[b][:, 0:cc * S].rearrange("p (c s) -> p c s", c=cc)
                ins = nc.scalar.activation(o, i_, ACT.Copy) if q is act else nc.vector.tensor_copy(o, i_)
                free[b] = q.did(ins)
            else:
                for j in range(cc):
                    o, i_, g = dst[:, c + j, :], self.ps[b][:, j * S:(j + 1) * S], gain[:, c + j:c + j + 1]
                    ins = (nc.scalar.activation(o, i_, ACT.Copy, scale=g) if q is act
                           else nc.vector.tensor_scalar(o, i_, g, None, ALU.mult))
                    free[b] = q.did(ins)
            done.append(free[b])
        return done

    def inv_rms(self, ss, width, n, eps=EPS):
        nc, dve, pool = self.nc, self.dve, self.pool
        m = dve.did(nc.vector.tensor_scalar(ss, ss, 1.0 / n, eps, ALU.mult, ALU.add))
        pool.wait(m)
        mh = self.minus_half.broadcast_to([ss.shape[0], ss.shape[1]]) if False else self.minus_half[0:ss.shape[0], 0:ss.shape[1]]
        m = pool.did(nc.gpsimd.tensor_tensor(ss, ss, mh, ALU.pow))
        dve.wait(m)

    def norm_to_hT(self, src, gain):
        nc, act, dve = self.nc, self.act, self.dve
        ss = self.rowstat[:, 0:T]
        for t in range(T):
            m = act.did(nc.scalar.activation(self.mixed[:, t, :], src[:, t, :], ACT.Square, accum_out=ss[:, t:t + 1]))
        dve.wait(m)
        self.inv_rms(ss, T, D)
        for t in range(T):
            m = dve.did(nc.vector.tensor_scalar(self.mixed[:, t, :], src[:, t, :], ss[:, t:t + 1], None, ALU.mult))
        self.pe.wait(m)
        self.transpose_split(self.mixed, gain)
        self.meet()

    def head_norm(self, src, tmp, heads, d, gain, rows=P):
        nc, dve = self.nc, self.dve
        ss = self.rowstat[0:rows, 4:4 + heads]
        dve.seq(nc.vector.tensor_tensor(tmp, src, src, ALU.mult))
        dve.seq(nc.vector.tensor_reduce(ss, tmp, AX.X, ALU.add))
        self.inv_rms(ss, heads, d)
        dve.seq(nc.vector.tensor_tensor(tmp, src, ss.unsqueeze(2).broadcast_to([rows, heads, d]), ALU.mult))
        if gain is not None:
            dve.seq(nc.vector.tensor_tensor(tmp, tmp, gain[0:rows].unsqueeze(1).broadcast_to([rows, heads, d]), ALU.mult))

    def rope(self, src, dst, heads, d, cos, sin, rows=P):
        nc, dve = self.nc, self.dve
        h = d // 2
        cb = cos.unsqueeze(1).broadcast_to([rows, heads, h])
        sb_ = sin.unsqueeze(1).broadcast_to([rows, heads, h])
        x1, x2, o1, o2 = src[:, :, 0:h], src[:, :, h:d], dst[:, :, 0:h], dst[:, :, h:d]
        tmp = self.rope_tmp[0:rows, 0:heads * h].rearrange("p (n d) -> p n d", n=heads)
        dve.did(nc.vector.tensor_tensor(o1, x1, cb, ALU.mult))
        dve.seq(nc.vector.tensor_tensor(tmp, x2, sb_, ALU.mult))
        dve.did(nc.vector.tensor_tensor(o1, o1, tmp, ALU.subtract))
        dve.seq(nc.vector.tensor_tensor(o2, x2, cb, ALU.mult))
        dve.seq(nc.vector.tensor_tensor(tmp, x1, sb_, ALU.mult))
        return dve.seq(nc.vector.tensor_tensor(o2, o2, tmp, ALU.add))

    def prep(self, view, heads, d, gain, rope, norm=True):
        nc, dve = self.nc, self.dve
        for t in range(T):
            src = view(t)
            tmp = self.prep_tmp[:, 0:heads * d].rearrange("p (n d) -> p n d", n=heads)
            if norm:
                self.head_norm(src, tmp, heads, d, gain)
            else:
                dve.seq(nc.vector.tensor_copy(tmp, src))
            if rope:
                half = d // 2
                m = self.rope(tmp, src, heads, d, self.c(f"cos{d}")[:, t * half:(t + 1) * half],
                              self.c(f"sin{d}")[:, t * half:(t + 1) * half])
            else:
                m = dve.seq(nc.vector.tensor_copy(src, tmp))
        return m

    def attention(self, units):
        nc, pe, act, dve = self.nc, self.pe, self.act, self.dve
        R = 2
        n = len(units)
        st = [dict() for _ in units]

        def scores(i):
            u, s = units[i], st[i]
            s["ps"] = self.ps[2 + i % R][:, 0:u["keys"]]
            if i >= R:
                pe.wait(st[i - R]["masked"])
            s["scored"] = pe.did(nc.tensor.matmul(s["ps"], u["qT"], u["kT"], start=True, stop=True))
            if u.get("mlstm"):
                for c, g in enumerate(u["gates"]):
                    s["scored"] = pe.did(nc.tensor.matmul(self.ps[2 + i % R][:, S + c * P:S + (c + 1) * P],
                                                          g.broadcast_to([P, P]), self.c("ident"), start=True, stop=True))

        def soften(i):
            u, s = units[i], st[i]
            k, j = u["keys"], i % 3
            s["e"] = self.sm_e[:, j * S:j * S + k]
            stat = self.sm_stat[:, 4 * j:4 * j + 4]
            dve.wait(s["scored"])
            if i >= 3:
                dve.wait(st[i - 3]["exp"], st[i - 3]["out"])
            if u.get("mlstm"):
                return soften_mlstm(i, u, s, k, j)
            dve.hold(self.passed)
            s["masked"] = dve.did(nc.vector.tensor_tensor_reduce(
                out=self.sm_s[:, j * S:j * S + k], in0=s["ps"], in1=u["mask"], scale=1.0, scalar=3e38,
                op0=ALU.add, op1=ALU.min, accum_out=stat[:, 0:1]))
            act.wait(s["masked"])
            if i >= 3:
                act.wait(st[i - 3]["flipped"])
            s["exp"] = act.did(nc.scalar.activation(s["e"], self.sm_s[:, j * S:j * S + k], ACT.Exp,
                                                    bias=stat[:, 0:1], scale=-1.0, accum_out=stat[:, 1:2]))
            dve.wait(s["exp"])
            if u.get("keep") is not None:
                dve.hold(self.passed)
                s["exp"] = dve.seq(nc.vector.tensor_tensor_reduce(
                    out=s["e"], in0=s["e"], in1=u["keep"], scale=1.0, scalar=0.0,
                    op0=ALU.mult, op1=ALU.add, accum_out=stat[:, 1:2]))
            dve.seq(nc.vector.tensor_scalar(stat[:, 2:3], stat[:, 1:2], 1e-30, None, ALU.max))
            s["recip"] = dve.did(nc.vector.reciprocal(stat[:, 3:4], stat[:, 2:3]))
            s["r"] = stat[:, 3:4]

        def soften_mlstm(i, u, s, k, j):
            G = self.ps[2 + i % R][:, S:S + k]
            stat = self.sm_stat[:, 8 * j:8 * j + 8]
            M, neg, m, floor, den, recip = [stat[:, c:c + 1] for c in range(6)]
            buf = self.sm_s[:, j * S:j * S + k]
            dve.hold(self.passed)
            dve.seq(nc.vector.tensor_tensor_reduce(out=buf, in0=G, in1=u["mask"], scale=1.0, scalar=0.0,
                                                   op0=ALU.subtract, op1=ALU.max, accum_out=M))
            dve.did(nc.vector.tensor_scalar(neg, M, -1.0, None, ALU.mult))
            act.wait(dve.did(nc.vector.tensor_tensor(m, M, u["F"], ALU.add)))
            act.did(nc.scalar.activation(buf, buf, ACT.Exp, bias=neg))
            dve.wait(act.did(nc.scalar.activation(floor, m, ACT.Exp, scale=-1.0)))
            if i >= 3:
                dve.wait(st[i - 3]["flipped"])
            dve.hold(self.passed)
            s["masked"] = s["exp"] = dve.seq(nc.vector.tensor_tensor_reduce(
                out=s["e"], in0=s["ps"], in1=buf, scale=HD2 ** -0.5, scalar=0.0, op0=ALU.mult, op1=ALU.add, accum_out=den))
            dve.seq(nc.vector.scalar_tensor_tensor(floor, den, -1.0, floor, ALU.mult, ALU.max))
            dve.seq(nc.vector.tensor_tensor(den, den, floor, ALU.max))
            s["recip"] = dve.did(nc.vector.reciprocal(recip, den))
            s["r"] = recip

        def flip(i):
            u, s = units[i], st[i]
            k = u["keys"]
            kt = -(-k // P)
            bank = self.ps[4 + i % R]
            pe.wait(s["exp"])
            if i >= R:
                pe.wait(st[i - R]["eT"])
            for c in range(kt):
                w = min(P, k - c * P)
                ins = nc.tensor.transpose(bank[0:w, c * P:(c + 1) * P], s["e"][:, c * P:c * P + w], self.c("ident"))
            s["flipped"] = pe.did(ins)
            q = act if i % 2 else dve
            q.wait(s["flipped"])
            if i >= R:
                q.wait(st[i - R]["mixed"])
            w = min(P, k)
            s["eT_buf"] = self.sm_eT[0:w, (i % R) * S:(i % R) * S + kt * P]
            ins = (nc.scalar.activation(s["eT_buf"], bank[0:w, 0:kt * P], ACT.Copy) if q is act
                   else nc.vector.tensor_copy(s["eT_buf"], bank[0:w, 0:kt * P]))
            s["eT"] = q.did(ins)

        def mix(i):
            u, s = units[i], st[i]
            kt = -(-u["keys"] // P)
            o = self.ps[6 + i % R][:, 0:u["dv"]]
            pe.wait(s["eT"])
            if i >= R:
                pe.wait(st[i - R]["out"])
            for c in range(kt):
                ins = nc.tensor.matmul(o, s["eT_buf"][:, c * P:(c + 1) * P], u["v"][c], start=(c == 0), stop=(c == kt - 1))
            s["mixed"] = pe.did(ins)
            dve.wait(s["mixed"], s["recip"])
            s["out"] = u["out"](o, s["r"])

        for w in range(n + 2):
            if w < n:
                scores(w)
                soften(w)
            if 0 <= w - 1 < n:
                flip(w - 1)
            if 0 <= w - 2 < n:
                mix(w - 2)

    def stage_q(self, src, dst):
        nc, pe, act = self.nc, self.pe, self.act
        d = src.shape[2]
        q = self.q_stage[:, 0:T * d].rearrange("p (t d) -> p t d", t=T)
        m = act.did(nc.scalar.activation(q, src, ACT.Copy))
        pe.wait(m)
        pe.hold(self.passed)
        for t in range(T):
            ins = nc.tensor.transpose(self.ps[0][0:d, t * P:(t + 1) * P], q[:, t, :], self.c("ident"))
        m = pe.did(ins)
        act.wait(m)
        m = act.did(nc.scalar.activation(dst, self.ps[0][0:d, 0:S], ACT.Copy))
        pe.wait(m)

    def causal(self, t):
        return self.c("causal")[:, P:2 * P] if t == 0 else self.c("causal")

    def scaled(self, out, O, r):
        return self.dve.did(self.nc.vector.tensor_scalar(out, O, r, None, ALU.mult))

    def gate_with_silu(self, z, out):
        nc, act, dve = self.nc, self.act, self.dve
        for t in range(T):
            m = act.did(nc.scalar.activation(z[:, t, :], z[:, t, :], ACT.Silu))
            dve.wait(m)
            m = dve.did(nc.vector.tensor_tensor(out[:, t, :], out[:, t, :], z[:, t, :], ALU.mult))

    def project_out(self, W):
        nc, dve, pe = self.nc, self.dve, self.pe
        self.meet()
        self.transpose_split(self.mixed)
        self.meet()
        dve.wait(*self.project_tokens(self.hT, W, D, 0, D, self.mixed))
        for t in range(T):
            dve.did(nc.vector.tensor_tensor(self.x[:, t, :], self.x[:, t, :], self.mixed[:, t, :], ALU.add))
        self.meet()

    def load_params(self):
        nc, A = self.nc, self.A
        self.rowstat = self.take_fixed(64)
        self.minus_half = self.take_fixed(32)
        self.small.count(nc.scalar.dma_start(self.const[:, :], A["const_small"]))
        for t in range(T):
            self.small.count(nc.scalar.dma_start(self.x[:, t, :], A["x"][0, t * P:(t + 1) * P, :]))
        self.g_norm = [self.param_cols(A["norm_gain"][i], KC) for i in range(2)]
        self.g_mem = self.param_cols(A["mem_norm_gain"], KC)
        self.g_memqk = [[self.param(A["mem_qk_gain"][i, j], HD) for j in range(2)] for i in range(2)]
        self.g_nsa = [self.param(A["nsa_qk_gain"][0, j], HD) for j in range(4)]
        self.g_diff = [self.param(A["diff_qk_gain"][0, j], HD2) for j in range(2)]
        self.g_subln = self.param(A["diff_subln_gain"][0], HD)
        self.g_dsa = [self.param(A["dsa_qk_gain"][0, j], HD) for j in range(2)]
        self.lam = self.param(A["diff_lambda"][0].rearrange("a b -> (a b)"), 4 * HD2)
        self.second_params()
        nc.gpsimd.memset(self.minus_half[:, :], -0.5).then_inc(self.pool.sem, 1)
        self.pool.k += 1
        self.params_landed = self.small.now()
        for q in (self.pe, self.act, self.dve, self.pool):
            q.wait(self.params_landed)
        dve = self.dve
        for g, d in ((self.g_nsa[0], HD), (self.g_dsa[0], HD), (self.g_diff[0], HD2),
                     (self.g_memqk[0][0], HD), (self.g_memqk[1][0], HD)):
            dve.seq(nc.vector.tensor_scalar(g, g, -float(d) ** -0.5, None, ALU.mult))
        self.meet()

    def take_fixed(self, cols):
        self.fixed_at += cols
        assert self.fixed_at <= FIXED
        return self.fixed[:, self.fixed_at - cols:self.fixed_at]

    def fresh_work(self):
        self.meet()
        self.work_at, self.spare_at = self.work_fixed, 0

    def attention_buffers(self, heads=8):
        self.prep_tmp = self.take(heads * HD)
        self.rope_tmp = self.take(heads * HD // 2)
        self.sm_s = self.take_spare(3 * S)
        self.sm_e = self.take_spare(3 * S)
        self.sm_eT = self.take_spare(2 * S)
        self.sm_stat = self.take_spare(12)
        self.q_stage = self.take_spare(T * P)
        self.qT = self.take_spare(S)
        self.q2 = self.take_spare(2 * S)

    def first_block(self):
        nc, A, pe, act, dve, pool = self.nc, self.A, self.pe, self.act, self.dve, self.pool
        self.mkv = [self.proj[:, 8192 * i:8192 * i + 2048].rearrange("p (t n) -> p t n", t=T) for i in range(2)]
        self.memkT = [self.proj[:, 14336 + i * 4 * S:14336 + (i + 1) * 4 * S] for i in range(2)]
        self.memv = [self.take(T * 512) for i in range(2)]
        self.work_fixed = self.work_at
        for t in range(T):
            m = self.work_ld.count(nc.scalar.dma_start(self.proj[:, t * D:(t + 1) * D], A["mem"][0, t * P:(t + 1) * P, :]))
        act.wait(m)
        dve.wait(m)
        self.norm_to_hT(self.proj[:, 0:T * D].rearrange("p (t n) -> p t n", t=T), self.g_mem)
        self.attention_buffers()
        for i in range(2):
            kv = self.mkv[i]
            dve.wait(*self.project_tokens(self.hT, A["mem_w_kv"][i], D, 0, 1024, kv))
            self.prep(lambda t: kv[:, t, 0:512].rearrange("p (n d) -> p n d", d=HD), 4, HD, self.g_memqk[i][1], False)
            for t in range(T):
                m = dve.did(nc.vector.tensor_copy(self.memv[i][:, t * 512:(t + 1) * 512], kv[:, t, 512:1024]))
            self.meet()
            self.transpose_tokens(kv[:, :, 0:512], self.memkT[i].rearrange("p (c s) -> p c s", c=4))
            self.meet()
        self.even_layer()
        self.odd_layer()
        self.meet()

    def memory_heads(self, i, pr, q_col, out_col):
        nc = self.nc
        mv = self.memv[i].rearrange("p (t n) -> p t n", t=T)
        kT = self.memkT[i].rearrange("p (h s) -> p h s", h=4)
        with self.loop(4, ("pe", "act", "dve", "pool"), **self.per["mem"]) as h:
            self.meet()
            self.stage_q(pr[:, :, ds(h * HD + q_col, HD)], self.qT)
            self.attention([dict(qT=self.qT[:, t * P:(t + 1) * P], kT=kT[:, ds(h, 1), :].rearrange("p a s -> p (a s)"), keys=S,
                                 mask=self.c("zeros"), v=[mv[:, c, ds(h * HD, HD)] for c in range(T)], dv=HD,
                                 out=lambda O, r, t=t: self.scaled(self.mixed[:, t, ds(h * HD + out_col, HD)], O, r))
                            for t in range(T)])
        self.meet()

    per = dict(mem=dict(pe=7, act=5, dve=9),
               nsa=dict(pe=19, act=11, dve=35), diff=dict(pe=16, act=14, dve=20), dsa=dict(pe=7, act=5, dve=9),
               idx=dict(pe=3, act=4, dve=2), ret=dict(pe=4, act=4, dve=4), mlstm=dict(pe=18, act=12, dve=36), rwkv=dict(pe=71, act=32, dve=84))

    def even_layer(self):
        nc, A, pe, act, dve, pool = self.nc, self.A, self.pe, self.act, self.dve, self.pool
        E = EVEN
        self.fresh_work()
        self.attention_buffers()
        self.norm_to_hT(self.x, self.g_norm[0])
        pr = self.proj[:, 0:T * EVEN_IN].rearrange("p (t n) -> p t n", t=T)
        kvT = self.take_spare(4 * S).rearrange("p (c s) -> p c s", c=4)
        rawT = self.take_spare(S)
        blkT = self.take_spare(CMP_LEN * 2 * NCMP).rearrange("p (l g c) -> p l g c", l=CMP_LEN, g=2)
        peT = self.take(CMP_LEN)
        pe_rows = self.take(HD)
        hid = self.take(CMP_HID)
        hidT = self.take(2 * 2 * NCMP)
        kc = self.take(HD)
        kcT = self.take(2 * NCMP)
        vc = self.take(HD)
        w2 = [self.take(2 * HD).rearrange("p (c n) -> p c n", c=2) for _ in range(2)]
        pos = [pe_rows, self.take(HD)]
        for j in range(2):
            m = self.work_ld.count(nc.scalar.dma_start(w2[j], A["nsa_cmp_w2"][0, j].rearrange("(c p) n -> p c n", p=P)))
            m = self.work_ld.count(nc.scalar.dma_start(pos[j][0:CMP_LEN, :], A["nsa_cmp_pos"][0, j]))
        pe.wait(m)

        dve.wait(*self.project_tokens(self.hT, A["even_w_in"][0], D, 0, EVEN_IN, pr))
        heads = lambda col, n, d: (lambda t: pr[:, t, col:col + n * d].rearrange("p (n d) -> p n d", d=d))
        self.prep(heads(E["a_q"], 8, HD), 8, HD, self.g_nsa[0], True)
        self.prep(heads(E["a_kv"] + 2 * 256, 2, HD), 2, HD, self.g_nsa[2], True)
        self.prep(heads(E["a_kv"] + 4 * 256, 2, HD), 2, HD, self.g_nsa[3], True)
        self.prep(heads(E["b_q"], 8, HD2), 8, HD2, self.g_diff[0], True)
        self.prep(heads(E["b_k"], 8, HD2), 8, HD2, self.g_diff[1], True)
        self.prep(heads(E["m_q"], 4, HD), 4, HD, self.g_memqk[0][0], False)
        self.meet()
        act.seq(nc.scalar.activation(pr[:, :, E["a_g"]:E["a_z"]], pr[:, :, E["a_g"]:E["a_z"]], ACT.Sigmoid))

        w1 = [A["nsa_cmp_w1"][0, j].rearrange("(u l p) n -> u p l n", l=4, p=P) for j in range(2)]
        slot_read = {}
        for j in range(2):
            pe.seq(nc.tensor.transpose(self.ps[2][:, 0:CMP_LEN], pos[j][0:CMP_LEN, :], self.c("ident")[0:CMP_LEN, 0:CMP_LEN]))
            dve.wait(pe.now())
            dve.seq(nc.vector.tensor_copy(peT, self.ps[2][:, 0:CMP_LEN]))
            for g in range(2):
                col = E["a_kv"] + j * 256 + g * HD
                if g:
                    pe.wait(dve.now())
                for t in range(T):
                    ins = nc.tensor.transpose(self.ps[3][:, t * P:(t + 1) * P], pr[:, t, col:col + HD], self.c("ident"))
                dve.wait(pe.did(ins))
                dve.seq(nc.vector.tensor_copy(rawT, self.ps[3][:, 0:S]))
                win = bass.AP(rawT.tensor, rawT.offset, [rawT.ap[0], [1, CMP_LEN], [CMP_STRIDE, NCMP]])
                dve.seq(nc.vector.tensor_tensor(blkT[:, :, g, :], win, peT.unsqueeze(2).broadcast_to([P, CMP_LEN, NCMP]), ALU.add))
            pe.wait(dve.now())
            for u in range(8):
                i = u % SLOTS
                nc.sync.wait_ge(*self.ready[i].now())
                if u >= SLOTS:
                    nc.sync.wait_ge(*slot_read[i])
                wv = self.raw[i][:, :, :].rearrange("p c n -> p (c n)").rearrange("p (l n) -> p l n", l=4)
                self.full[i].count(nc.sync.dma_start(wv, w1[j][u]))
                pe.wait(self.full[i].now())
                for l in range(4):
                    k = u * 4 + l
                    ins = nc.tensor.matmul(self.ps[4][0:2 * NCMP, 0:CMP_HID], blkT[:, k, :, :].rearrange("p g c -> p (g c)"), wv[:, l, :],
                                           start=(k == 0), stop=(k == CMP_LEN - 1))
                slot_read[i] = released = pe.did(ins)
            nc.sync.wait_ge(*released)
            act.wait(released)
            act.seq(nc.scalar.activation(hid[0:2 * NCMP, :], self.ps[4][0:2 * NCMP, 0:CMP_HID], ACT.Silu))
            pe.wait(act.now())
            for c in range(2):
                ins = nc.tensor.transpose(self.ps[5][:, c * 2 * NCMP:(c + 1) * 2 * NCMP], hid[0:2 * NCMP, c * P:(c + 1) * P],
                                          self.c("ident")[0:2 * NCMP, 0:2 * NCMP])
            dve.wait(pe.did(ins))
            dve.seq(nc.vector.tensor_copy(hidT, self.ps[5][:, 0:4 * NCMP]))
            pe.wait(dve.now())
            for c in range(2):
                ins = nc.tensor.matmul(self.ps[6][0:2 * NCMP, 0:HD], hidT[:, c * 2 * NCMP:(c + 1) * 2 * NCMP], w2[j][:, c, :],
                                       start=(c == 0), stop=(c == 1))
            dve.wait(pe.did(ins))
            if j == 1:
                dve.seq(nc.vector.tensor_copy(vc[0:2 * NCMP, :], self.ps[6][0:2 * NCMP, 0:HD]))
            else:
                R2 = 2 * NCMP
                three = lambda a: a[0:R2, :].rearrange("p (n d) -> p n d", n=1)
                dve.seq(nc.vector.tensor_copy(kc[0:R2, :], self.ps[6][0:R2, 0:HD]))
                tmp = self.prep_tmp[:, 0:HD]
                self.head_norm(three(kc), three(tmp), 1, HD, self.g_nsa[1], rows=R2)
                self.rope(three(tmp), three(kc), 1, HD, self.c("cos_cmp")[0:R2], self.c("sin_cmp")[0:R2], rows=R2)
                pe.wait(dve.now())
                pe.seq(nc.tensor.transpose(self.ps[7][:, 0:R2], kc[0:R2, :], self.c("ident")[0:R2, 0:R2]))
                dve.wait(pe.now())
                dve.seq(nc.vector.tensor_copy(kcT, self.ps[7][:, 0:R2]))
            self.meet()

        self.transpose_tokens(pr[:, :, E["a_kv"] + 512:E["a_kv"] + 768], kvT[:, 0:2, :])
        self.meet()
        self.transpose_tokens(pr[:, :, E["a_kv"] + 1024:E["a_kv"] + 1280], kvT[:, 2:4, :])
        self.meet()
        gates = pr[:, :, E["a_g"]:E["a_z"]]
        for g in range(2):
            with self.loop(4, ("pe", "act", "dve", "pool"), **self.per["nsa"]) as r:
                self.meet()
                self.stage_q(pr[:, :, ds(r * HD + g * 4 * HD, HD)], self.qT)
                units = []
                for t in range(T):
                    for b in range(3):
                        def out(O, rc, t=t, b=b):
                            dst = self.mixed[:, t, ds(r * HD + g * 4 * HD, HD)]
                            dve.seq(nc.vector.tensor_tensor(self.coef, rc, gates[:, t, ds(r * 3 + (g * 12 + b), 1)], ALU.mult))
                            if b == 0:
                                return dve.seq(nc.vector.tensor_scalar(dst, O, self.coef, None, ALU.mult))
                            return dve.seq(nc.vector.scalar_tensor_tensor(dst, O, self.coef, dst, ALU.mult, ALU.add))
                        u = dict(qT=self.qT[:, t * P:(t + 1) * P], dv=HD, out=out)
                        if b == 0:
                            u.update(kT=kcT, keys=2 * NCMP, mask=self.c(f"cmp_drop{g}{t}"), keep=self.c(f"cmp_keep{g}{t}"),
                                     v=[vc[0:2 * NCMP, :]])
                        else:
                            vcol = E["a_kv"] + (3 if b == 1 else 5) * 256 + g * HD
                            u.update(kT=kvT[:, 2 * (b - 1) + g, 0:(t + 1) * P], keys=(t + 1) * P, mask=self.causal(t),
                                     v=[pr[:, c, vcol:vcol + HD] for c in range(t + 1)])
                        units.append(u)
                self.attention(units)
            self.meet()

        lam, lt = self.rowstat[:, 20:24], self.prep_tmp
        for j in range(2):
            dve.seq(nc.vector.tensor_tensor(lt[:, 0:HD2], self.lam[:, 2 * j * HD2:(2 * j + 1) * HD2],
                                            self.lam[:, (2 * j + 1) * HD2:(2 * j + 2) * HD2], ALU.mult))
            dve.seq(nc.vector.tensor_reduce(lam[:, j:j + 1], lt[:, 0:HD2], AX.X, ALU.add))
        act.wait(dve.now())
        act.seq(nc.scalar.activation(lam[:, 0:2], lam[:, 0:2], ACT.Exp))
        dve.wait(act.now())
        dve.seq(nc.vector.tensor_tensor(lam[:, 2:3], lam[:, 1:2], lam[:, 0:1], ALU.subtract))
        dve.seq(nc.vector.tensor_scalar(lam[:, 2:3], lam[:, 2:3], LAMBDA_INIT, None, ALU.subtract))
        kT2 = self.take_spare(2 * S)
        self.meet()
        with self.loop(4, ("pe", "act", "dve", "pool"), **self.per["diff"]) as h:
            self.meet()
            units = []
            for c in range(2):
                self.stage_q(pr[:, :, ds(h * HD + (E["b_q"] + c * HD2), HD2)], self.q2[0:HD2, c * S:(c + 1) * S])
                self.stage_q(pr[:, :, ds(h * HD + (E["b_k"] + c * HD2), HD2)], kT2[0:HD2, c * S:(c + 1) * S])
            for t in range(T):
                for c in range(2):
                    def out(O, rc, t=t, c=c):
                        dst = self.mixed[:, t, ds(h * HD + 1024, HD)]
                        if c == 0:
                            return dve.seq(nc.vector.tensor_scalar(dst, O, rc, None, ALU.mult))
                        dve.seq(nc.vector.tensor_tensor(self.coef, rc, lam[:, 2:3], ALU.mult))
                        return dve.seq(nc.vector.scalar_tensor_tensor(dst, O, self.coef, dst, ALU.mult, ALU.add))
                    units.append(dict(qT=self.q2[0:HD2, c * S + t * P:c * S + (t + 1) * P], dv=HD, out=out,
                                      kT=kT2[0:HD2, c * S:c * S + (t + 1) * P], keys=(t + 1) * P, mask=self.causal(t),
                                      v=[pr[:, k, ds(h * HD + E["b_v"], HD)] for k in range(t + 1)]))
            self.attention(units)
        self.meet()
        for t in range(T):
            o = self.mixed[:, t, 1024:1536].rearrange("p (n d) -> p n d", d=HD)
            tmp = self.prep_tmp[:, 0:512].rearrange("p (n d) -> p n d", d=HD)
            self.head_norm(o, tmp, 4, HD, self.g_subln)
            dve.seq(nc.vector.tensor_scalar(o, tmp, 1.0 - LAMBDA_INIT, None, ALU.mult))
        self.meet()
        self.memory_heads(0, pr, E["m_q"], 1536)
        self.gate_with_silu(pr[:, :, E["a_z"]:E["a_z"] + 1024], self.mixed[:, :, 0:1024])
        self.gate_with_silu(pr[:, :, E["b_z"]:E["b_z"] + 512], self.mixed[:, :, 1024:1536])
        self.gate_with_silu(pr[:, :, E["m_z"]:E["m_z"] + 512], self.mixed[:, :, 1536:2048])
        self.project_out(A["w_out"][0])

    def odd_layer(self):
        nc, A, pe, act, dve, pool = self.nc, self.A, self.pe, self.act, self.dve, self.pool
        O_ = ODD
        self.fresh_work()
        self.attention_buffers(12)
        self.norm_to_hT(self.x, self.g_norm[1])
        pr = self.proj[:, 0:T * ODD_IN].rearrange("p (t n) -> p t n", t=T)
        kT = self.take_spare(4 * S).rearrange("p (c s) -> p c s", c=4)
        kiT = self.take_spare(S)
        score = self.take_spare(T * S).rearrange("p (t s) -> p t s", t=T)
        drop = self.take_spare(T * S).rearrange("p (t s) -> p t s", t=T)
        rel = self.take_spare(T * S).rearrange("p (t s) -> p t s", t=T)
        best = self.take(8 * T)
        dve.wait(*self.project_tokens(self.hT, A["odd_w_in"][0], D, 0, ODD_IN, pr))
        heads = lambda col, n, d: (lambda t: pr[:, t, col:col + n * d].rearrange("p (n d) -> p n d", d=d))
        self.prep(heads(O_["c_q"], 12, HD), 12, HD, self.g_dsa[0], True)
        self.prep(heads(O_["c_k"], 4, HD), 4, HD, self.g_dsa[1], True)
        self.prep(heads(O_["i_q"], 16, HD2), 16, HD2, None, True, norm=False)
        self.prep(heads(O_["i_k"], 1, HD2), 1, HD2, None, True, norm=False)
        wi = pr[:, :, O_["i_w"]:O_["c_z"]]
        dve.seq(nc.vector.tensor_scalar(wi, wi, 16.0 ** -0.5 * 64.0 ** -0.5, None, ALU.mult))
        self.prep(heads(O_["m_q"], 4, HD), 4, HD, self.g_memqk[1][0], False)
        dve.seq(nc.vector.memset(score, 0.0))
        self.meet()
        self.transpose_tokens(pr[:, :, O_["c_k"]:O_["c_v"]], kT)
        self.meet()
        self.stage_q(pr[:, :, O_["i_k"]:O_["i_w"]], kiT[0:HD2, :])
        self.meet()
        with self.loop(16, ("pe", "act", "dve", "pool"), **self.per["idx"]) as h:
            self.meet()
            self.stage_q(pr[:, :, ds(h * HD2 + O_["i_q"], HD2)], self.q2[0:HD2, 0:S])
            for t in range(T):
                k = (t + 1) * P
                m = pe.did(nc.tensor.matmul(self.ps[2 + t][:, 0:k], self.q2[0:HD2, t * P:(t + 1) * P], kiT[0:HD2, 0:k],
                                            start=True, stop=True))
                act.wait(m)
                m = act.did(nc.scalar.activation(rel[:, t, 0:k], self.ps[2 + t][:, 0:k], ACT.Relu))
                dve.wait(m)
                dve.did(nc.vector.scalar_tensor_tensor(score[:, t, 0:k], rel[:, t, 0:k], pr[:, t, ds(h + O_["i_w"], 1)],
                                                       score[:, t, 0:k], ALU.mult, ALU.add))
        self.meet()
        TAKEN = -3e38
        for t in range(T):
            k = (t + 1) * P
            s_, m_ = score[:, t, 0:k], self.causal(t)
            dve.seq(nc.vector.tensor_tensor(s_, s_, m_, ALU.subtract))
        for rnd in range(TOPK // 8):
            for t in range(T):
                s_ = score[:, t, 0:(t + 1) * P]
                dve.did(nc.vector.max(best[:, 8 * t:8 * t + 8], s_))
            dve.wait(dve.now())
            for t in range(T):
                s_ = score[:, t, 0:(t + 1) * P]
                dve.did(nc.vector.match_replace(s_, best[:, 8 * t:8 * t + 8], s_, TAKEN))
            dve.wait(dve.now())
        for t in range(T):
            k = (t + 1) * P
            dve.seq(nc.vector.tensor_scalar(drop[:, t, 0:k], score[:, t, 0:k], -2e38, BIG, ALU.is_gt, ALU.mult))
            dve.seq(nc.vector.tensor_tensor(drop[:, t, 0:k], drop[:, t, 0:k], self.causal(t), ALU.add))
        for g in range(4):
            with self.loop(3, ("pe", "act", "dve", "pool"), **self.per["dsa"]) as r:
                self.meet()
                self.stage_q(pr[:, :, ds(r * HD + g * 3 * HD, HD)], self.qT)
                vcol = O_["c_v"] + g * HD
                self.attention([dict(qT=self.qT[:, t * P:(t + 1) * P], dv=HD, kT=kT[:, g, 0:(t + 1) * P], keys=(t + 1) * P,
                                     mask=drop[:, t, 0:(t + 1) * P], v=[pr[:, c, vcol:vcol + HD] for c in range(t + 1)],
                                     out=lambda O, rc, t=t: self.scaled(self.mixed[:, t, ds(r * HD + g * 3 * HD, HD)], O, rc))
                                for t in range(T)])
            self.meet()
        self.memory_heads(1, pr, O_["m_q"], 1536)
        self.gate_with_silu(pr[:, :, O_["c_z"]:O_["c_z"] + 1536], self.mixed[:, :, 0:1536])
        self.gate_with_silu(pr[:, :, O_["m_z"]:O_["m_z"] + 512], self.mixed[:, :, 1536:2048])
        self.project_out(A["w_out"][1])

    def main(self):
        self.coef = self.take_fixed(1)
        self.first_block()
        self.second_block()

    def second_params(self):
        A = self.A
        self.b2 = []
        for l in range(2):
            q = {}
            for name, n in (("norm_pre_mix_2", KC), ("norm_pre_ffn_2", KC), ("rwkv_mu_2", 14), ("rwkv_w0_2", 4),
                            ("rwkv_a0_2", 4), ("rwkv_k_k_2", 4), ("rwkv_k_a_2", 4), ("rwkv_r_k_2", 4),
                            ("mlstm_conv_b_2", 8)):
                q[name] = self.param_cols(A[name][l], n)
            q["conv"] = [self.param_cols(A["mlstm_conv_w_2"][l, j], 8) for j in range(4)]
            q["lb"] = self.param_cols(A["hgrn_lb_logits_2"][l], 4)
            q["ib"] = self.param(A["mlstm_i_bias_2"][l], H2)
            q["fb"] = self.param(A["mlstm_f_bias_2"][l], H2)
            self.b2.append(q)
        self.b2[1]["v0"] = self.param_cols(A["rwkv_v0_2"][0], 4)

    def load_row(self, dram_row, width):
        dst = self.take(width)
        self.work_ld.count(self.nc.scalar.dma_start(dst, dram_row.partition_broadcast(P)))
        return dst

    def load_work(self, dst, src):
        self.work_ld.count(self.nc.scalar.dma_start(dst, src))

    def work_landed(self):
        for q in (self.pe, self.act, self.dve, self.pool):
            q.wait(self.work_ld.now())

    def second_block(self):
        self.v_first = self.take_fixed(4 * S)
        for l in range(2):
            self.second_layer(l)

    def second_layer(self, l):
        nc, A, pe, act, dve, pool = self.nc, self.A, self.pe, self.act, self.dve, self.pool
        self.meet()
        self.work_at = self.work_fixed = self.spare_at = 0
        q = self.b2[l]
        self.norm_to_hT(self.x, q["norm_pre_mix_2"])
        NT = 8 * GW + 2 * H2
        pt = self.proj[:, 0:T * NT].rearrange("p (t n) -> p t n", t=T)
        pf = self.proj[:, T * NT:T * NT + 30 * S].rearrange("p (c s) -> p c s", c=30)
        W = A["w_in_2"][l]
        Wu = self.units_of(W)
        self.run_steps(lambda i: [self.tokens(self.hT, Wu, 8, i * GW, GW, lambda t: pt[:, t, ds(i * GW, GW)])], 4)
        fm = lambda c0, i, w: (lambda j: pf[:, ds(i * w + (c0 + j), 1), :].rearrange("p a s -> p (a s)"))
        c0, rw = 4 * GW, 12 * GW + 2 * H2
        self.run_steps(lambda i: [
            self.features(self.hT, Wu, 8, i * 4 * GW + c0, 4, fm(0, i, 8)),
            self.features(self.hT, Wu, 8, i * 4 * GW + (c0 + GW), 4, fm(4, i, 8)),
            self.tokens(self.hT, Wu, 8, i * 4 * GW + (c0 + 2 * GW), GW, lambda t: pt[:, t, ds(i * 2 * GW + 4 * GW, GW)]),
            self.tokens(self.hT, Wu, 8, i * 4 * GW + (c0 + 3 * GW), GW, lambda t: pt[:, t, ds(i * 2 * GW + 5 * GW, GW)])], 2)
        self.run_steps(lambda i: [self.features(self.hT, Wu, 8, i * GW + rw, 4, fm(16, i, 4))], 3, [
            self.tokens(self.hT, Wu, 8, 12 * GW, 2 * H2, lambda t: pt[:, t, 8 * GW:NT]),
            self.features(self.hT, Wu, 8, rw + 3 * GW, 2, lambda j: pf[:, 28 + j, :])])
        self.meet()
        self.retention(l, pt)
        self.hgrn(l, pt, pf)
        self.mlstm(l, pt, pf)
        self.rwkv(l, pt, pf)
        self.work_at = self.work_fixed
        self.meet()
        self.transpose_split(self.mixed)
        self.meet()
        gain = self.load_row(A["norm_post_mix_2"][l], D)
        self.project_tokens(self.hT, A["w_out_2"][l], D, 0, D, self.mixed)
        self.meet()
        self.add_normed(self.mixed, gain)
        self.norm_to_hT(self.x, q["norm_pre_ffn_2"])
        gain = self.ff_small[:, 0:D]
        self.load_work(gain, A["norm_post_ffn_2"][l].partition_broadcast(P))
        gate = self.ff_small[:, D:D + 4 * S].rearrange("p (c s) -> p c s", c=4)
        prod = self.ff_small[:, D + 4 * S:D + 8 * S].rearrange("p (c s) -> p c s", c=4)
        Gu, Uu = self.units_of(A["w_ffn_gate_2"][l]), self.units_of(A["w_ffn_up_2"][l])

        def gate_and_up(i):
            multiplied = [self.emptied[4 + j].now() for j in range(4)]
            silus = {}

            def silu(j, b, mark):
                act.wait(mark, self.emptied[4 + j].now())
                silus[j] = self.emptied[b].count(nc.scalar.activation(gate[:, j, :], self.ps[b][:, 0:S], ACT.Silu))

            def times(j, b, mark):
                dve.wait(mark, self.emptied[j].now())
                dst = [a[:, ds(i * 4 + j, 1), :].rearrange("p a s -> p (a s)") for a in self.actT]
                m = self.emptied[b].count(nc.vector.tensor_tensor(prod[:, j, :], gate[:, j, :], self.ps[b][:, 0:S], ALU.mult))
                act.wait(m)
                dve.wait(m, act.did(nc.scalar.activation(dst[0], prod[:, j, :], ACT.Copy)))
                dve.did(nc.vector.tensor_tensor(dst[1], prod[:, j, :], dst[0].bitcast(F32), ALU.subtract))
            return [self.features(self.hT, Gu, 8, i * TILE, 4, None, 0, silu),
                    self.features(self.hT, Uu, 8, i * TILE, 4, None, 4, times)]
        self.run_steps(gate_and_up, D_FF // TILE, act=4, dve=4)
        self.meet()
        down = self.spare[:, 0:T * D].rearrange("p (t n) -> p t n", t=T)
        self.project_tokens(self.actT, A["w_ffn_down_2"][l], D_FF, 0, D, down)
        self.meet()
        self.add_normed(down, gain)

    def add_normed(self, y, gain):
        nc, act, dve = self.nc, self.act, self.dve
        ss = self.rowstat[:, 0:T]
        for t in range(T):
            m = act.did(nc.scalar.activation(self.spare[:, T * D + t * D:T * D + (t + 1) * D], y[:, t, :], ACT.Square, accum_out=ss[:, t:t + 1]))
        dve.wait(m)
        self.inv_rms(ss, T, D)
        dve.wait(self.work_ld.now())
        for t in range(T):
            dve.seq(nc.vector.scalar_tensor_tensor(y[:, t, :], y[:, t, :], ss[:, t:t + 1], gain, ALU.mult, ALU.mult))
            dve.seq(nc.vector.tensor_tensor(self.x[:, t, :], self.x[:, t, :], y[:, t, :], ALU.add))
        self.meet()

    def head_rms_gate(self, col, z, func, gain):
        nc, act, dve = self.nc, self.act, self.dve
        for t in range(T):
            o = self.mixed[:, t, col:col + GW].rearrange("p (n d) -> p n d", d=HD2)
            tmp = self.take(GW)
            self.head_norm(o, tmp.rearrange("p (n d) -> p n d", d=HD2), H2, HD2, None)
            if gain is not None:
                dve.seq(nc.vector.tensor_tensor(tmp, tmp, gain, ALU.mult))
            m = act.did(nc.scalar.activation(z[:, t, :], z[:, t, :], func))
            dve.wait(m)
            dve.seq(nc.vector.tensor_tensor(self.mixed[:, t, col:col + GW], tmp, z[:, t, :], ALU.mult))

    def pair(self, fm, j):
        return fm[:, ds(j, 1), :].rearrange("p a s -> p (a s)")

    def retention(self, l, pt):
        nc, pe, act, dve, pool = self.nc, self.pe, self.act, self.dve, self.pool
        self.fresh_work()
        self.prep_tmp, self.rope_tmp = self.take(GW), self.take(GW // 2)
        decay = self.take(H2 * 2 * P)
        self.load_work(decay, self.A["const_decay"])
        qT, kT = [self.take(4 * S).rearrange("p (c s) -> p c s", c=4) for _ in range(2)]
        qs, ks = self.take(S), self.take(S)
        sT = [self.take(3 * P) for _ in range(2)]
        for c in range(2):
            self.prep(lambda t: pt[:, t, c * GW:(c + 1) * GW].rearrange("p (n d) -> p n d", d=HD2), H2, HD2, None, True, norm=False)
        self.meet()
        self.transpose_tokens(pt[:, :, 0:GW], qT)
        self.meet()
        self.transpose_tokens(pt[:, :, GW:2 * GW], kT)
        self.meet()
        self.work_landed()
        dv = decay.rearrange("p (h n) -> p h n", h=H2)
        with self.loop(4, ("pe", "act", "dve", "pool"), **self.per["ret"]) as j:
            self.meet()
            act.did(nc.scalar.activation(qs, self.pair(qT, j), ACT.Copy))
            pe.wait(act.did(nc.scalar.activation(ks, self.pair(kT, j), ACT.Copy)))
            scored = []
            for e in range(2):
                h = slice(e * HD2, (e + 1) * HD2)
                b = self.ps[2 + e]
                nc.tensor.matmul(b[:, 0:S], ks[h, 0:P], qs[h, 0:S], start=True, stop=True)
                scored.append(pe.did(nc.tensor.matmul(b[:, S:S + P], ks[h, P:S], qs[h, P:S], start=True, stop=True)))
            for e in range(2):
                dve.wait(scored[e])
                dve.did(nc.vector.tensor_tensor(sT[e][:, 0:S], self.ps[2 + e][:, 0:S],
                                                dv[:, ds(j * 2 + e, 1), :].rearrange("p a n -> p (a n)"), ALU.mult))
                pe.wait(dve.did(nc.vector.tensor_tensor(sT[e][:, S:S + P], self.ps[2 + e][:, S:S + P],
                                                        dv[:, ds(j * 2 + e, 1), 0:P].rearrange("p a n -> p (a n)"), ALU.mult)))
                v = [pt[:, t, ds(j * 2 * HD2 + (2 * GW + e * HD2), HD2)] for t in range(T)]
                o = self.ps[4 + e]
                nc.tensor.matmul(o[:, 0:HD2], sT[e][:, 0:P], v[0], start=True, stop=True)
                nc.tensor.matmul(o[:, HD2:2 * HD2], sT[e][:, P:S], v[0], start=True, stop=False)
                act.wait(pe.did(nc.tensor.matmul(o[:, HD2:2 * HD2], sT[e][:, S:S + P], v[1], start=False, stop=True)))
                act.did(nc.scalar.activation(self.mixed[:, :, ds(j * 2 * HD2 + e * HD2, HD2)],
                                             o[:, 0:2 * HD2].rearrange("p (t d) -> p t d", t=T), ACT.Copy))
        self.meet()
        self.head_rms_gate(0, pt[:, :, 3 * GW:4 * GW], ACT.Silu, None)

    def cumulate(self, out, src, width):
        nc, dve = self.nc, self.dve
        n = src.shape[1]
        one = self.c("ones")[:, 0:1].broadcast_to([P, width])
        for k in range(0, n, width):
            dve.did(nc.vector.tensor_tensor_scan(out[:, k:k + width], one, src[:, k:k + width], 0.0, ALU.mult, ALU.add))
        dve.wait(dve.now())

    def hgrn(self, l, pt, pf):
        nc, pe, act, dve, pool = self.nc, self.pe, self.act, self.dve, self.pool
        self.fresh_work()
        flat = lambda a: a.rearrange("p c s -> p (c s)")
        q, f = flat(pf[:, 0:4, :]), flat(pf[:, 4:8, :])
        n = 4 * S
        masks = self.take(LEVELS * P)
        self.load_work(masks, self.A["const_halves_T"])
        gain = self.load_row(self.A["hgrn_norm_w_2"][l], GW)
        lb, keep = self.rowstat[:, 24:28], self.rowstat[:, 28:32]
        E, cum, k, qd, kd = [self.take(n) for _ in range(5)]
        acc = self.take(16 * P)
        cross = self.take(H2 * P)
        if l == 1:
            dve.seq(nc.vector.tensor_tensor(lb, self.b2[1]["lb"], self.b2[0]["lb"], ALU.subtract))
            act.wait(dve.now())
            act.seq(nc.scalar.activation(lb, lb, ACT.Sigmoid))
            dve.wait(act.now())
            dve.seq(nc.vector.tensor_scalar(keep, lb, -1.0, 1.0, ALU.mult, ALU.add))
        over = lambda a: a.unsqueeze(2).broadcast_to([P, 4, S])
        v3 = lambda a: a.rearrange("p (c s) -> p c s", c=4)
        act.did(nc.scalar.activation(k, f, ACT.Sigmoid, scale=-1.0))
        act.seq(nc.scalar.activation(q, q, ACT.Silu))
        act.seq(nc.scalar.activation(E, f, ACT.Abs))
        act.seq(nc.scalar.activation(E, E, ACT.Exp, scale=-1.0))
        act.seq(nc.scalar.activation(E, E, ACT.Ln, bias=1.0))
        dve.wait(act.now())
        dve.did(nc.vector.tensor_scalar(q, q, HD2 ** -0.5, None, ALU.mult))
        if l == 0:
            dve.seq(nc.vector.scalar_tensor_tensor(f, f, 0.0, E, ALU.min, ALU.subtract))
        else:
            dve.did(nc.vector.tensor_scalar(qd, f, 0.0, None, ALU.min))
            dve.did(nc.vector.tensor_scalar(kd, f, 0.0, None, ALU.max))
            dve.seq(nc.vector.tensor_tensor(v3(k), v3(k), over(keep), ALU.mult))
            act.wait(dve.now())
            act.did(nc.scalar.activation(qd, qd, ACT.Exp))
            act.did(nc.scalar.activation(kd, kd, ACT.Exp, scale=-1.0))
            dve.wait(act.now())
            dve.seq(nc.vector.tensor_tensor(v3(kd), v3(kd), over(lb), ALU.mult))
            dve.seq(nc.vector.tensor_tensor(qd, qd, kd, ALU.add))
            dve.seq(nc.vector.tensor_scalar(qd, qd, 2.0 ** -60, None, ALU.max))
            act.wait(dve.now())
            act.seq(nc.scalar.activation(qd, qd, ACT.Ln))
            dve.wait(act.now())
            dve.seq(nc.vector.tensor_tensor(f, qd, E, ALU.subtract))
        self.cumulate(cum, f, P)
        dve.seq(nc.vector.memset(acc, 0.0))
        self.work_landed()
        self.meet()
        heads = [(h // 2, slice((h % 2) * HD2, (h % 2 + 1) * HD2)) for h in range(H2)]

        def products(kk, qq, mask, first):
            k3, q3 = v3(kk), v3(qq)
            for g in range(4):
                b = self.ps[2 + g]
                if not first:
                    pe.wait(self.level_read[g])
                for i in range(4):
                    c, h = heads[4 * (g // 2) + g % 2 + 2 * (i // 2)]
                    t = i % 2
                    ins = nc.tensor.matmul(b[:, i * P:(i + 1) * P], k3[h, c, t * P:(t + 1) * P], q3[h, c, t * P:(t + 1) * P],
                                           start=True, stop=True)
                dve.wait(pe.did(ins))
                m = mask.bitcast(mybir.dt.uint32).unsqueeze(1).broadcast_to([P, 4, P])
                self.level_read[g] = dve.did(nc.vector.copy_predicated(
                    acc[:, g * 512:(g + 1) * 512].rearrange("p (i s) -> p i s", i=4), m,
                    b[:, :].rearrange("p (i s) -> p i s", i=4)))
        self.level_read = {}
        products(k, q, self.c("ident"), True)
        for lev in range(LEVELS):
            B = 1 << lev
            blk = lambda a: a.rearrange("p (n b) -> p n b", b=2 * B)
            c3 = blk(cum)
            if lev:
                dve.wait(self.exp_done)
            dve.seq(nc.vector.tensor_tensor(blk(E), c3, c3[:, :, B - 1:B].broadcast_to([P, n // (2 * B), 2 * B]), ALU.subtract))
            act.wait(dve.now())
            act.seq(nc.scalar.activation(E, E, ACT.Abs))
            self.exp_done = act.seq(nc.scalar.activation(E, E, ACT.Exp, scale=-1.0))
            dve.wait(act.now(), pe.now())
            dve.did(nc.vector.tensor_tensor(qd, q, E, ALU.mult))
            dve.seq(nc.vector.tensor_tensor(kd, k, E, ALU.mult))
            pe.wait(dve.now())
            products(kd, qd, masks[:, lev * P:(lev + 1) * P], False)
        c3, E3, qd3, kd3 = v3(cum), v3(E), v3(qd), v3(kd)
        dve.seq(nc.vector.tensor_tensor(E3[:, :, 0:P], c3[:, :, P - 1:P].broadcast_to([P, 4, P]), c3[:, :, 0:P], ALU.subtract))
        dve.seq(nc.vector.tensor_copy(E3[:, :, P:S], c3[:, :, P:S]))
        act.wait(dve.now())
        act.seq(nc.scalar.activation(E, E, ACT.Exp))
        dve.wait(act.now(), pe.now())
        dve.did(nc.vector.tensor_tensor(kd3[:, :, 0:P], v3(k)[:, :, 0:P], E3[:, :, 0:P], ALU.mult))
        dve.seq(nc.vector.tensor_tensor(qd3[:, :, P:S], v3(q)[:, :, P:S], E3[:, :, P:S], ALU.mult))
        pe.wait(dve.now())
        for g in range(2):
            for i in range(4):
                c, h = heads[g + 2 * i]
                ins = nc.tensor.matmul(self.ps[6 + g][:, i * P:(i + 1) * P], kd3[h, c, 0:P], qd3[h, c, P:S], start=True, stop=True)
            act.wait(pe.did(ins))
            pe.wait(act.did(nc.scalar.activation(cross[:, g * 512:(g + 1) * 512], self.ps[6 + g][:, :], ACT.Copy)))
        i0 = 4 * GW
        for t in range(T):
            o = self.ps[t]
            for h in range(H2):
                v = [pt[:, c, i0 + h * HD2:i0 + (h + 1) * HD2] for c in range(T)]
                at = 4 * (2 * (h // 4) + h % 2) + 2 * ((h % 4) // 2) + t
                a = acc[:, at * P:(at + 1) * P]
                x = cross[:, (4 * (h % 2) + h // 2) * P:(4 * (h % 2) + h // 2 + 1) * P]
                ins = nc.tensor.matmul(o[:, h * HD2:(h + 1) * HD2], a, v[t], start=True, stop=(t == 0))
                if t:
                    ins = nc.tensor.matmul(o[:, h * HD2:(h + 1) * HD2], x, v[0], start=False, stop=True)
            act.wait(pe.did(ins))
            act.did(nc.scalar.activation(self.mixed[:, t, GW:2 * GW], o[:, :], ACT.Copy))
        self.meet()
        self.head_rms_gate(GW, pt[:, :, 5 * GW:6 * GW], ACT.Sigmoid, gain)

    def mlstm(self, l, pt, pf):
        nc, pe, act, dve, pool = self.nc, self.pe, self.act, self.dve, self.pool
        q_ = self.b2[l]
        self.fresh_work()
        gain = self.load_row(self.A["mlstm_norm_w_2"][l], GW)
        self.sm_s, self.sm_e, self.sm_eT, self.sm_stat = self.take(3 * S), self.take(3 * S), self.take(2 * S), self.take(24)
        gates = self.take(4 * T * H2).rearrange("p (k t h) -> p k t h", k=4, t=T)
        li, lf, cum, G = [gates[:, k, :, :] for k in range(4)]
        qs, ks, gs, fs = self.take(S), self.take(S), self.take(T * 2), self.take(T * 2)
        for c in range(8):
            src, dst = pf[:, 8 + c, :], pf[:, c, :]
            w = [x[:, c:c + 1] for x in q_["conv"]]
            dve.seq(nc.vector.tensor_scalar(dst, src, w[3], q_["mlstm_conv_b_2"][:, c:c + 1], ALU.mult, ALU.add))
            for d in range(1, 4):
                dve.seq(nc.vector.scalar_tensor_tensor(dst[:, d:S], src[:, 0:S - d], w[3 - d], dst[:, d:S], ALU.mult, ALU.add))
        act.wait(dve.now())
        qk = pf[:, 0:8, :].rearrange("p c s -> p (c s)")
        act.seq(nc.scalar.activation(qk, qk, ACT.Silu))
        raw = pt[:, :, 8 * GW:8 * GW + 2 * H2]
        row = lambda a: a.unsqueeze(1).broadcast_to([P, T, H2])
        dve.did(nc.vector.tensor_tensor(li, raw[:, :, 0:H2], row(q_["ib"]), ALU.add))
        dve.seq(nc.vector.tensor_tensor(lf, raw[:, :, H2:2 * H2], row(q_["fb"]), ALU.add))
        act.wait(dve.now())
        act.seq(nc.scalar.activation(G, lf, ACT.Abs))
        act.seq(nc.scalar.activation(G, G, ACT.Exp, scale=-1.0))
        act.seq(nc.scalar.activation(G, G, ACT.Ln, bias=1.0))
        dve.wait(act.now())
        dve.seq(nc.vector.scalar_tensor_tensor(lf, lf, 0.0, G, ALU.min, ALU.subtract))
        pe.wait(dve.now())
        nc.tensor.matmul(self.ps[2][:, 0:H2], self.c("upto_T"), lf[:, 0, :], start=True, stop=True)
        nc.tensor.matmul(self.ps[2][:, H2:2 * H2], self.c("ones"), lf[:, 0, :], start=True, stop=False)
        dve.wait(pe.did(nc.tensor.matmul(self.ps[2][:, H2:2 * H2], self.c("upto_T"), lf[:, 1, :], start=False, stop=True)))
        dve.seq(nc.vector.tensor_copy(cum, self.ps[2][:, 0:2 * H2].rearrange("p (t h) -> p t h", t=T)))
        dve.seq(nc.vector.tensor_tensor(G, li, cum, ALU.subtract))
        self.meet()
        st3 = lambda a: a.rearrange("p (t e) -> p t e", t=T)
        with self.loop(4, ("pe", "act", "dve", "pool"), **self.per["mlstm"]) as j:
            self.meet()
            act.did(nc.scalar.activation(qs, self.pair(pf[:, 0:4, :], j), ACT.Copy))
            act.did(nc.scalar.activation(ks, self.pair(pf[:, 4:8, :], j), ACT.Copy))
            dve.did(nc.vector.tensor_copy(st3(gs), G[:, :, ds(j * 2, 2)]))
            dve.seq(nc.vector.tensor_copy(st3(fs), cum[:, :, ds(j * 2, 2)]))
            pe.wait(act.now(), dve.now())
            units = []
            for e in range(2):
                h = slice(e * HD2, (e + 1) * HD2)
                for t in range(T):
                    units.append(dict(
                        mlstm=True, qT=qs[h, t * P:(t + 1) * P], kT=ks[h, 0:(t + 1) * P], keys=(t + 1) * P, mask=self.causal(t),
                        gates=[st3(gs)[:, c, e:e + 1] for c in range(t + 1)], F=st3(fs)[:, t, e:e + 1], dv=HD2,
                        v=[pt[:, c, ds(j * 2 * HD2 + (6 * GW + e * HD2), HD2)] for c in range(t + 1)],
                        out=lambda O, r, t=t, e=e: self.scaled(self.mixed[:, t, ds(j * 2 * HD2 + (2 * GW + e * HD2), HD2)], O, r)))
            self.attention(units)
        self.meet()
        self.work_landed()
        self.head_rms_gate(2 * GW, pt[:, :, 7 * GW:8 * GW], ACT.Sigmoid, gain)

    def rwkv(self, l, pt, pf):
        nc, pe, act, dve, pool = self.nc, self.pe, self.act, self.dve, self.pool
        q_, A = self.b2[l], self.A
        self.fresh_work()
        lora, g_up = self.take(GW), self.take(GW)
        self.load_work(lora[0:64, :], A["rwkv_w_up_2"][l])
        self.load_work(lora[64:128, :], A["rwkv_a_up_2"][l])
        self.load_work(g_up, A["rwkv_g_up_2"][l])
        masks_T, low = self.take(LEVELS * P), self.take(P)
        self.load_work(masks_T, A["const_halves_T"])
        self.load_work(low, A["const_halves"][:, 0:P])
        vt = self.take(T * GW).rearrange("p (t n) -> p t n", t=T)
        gt = self.take(T * GW).rearrange("p (t n) -> p t n", t=T)
        col = lambda a, c: a[:, c:c + 1]
        over = lambda a: a.unsqueeze(2).broadcast_to([P, 4, S])
        p, d = pf[:, 16:30, :], pf[:, 0:14, :]
        dve.did(nc.vector.tensor_tensor(d[:, :, 1:S], p[:, :, 0:S - 1], p[:, :, 1:S], ALU.subtract))
        dve.seq(nc.vector.tensor_scalar(d[:, :, 0:1], p[:, :, 0:1], -1.0, None, ALU.mult))
        for c in range(14):
            dve.did(nc.vector.scalar_tensor_tensor(p[:, c, :], d[:, c, :], col(q_["rwkv_mu_2"], c), p[:, c, :], ALU.mult, ALU.add))
        dve.wait(dve.now())
        r, k, v, wa, gd = pf[:, 16:20, :], pf[:, 20:24, :], pf[:, 24:28, :], pf[:, 28, :], pf[:, 29, :]
        lw, a, kk, L = pf[:, 0:4, :], pf[:, 4:8, :], pf[:, 8:12, :], pf[:, 12:16, :]
        act.wait(dve.now())
        act.did(nc.scalar.activation(wa[0:64, :], wa[0:64, :], ACT.Tanh))
        act.seq(nc.scalar.activation(gd, gd, ACT.Sigmoid))
        self.work_landed()
        self.meet()
        if l == 1:
            vd = self.take(4 * 32).rearrange("p (c n) -> p c n", c=4)
            vu, low_v, mix = self.take(GW), self.take(S), self.take(S)
            self.load_work(vd, A["rwkv_v_down_2"][0].rearrange("(c p) n -> p c n", p=P))
            self.load_work(vu[0:32, :], A["rwkv_v_up_2"][0])
            self.work_landed()
            for c in range(4):
                ins = nc.tensor.matmul(self.ps[2][0:32, 0:S], vd[:, c, :], v[:, c, :], start=(c == 0), stop=(c == 3))
            act.wait(pe.did(ins))
            pe.wait(act.did(nc.scalar.activation(low_v[0:32, :], self.ps[2][0:32, 0:S], ACT.Copy)))
            for c in range(4):
                pe.wait(act.now())
                act.wait(pe.did(nc.tensor.matmul(self.ps[3][:, 0:S], vu[0:32, c * P:(c + 1) * P], low_v[0:32, :], start=True, stop=True)))
                act.wait(dve.now())
                dve.wait(act.did(nc.scalar.activation(mix, self.ps[3][:, 0:S], ACT.Sigmoid, bias=col(q_["v0"], c))))
                vf = self.v_first[:, c * S:(c + 1) * S]
                dve.seq(nc.vector.tensor_tensor(vf, vf, v[:, c, :], ALU.subtract))
                dve.seq(nc.vector.tensor_tensor(vf, vf, mix, ALU.mult))
                dve.seq(nc.vector.tensor_tensor(v[:, c, :], v[:, c, :], vf, ALU.add))
        else:
            dve.seq(nc.vector.tensor_copy(self.v_first, v.rearrange("p c s -> p (c s)")))
        pe.wait(act.now())
        for c in range(4):
            b = self.ps[4 + c]
            b2 = self.ps[c]
            nc.tensor.matmul(b[:, 0:S], lora[0:64, c * P:(c + 1) * P], wa[0:64, :], start=True, stop=True)
            act.wait(pe.did(nc.tensor.matmul(b2[:, 0:S], lora[64:128, c * P:(c + 1) * P], wa[64:128, :], start=True, stop=True)))
            act.did(nc.scalar.activation(lw[:, c, :], b[:, 0:S], ACT.Sigmoid, bias=col(q_["rwkv_w0_2"], c)))
            act.did(nc.scalar.activation(a[:, c, :], b2[:, 0:S], ACT.Sigmoid, bias=col(q_["rwkv_a0_2"], c)))
            dve.did(nc.vector.tensor_scalar(kk[:, c, :], k[:, c, :], col(q_["rwkv_k_k_2"], c), None, ALU.mult))
        pe.wait(act.now())
        for t in range(T):
            act.wait(pe.did(nc.tensor.matmul(self.ps[t][:, :], gd[:, t * P:(t + 1) * P], g_up, start=True, stop=True)))
            act.did(nc.scalar.activation(gt[:, t, :], self.ps[t][:, :], ACT.Copy))
        self.meet()
        f3 = lambda x: x.rearrange("p c s -> p (c s)")
        dve.did(nc.vector.tensor_scalar(lw, lw, -DECAY_SCALE, None, ALU.mult))
        before_sq = self.work_at, self.spare_at
        sq = self.take(4 * S)
        act.seq(nc.scalar.activation(sq, f3(kk), ACT.Square))
        pe.wait(act.now())
        for g in range(2):
            m = pe.did(nc.tensor.matmul(self.ps[2 + g][:, :], self.c("pair_ones"), sq[:, g * 512:(g + 1) * 512], start=True, stop=True))
            act.wait(m)
        for g in range(2):
            act.did(nc.scalar.activation(sq[:, g * 512:(g + 1) * 512], self.ps[2 + g][:, :], ACT.Sqrt))
        dve.wait(act.now())
        dve.seq(nc.vector.tensor_scalar(sq, sq, 1e-12, None, ALU.max))
        dve.seq(nc.vector.reciprocal(sq, sq))
        dve.seq(nc.vector.tensor_tensor(f3(kk), f3(kk), sq, ALU.mult))
        for c in range(4):
            dve.did(nc.vector.tensor_scalar(sq[:, c * S:(c + 1) * S], a[:, c, :], 1.0, col(q_["rwkv_k_a_2"], c), ALU.subtract, ALU.mult))
        dve.wait(dve.now())
        dve.seq(nc.vector.scalar_tensor_tensor(f3(k), sq, 1.0, f3(k), ALU.add, ALU.mult))
        dve.seq(nc.vector.tensor_tensor(sq, f3(r), f3(k), ALU.mult))
        for c in range(4):
            dve.did(nc.vector.tensor_scalar(sq[:, c * S:(c + 1) * S], sq[:, c * S:(c + 1) * S], col(q_["rwkv_r_k_2"], c), None, ALU.mult))
        bonus = self.take(T * H2).rearrange("p (t h) -> p t h", t=T)
        pe.wait(dve.now())
        for t in range(T):
            for c in range(4):
                ins = nc.tensor.matmul(self.ps[2][:, t * H2 + 2 * c:t * H2 + 2 * c + 2], sq[:, c * S + t * P:c * S + (t + 1) * P],
                                       self.c("pair_pick"), start=True, stop=True)
        dve.wait(pe.did(ins))
        dve.seq(nc.vector.tensor_copy(bonus, self.ps[2][:, 0:T * H2].rearrange("p (t h) -> p t h", t=T)))
        dve.seq(nc.vector.tensor_tensor(f3(a), f3(a), f3(kk), ALU.mult))
        self.cumulate(f3(L), f3(lw), P)
        L4 = f3(L).rearrange("p (n s) -> p n s", s=P)
        ends = self.rowstat[:, 32:64].rearrange("p (k n) -> p k n", k=4)
        dve.did(nc.vector.tensor_copy(ends[:, 0, :].unsqueeze(2), L4[:, :, P // 2 - 1:P // 2]))
        dve.seq(nc.vector.tensor_copy(ends[:, 1, :].unsqueeze(2), L4[:, :, P - 1:P]))
        dve.seq(nc.vector.tensor_tensor(L4, L4, ends[:, 0, :].unsqueeze(2).broadcast_to([P, 8, P]), ALU.subtract))
        mid = ends[:, 0, :].rearrange("p (c t) -> p c t", t=T)
        end = ends[:, 1, :].rearrange("p (c t) -> p c t", t=T)
        fac = ends[:, 2, 0:4].unsqueeze(2)
        dve.seq(nc.vector.tensor_tensor(fac, end[:, :, 0:1], mid[:, :, 0:1], ALU.subtract))
        dve.seq(nc.vector.tensor_tensor(fac, fac, mid[:, :, 1:2], ALU.add))
        act.wait(dve.now())
        act.seq(nc.scalar.activation(ends[:, 2, 0:4], ends[:, 2, 0:4], ACT.Exp))
        self.meet()
        for t in range(T):
            for c in range(4):
                ins = nc.tensor.transpose(self.ps[2 + t][:, c * P:(c + 1) * P], v[:, c, t * P:(t + 1) * P], self.c("ident"))
            act.wait(pe.did(ins))
            act.did(nc.scalar.activation(vt[:, t, :], self.ps[2 + t][:, :], ACT.Copy))
        self.meet()
        self.work_at, self.spare_at = before_sq
        bonus2 = self.take(T * H2).rearrange("p (t h) -> p t h", t=T)
        dve.seq(nc.vector.tensor_copy(bonus2, bonus))
        eP, eN = self.take(S), self.take(S)
        kr = self.take(2 * S).rearrange("p (t k s) -> p t k s", t=T, k=2)
        bt, kt = self.take(S), self.take(S)
        units = [(e, t) for t in range(T) for e in range(2)]
        M4 = [self.take(512) for _ in units]
        TT = [self.take(2 * P) for _ in units]
        AmT = self.take(4 * P)
        Y = [self.take(P) for _ in units]
        RU = [self.take(2 * HD2) for _ in units]
        bk = self.take(2 * P)
        S1 = self.take(HD2)
        vs = self.take(T * P).rearrange("p (t n) -> p t n", t=T)
        with self.loop(4, ("pe", "act", "dve", "pool"), **self.per["rwkv"]) as j:
            self.meet()
            Lj = self.pair(L, j)
            act.did(nc.scalar.activation(eP, Lj, ACT.Exp))
            act.did(nc.scalar.activation(eN, Lj, ACT.Exp, scale=-1.0))
            act.did(nc.scalar.activation(vs, vt[:, :, ds(j * P, P)], ACT.Copy))
            tmp = AmT[:, 0:S]
            dve.seq(nc.vector.tensor_tensor(tmp, Lj, self.pair(lw, j), ALU.subtract))
            act.wait(dve.now())
            act.seq(nc.scalar.activation(tmp, tmp, ACT.Exp))
            dve.wait(act.now())
            t3 = lambda x: x.rearrange("p (t s) -> p t s", t=T)
            dve.did(nc.vector.tensor_tensor(kr[:, :, 0, :], t3(tmp), t3(self.pair(kk, j)), ALU.mult))
            dve.did(nc.vector.tensor_tensor(kr[:, :, 1, :], t3(eP), t3(self.pair(r, j)), ALU.mult))
            dve.did(nc.vector.tensor_tensor(bt, eN, self.pair(a, j), ALU.mult))
            dve.did(nc.vector.tensor_tensor(kt, eN, self.pair(k, j), ALU.mult))
            pe.wait(dve.now(), act.now())
            dve.wait(dve.now())
            for n, (e, t) in enumerate(units):
                h, tok = slice(e * HD2, (e + 1) * HD2), slice(t * P, (t + 1) * P)
                b = self.ps[4 + n]
                rhs = kr[h, t, :, :].rearrange("p k s -> p (k s)")
                nc.tensor.matmul(b[:, 0:S], bt[h, tok], rhs, start=True, stop=True)
                m = pe.did(nc.tensor.matmul(b[:, S:2 * S], kt[h, tok], rhs, start=True, stop=True))
                m2 = pe.did(nc.tensor.matmul(self.ps[n][:, 0:P], kr[h, t, 0, :], bt[h, tok], start=True, stop=True))
                dve.wait(m)
                v4 = lambda x: x.rearrange("p (g k s) -> p g k s", g=2, k=2)
                dve.did(nc.vector.tensor_tensor(v4(M4[n])[:, :, 0, :], v4(b[:, :])[:, :, 0, :],
                                                self.c("before_T").unsqueeze(1).broadcast_to([P, 2, P]), ALU.mult))
                dve.did(nc.vector.tensor_tensor(v4(M4[n])[:, :, 1, :], v4(b[:, :])[:, :, 1, :],
                                                self.c("upto_T").unsqueeze(1).broadcast_to([P, 2, P]), ALU.mult))
                dve.wait(m2)
                dve.did(nc.vector.tensor_tensor(TT[n][:, 0:P], self.ps[n][:, 0:P], low, ALU.mult))
                dve.wait(dve.now())
                dve.did(nc.vector.tensor_tensor(TT[n][:, P:2 * P], M4[n][:, 0:P], masks_T[:, 0:P], ALU.mult))
                dve.wait(dve.now())
                dve.did(nc.vector.tensor_tensor(TT[n][:, :].rearrange("p (k s) -> p k s", k=2),
                                                self.c("ident").unsqueeze(1).broadcast_to([P, 2, P]),
                                                TT[n][:, :].rearrange("p (k s) -> p k s", k=2), ALU.subtract))
            pe.wait(dve.now())
            nc.tensor.transpose(self.ps[0][:, P:2 * P], bt[:, 0:P], self.c("ident"))
            m = pe.did(nc.tensor.transpose(self.ps[0][:, 2 * P:3 * P], kt[:, 0:P], self.c("ident")))
            dve.wait(m)
            dve.did(nc.vector.tensor_copy(bk, self.ps[0][:, P:3 * P]))
            dve.wait(dve.now())
            for lev in range(1, LEVELS):
                marks, ys = [], []
                for n in range(4):
                    am = AmT[:, n * P:(n + 1) * P]
                    if lev > 1:
                        dve.wait(am_read[n])
                    marks.append(dve.did(nc.vector.tensor_tensor(am, M4[n][:, 0:P], masks_T[:, lev * P:(lev + 1) * P], ALU.mult)))
                am_read = []
                for n in range(4):
                    pe.wait(marks[n])
                    am_read.append(pe.did(nc.tensor.matmul(self.ps[n][:, 0:P], AmT[:, n * P:(n + 1) * P], TT[n][:, 0:P], start=True, stop=True)))
                    act.wait(am_read[n])
                    ys.append(act.did(nc.scalar.activation(Y[n], self.ps[n][:, 0:P], ACT.Copy)))
                last = lev == LEVELS - 1
                for n in range(4):
                    b = self.ps[4 + n]
                    pe.wait(ys[n])
                    if not last:
                        nc.tensor.matmul(b[:, 0:P], TT[n][:, P:2 * P], Y[n], start=True, stop=True)
                    dve.wait(pe.did(nc.tensor.matmul(b[:, P:2 * P], Y[n], TT[n][:, P:2 * P], start=True, stop=True)))
                    lo = P if last else 0
                    dve.did(nc.vector.tensor_tensor(TT[n][:, lo:2 * P], TT[n][:, lo:2 * P], b[:, lo:2 * P], ALU.subtract))
                    pe.wait(dve.now())
                dve.wait(dve.now())
            for n, (e, t) in enumerate(units):
                h = slice(e * HD2, (e + 1) * HD2)
                vj = vs[:, t, e * HD2:(e + 1) * HD2]
                b = self.ps[n]
                nc.tensor.matmul(b[:, 0:HD2], M4[n][:, S:S + P], vj, start=True, stop=(t == 0))
                if t:
                    nc.tensor.matmul(b[:, 0:HD2], kr[h, 1, 0, :], S1[h, :], start=False, stop=True)
                dve.wait(pe.did(nc.tensor.matmul(self.ps[4 + n][:, 0:HD2], M4[n][:, S + P:2 * S], vj, start=True, stop=False)))
                pe.wait(dve.did(nc.vector.tensor_scalar(RU[n][:, 0:HD2], b[:, 0:HD2], -1.0, None, ALU.mult)))
                dve.wait(pe.did(nc.tensor.matmul(b[:, HD2:2 * HD2], TT[n][:, P:2 * P], RU[n][:, 0:HD2], start=True, stop=True)))
                pe.wait(dve.did(nc.vector.tensor_copy(RU[n][:, HD2:2 * HD2], b[:, HD2:2 * HD2])))
                U = RU[n][:, HD2:2 * HD2]
                y = self.ps[4 + n][:, 0:HD2]
                if t:
                    nc.tensor.matmul(y, kr[h, 1, 1, :], S1[h, :], start=False, stop=False)
                act.wait(pe.did(nc.tensor.matmul(y, M4[n][:, P:2 * P], U, start=False, stop=True)))
                act.did(nc.scalar.activation(self.mixed[:, t, ds(j * 2 * HD2 + (3 * GW + e * HD2), HD2)], y, ACT.Copy))
                if t == 0:
                    s_ = b[h, 2 * HD2:3 * HD2]
                    nc.tensor.matmul(s_, bk[:, e * HD2:(e + 1) * HD2], U, start=True, stop=False)
                    dve.wait(pe.did(nc.tensor.matmul(s_, bk[:, P + e * HD2:P + (e + 1) * HD2], vj, start=False, stop=True)))
                    pe.wait(dve.did(nc.vector.tensor_scalar(S1[h, :], s_, ends[h, 2, ds(j, 1)], None, ALU.mult)))
        self.meet()
        row_w, row_b = M4[0], M4[1]
        self.work_ld.count(nc.scalar.dma_start(row_w, A["rwkv_ln_w_2"][l].partition_broadcast(P)))
        self.work_ld.count(nc.scalar.dma_start(row_b, A["rwkv_ln_b_2"][l].partition_broadcast(P)))
        self.work_landed()
        tmp = M4[2].rearrange("p (n d) -> p n d", d=HD2)
        st = self.rowstat[:, 4:4 + H2]
        over = lambda x: x.unsqueeze(2).broadcast_to([P, H2, HD2])
        for t in range(T):
            y2 = self.mixed[:, t, 3 * GW:4 * GW]
            y = y2.rearrange("p (n d) -> p n d", d=HD2)
            v8 = vt[:, t, :].rearrange("p (n d) -> p n d", d=HD2)
            dve.seq(nc.vector.tensor_reduce(st, y, AX.X, ALU.add))
            dve.seq(nc.vector.tensor_scalar(st, st, 1.0 / HD2, None, ALU.mult))
            dve.seq(nc.vector.tensor_tensor(y, y, over(st), ALU.subtract))
            dve.seq(nc.vector.tensor_tensor(tmp, y, y, ALU.mult))
            dve.seq(nc.vector.tensor_reduce(st, tmp, AX.X, ALU.add))
            self.inv_rms(st, H2, HD2, LN_EPS)
            dve.seq(nc.vector.tensor_tensor(y, y, over(st), ALU.mult))
            dve.seq(nc.vector.tensor_tensor(y2, y2, row_w, ALU.mult))
            dve.seq(nc.vector.tensor_tensor(y2, y2, row_b, ALU.add))
            dve.seq(nc.vector.tensor_tensor(tmp, v8, over(bonus2[:, t, :]), ALU.mult))
            dve.seq(nc.vector.tensor_tensor(y, y, tmp, ALU.add))
            dve.seq(nc.vector.tensor_tensor(y2, y2, gt[:, t, :], ALU.mult))
        self.meet()

    def finish(self):
        nc = self.nc
        for q in (self.pe, self.act, self.dve, self.pool):
            nc.sync.wait_ge(*q.now())
        for t in range(T):
            self.outs.count(nc.sync.dma_start(self.out_dram[0, t * P:(t + 1) * P, :], self.x[:, t, :]))
        nc.sync.wait_ge(*self.outs.now())


def build(nc, A, consts, out):
    Program(nc, A, consts, out).build()


_INS = ['x', 'mem', 'norm_gain', 'mem_norm_gain', 'mem_w_kv', 'mem_qk_gain', 'w_out', 'even_w_in', 'nsa_qk_gain',
        'nsa_cmp_pos', 'nsa_cmp_w1', 'nsa_cmp_w2', 'diff_qk_gain', 'diff_lambda', 'diff_subln_gain', 'odd_w_in',
        'dsa_qk_gain', 'w_in_2', 'w_out_2', 'norm_pre_mix_2', 'norm_post_mix_2', 'norm_pre_ffn_2', 'norm_post_ffn_2',
        'w_ffn_gate_2', 'w_ffn_up_2', 'w_ffn_down_2', 'hgrn_lb_logits_2', 'hgrn_norm_w_2', 'mlstm_conv_w_2',
        'mlstm_conv_b_2', 'mlstm_i_bias_2', 'mlstm_f_bias_2', 'mlstm_norm_w_2', 'rwkv_mu_2', 'rwkv_w0_2',
        'rwkv_w_up_2', 'rwkv_a0_2', 'rwkv_a_up_2', 'rwkv_g_up_2', 'rwkv_k_k_2', 'rwkv_k_a_2', 'rwkv_r_k_2',
        'rwkv_ln_w_2', 'rwkv_ln_b_2', 'rwkv_v0_2', 'rwkv_v_down_2', 'rwkv_v_up_2']


def kernel(**inputs):
    import numpy as _np
    import concourse.bacc as _bacc
    from concourse import mybir as _mybir
    from concourse.bass_utils import run_bass_kernel_spmd as _run

    nc = _bacc.Bacc("TRN2", target_bir_lowering=False, num_devices=1, dynamic_dma_scratch_size=1024)
    small, offs, halves_T, halves, decay = shape_constants()
    arrays, A = {}, {}
    tables = dict(const_small=small, const_halves_T=halves_T, const_halves=halves, const_decay=decay)
    for name, a in [(n, inputs[n]) for n in _INS] + list(tables.items()):
        a = _np.ascontiguousarray(a)
        arrays[f"in_{name}_dram"] = a
        A[name] = nc.dram_tensor(f"in_{name}_dram", a.shape, _mybir.dt.from_np(a.dtype), kind="ExternalInput").ap()
    out = nc.dram_tensor("out_0_dram", (1, S, D), _mybir.dt.float32, kind="ExternalOutput").ap()
    build(nc, A, dict(small=small, offs=offs), out)
    r = _run(nc, [arrays], core_ids=[0])
    return r.results[0]["out_0_dram"]
```

```python
import concourse.bass as bass
from concourse import mybir
from contextlib import ExitStack, contextmanager
import math
import numpy as np

F32 = mybir.dt.float32
F32R = mybir.dt.float32r
ALU = mybir.AluOpType
ACT = mybir.ActivationFunctionType
AX = mybir.AxisListType
ds = bass.ds

P = 128
S = 256
T = S // P
D = 2048
KC = D // P
TILE = 512
UNIT = 2
AHEAD = 3
SLOTS = 4
EPS = 1e-6
BIG = 1e30

EVEN = dict(a_q=0, a_kv=1024, a_g=2560, a_z=2584, b_q=3608, b_k=4120, b_v=4632, b_z=5144, m_q=5656, m_z=6168)
EVEN_IN = 6680
ODD = dict(c_q=0, c_k=1536, c_v=2048, i_q=2560, i_k=3584, i_w=3648, c_z=3664, m_q=5200, m_z=5712)
ODD_IN = 6224
HD = 128
CMP_LEN, CMP_STRIDE, CMP_HID = 32, 16, 256
NCMP = (S - CMP_LEN) // CMP_STRIDE + 1
TOPK = S // 4
DEPTH = 4
LAMBDA_INIT = 0.8 - 0.6 * math.exp(0.0)

GW, H2, HD2 = 512, 8, 64
N_IN = 7952
D_FF = 5632
LEVELS = 7
DECAY_SCALE = 0.6065306597126334
LN_EPS = 64e-5
WORK = 6650
FIXED = 1128
SPARE = 2 * KC * S


def shape_constants():
    t = np.arange(S)
    p = np.arange(P)
    parts = {}

    def put(name, a):
        full = np.zeros((P, a.shape[1]), np.float32)
        full[:a.shape[0]] = a
        parts[name] = full

    def rope_tables(pos, half):
        inv = (np.float32(10000.0) ** (-np.arange(half, dtype=np.float32) / np.float32(half))).astype(np.float32)
        ang = pos.astype(np.float32)[:, None] * inv[None, :]
        return np.cos(ang).astype(np.float32), np.sin(ang).astype(np.float32)

    def by_tile(a):
        return a.reshape(T, P, -1).transpose(1, 0, 2).reshape(P, -1)

    put("ident", np.eye(P, dtype=np.float32))
    future = (p[None, :] > p[:, None]).astype(np.float32)
    put("causal", np.concatenate([np.zeros((P, P)), future * BIG], 1))
    put("zeros", np.zeros((P, S)))
    put("ones", np.ones((P, P)))
    put("pair_ones", np.kron(np.eye(2), np.ones((HD2, HD2))))
    put("pair_pick", np.kron(np.eye(2), np.ones((HD2, 1))))
    for d in (HD, HD2):
        c, s = rope_tables(t, d // 2)
        put(f"cos{d}", by_tile(c))
        put(f"sin{d}", by_tile(s))
    last = np.arange(NCMP) * CMP_STRIDE + CMP_LEN - 1
    c, s = rope_tables(np.tile(last, 2), HD // 2)
    put("cos_cmp", c)
    put("sin_cmp", s)
    for g in range(2):
        for tt in range(T):
            ok = np.zeros((P, 2 * NCMP), np.float32)
            ok[:, g * NCMP:(g + 1) * NCMP] = last[None, :] <= (tt * P + p)[:, None]
            put(f"cmp_keep{g}{tt}", ok)
            put(f"cmp_drop{g}{tt}", (1 - ok) * BIG)
    put("upto_T", (p[:, None] <= p[None, :]).astype(np.float32))
    put("before_T", (p[:, None] < p[None, :]).astype(np.float32))
    offs, at = {}, 0
    for n, a in parts.items():
        offs[n] = (at, a.shape[1])
        at += a.shape[1]
    small = np.concatenate(list(parts.values()), 1).astype(np.float32)

    half = [((p[:, None] // (2 * b) == p[None, :] // (2 * b)) & (p[:, None] % (2 * b) < b) & (p[None, :] % (2 * b) >= b))
            .astype(np.float32) for b in (1 << np.arange(LEVELS))]
    halves_T = np.concatenate(half, 1)
    halves = np.concatenate([h.T for h in half], 1)
    lg = np.log1p(-np.exp2(-5.0 - np.arange(H2)))
    rel = p[None, :] - p[:, None]
    dec = [[np.exp(lg[h] * np.maximum(rel + off, 0)) * (rel + off >= 0) * HD2 ** -0.5 for off in (0, P)] for h in range(H2)]
    decay = np.concatenate([np.concatenate(d2, 1) for d2 in dec], 1).astype(np.float32)
    return small, offs, halves_T.astype(np.float32), halves.astype(np.float32), decay


class Counter:

    def __init__(self, sem, step=1):
        self.sem, self.step, self.base, self.k = sem, step, 0, 0

    def count(self, ins):
        ins.then_inc(self.sem, self.step)
        self.k += 1
        return self.now()

    def now(self, back=0):
        return (self.sem, self.base + (self.k - back) * self.step)


class Queue(Counter):

    def __init__(self, eng, sem):
        super().__init__(sem)
        self.eng = eng

    def wait(self, *marks):
        for sem, value in marks:
            self.eng.wait_ge(sem, value)

    def did(self, ins):
        return self.count(ins)

    def hold(self, passed):
        self.eng.sem_inc(passed, 1)

    def seq(self, ins):
        m = self.count(ins)
        self.wait(m)
        return m


class Program:
    def __init__(self, nc, A, consts, out):
        self.nc, self.A, self.C, self.out_dram = nc, A, consts, out

    def build(self):
        nc = self.nc
        with ExitStack() as ctx:
            def sem(name):
                return ctx.enter_context(nc.semaphore(name))

            at = [(nc.sbuf_base + 31) // 32 * 32]

            def sb(name, shape, dtype=F32, offset=None):
                if offset is None:
                    offset = at[0]
                    at[0] += (int(np.prod(shape[1:])) * 4 + 31) // 32 * 32
                return nc.alloc_sbuf_tensor_at(name, shape, dtype, offset=offset)

            self.pe = Queue(nc.tensor, sem("pe_done"))
            self.act = Queue(nc.scalar, sem("act_done"))
            self.dve = Queue(nc.vector, sem("dve_done"))
            self.pool = Queue(nc.gpsimd, sem("pool_done"))
            self.full = [Counter(sem(f"slot_full{i}"), 16) for i in range(SLOTS)]
            self.ready = [Counter(sem(f"unit_split{i}")) for i in range(SLOTS)]
            self.used = [Counter(sem(f"unit_used{i}")) for i in range(SLOTS)]
            self.emptied = [Counter(sem(f"bank_emptied{b}")) for b in range(8)]
            self.open = []
            self.small = Counter(sem("small_loads"), 16)
            self.work_ld = Counter(sem("work_loads"), 16)
            self.passed = sem("passed")
            self.outs = Counter(sem("out_stores"), 16)
            self.counters = dict(pe=self.pe, act=self.act, dve=self.dve, pool=self.pool)
            for i in range(SLOTS):
                self.counters[f"full{i}"] = self.full[i]
                self.counters[f"ready{i}"] = self.ready[i]
                self.counters[f"used{i}"] = self.used[i]
            for b in range(8):
                self.counters[f"emptied{b}"] = self.emptied[b]

            self.x = sb("x_residual", [P, T, D])
            mixed_at = at[0]
            self.mixed = sb("mixed", [P, T, D])
            spare_at = at[0]
            self.hT = (sb("h_high", [P, KC, S], F32R), sb("h_low", [P, KC, S], F32R))
            self.raw = [sb(f"weights{i}", [P, UNIT, TILE]) for i in range(SLOTS)]
            self.w_high = [sb(f"weights_high{i}", [P, UNIT, TILE], F32R) for i in range(SLOTS)]
            self.w_low = [sb(f"weights_low{i}", [P, UNIT, TILE], F32R) for i in range(SLOTS)]
            self.const = sb("const", [P, self.C["small"].shape[1]])
            self.params = sb("params", [P, 2250])
            self.params_at = 0
            self.fixed = sb("fixed", [P, FIXED])
            self.fixed_at = 0
            proj_at = at[0]
            self.proj = sb("proj", [P, 16384])
            self.work = sb("work", [P, WORK])
            self.spare = sb("spare", [P, SPARE], offset=spare_at)
            ff = D_FF // P
            self.actT = (sb("act_high", [P, ff, S], F32R, offset=proj_at),
                         sb("act_low", [P, ff, S], F32R, offset=proj_at + ff * S * 4))
            assert proj_at + 2 * ff * S * 4 <= at[0] <= nc.sbuf_usable_end
            self.ff_small = sb("ff_small", [P, T * D], offset=mixed_at)
            self.work_at = self.spare_at = self.work_fixed = 0
            self.ps = [ctx.enter_context(nc.psum_tensor(f"bank{b}", [P, 512], F32)) for b in range(8)]

            for c in self.ready + self.used + self.emptied:
                nc.sync.sem_inc(c.sem, 1)
                c.base = 1
            self.load_params()
            self.main()
            self.finish()

    def c(self, name):
        at, w = self.C["offs"][name]
        return self.const[:, at:at + w]

    def take(self, cols):
        if self.work_at + cols <= WORK:
            self.work_at += cols
            return self.work[:, self.work_at - cols:self.work_at]
        return self.take_spare(cols)

    def take_spare(self, cols):
        self.spare_at += cols
        assert self.spare_at <= SPARE, self.spare_at
        return self.spare[:, self.spare_at - cols:self.spare_at]

    @contextmanager
    def loop(self, n, engines, **per):
        nc = self.nc
        kinds = dict(pe=mybir.EngineType.PE, act=mybir.EngineType.Activation, dve=mybir.EngineType.DVE,
                     pool=mybir.EngineType.Pool, sp=mybir.EngineType.SP)
        old = {k: (c.base, c.k) for k, c in self.counters.items()}
        with nc.Fori(0, n, engines=[kinds[e] for e in engines]) as i:
            for k, c in self.counters.items():
                if per.get(k):
                    c.base, c.k = c.base + c.k * c.step + i * (per[k] * c.step), 0
                else:
                    c.base, c.k = c.base + c.k * c.step, 0
            yield i
            made = {k: c.k for k, c in self.counters.items() if c.k}
            assert made == {k: v for k, v in per.items() if v}, f"a turn makes {made}"
        for k, c in self.counters.items():
            c.base, c.k = old[k][0], old[k][1] + n * per.get(k, 0)

    def meet(self, names=("pe", "act", "dve", "pool")):
        qs = [self.counters[n] for n in names]
        marks = [q.now() for q in qs] + self.open
        self.open = []
        for q in qs:
            q.wait(*marks)

    def param(self, dram_row, width):
        dst = self.params[:, self.params_at:self.params_at + width]
        self.params_at += width
        self.small.count(self.nc.scalar.dma_start(dst, dram_row.partition_broadcast(P)))
        return dst

    def param_cols(self, dram_vec, chunks):
        dst = self.params[:, self.params_at:self.params_at + chunks]
        self.params_at += chunks
        with self.nc.allow_non_contiguous_dma(reason="a few thousand parameters"):
            self.small.count(self.nc.scalar.dma_start(dst, dram_vec.rearrange("(c p) -> p c", p=P)))
        return dst

    def split_unit(self, st, u):
        nc, act, dve = self.nc, self.act, self.dve
        i, w = (st["slot0"] + u) % SLOTS, st["width"]
        raw, high, low = [a[i][:, :, 0:w] for a in (self.raw, self.w_high, self.w_low)]
        nc.sync.wait_ge(*self.ready[i].now())
        nc.sync.sem_inc(self.passed, 1)
        self.full[i].count(nc.sync.dma_start(raw, st["W"][u, :, :, ds(st["col"], w)]))
        act.wait(self.full[i].now(), self.used[i].now())
        dve.wait(act.did(nc.scalar.activation(high, raw, ACT.Copy)))
        self.ready[i].count(nc.vector.tensor_tensor(low, raw, high.bitcast(F32), ALU.subtract))

    def split_first(self, st):
        for u in range(AHEAD):
            self.split_unit(st, u)

    def run_step(self, st, after=None):
        nc, pe = self.nc, self.pe
        AT, w, units, banks = st["AT"], st["width"], st["units"], st["banks"]
        marks = []
        for u in range(units):
            i = (st["slot0"] + u) % SLOTS
            if u >= AHEAD:
                self.split_unit(st, u)
            pe.wait(self.ready[i].now())
            for n, b in enumerate(banks):
                if u == 0:
                    pe.wait(self.emptied[b].now())
                for c in range(UNIT):
                    k = u * UNIT + c
                    for x, y in ((0, 0), (1, 0), (0, 1)):
                        wt = (self.w_high, self.w_low)[y][i]
                        if st["kind"] == "tokens":
                            out, l, r = self.ps[b][:, 0:w], AT[x][:, k, n * P:(n + 1) * P], wt[:, c, 0:w]
                        else:
                            out, l, r = self.ps[b][:, 0:S], wt[:, c, n * P:(n + 1) * P], AT[x][:, k, :]
                        ins = nc.tensor.matmul(out, l, r, start=(k == 0 and x + y == 0),
                                               stop=(k == units * UNIT - 1 and y == 1))
                if u == units - 1 and n < len(banks) - 1:
                    marks.append(pe.did(ins))
            released = self.used[i].count(ins)
        marks.append(released)
        if after is not None:
            self.split_first(after)
        for n, b in enumerate(banks):
            st["evac"](n, b, marks[n])

    def copy_out(self, dst):
        def evac(n, b, mark):
            d = dst(n)
            w = d.shape[-1]
            self.act.wait(mark)
            self.emptied[b].count(self.nc.scalar.activation(d, self.ps[b][:, 0:w], ACT.Copy))
        return evac

    def tokens(self, AT, Wu, units, col, width, dst, slot0=0):
        return dict(kind="tokens", slot0=slot0, AT=AT, W=Wu, units=units, col=col, width=width, banks=range(T), evac=self.copy_out(dst))

    def features(self, AT, Wu, units, col, chunks, dst, bank0=0, evac=None):
        return dict(kind="features", slot0=0, AT=AT, W=Wu, units=units, col=col, width=chunks * P,
                    banks=range(bank0, bank0 + chunks), evac=evac or self.copy_out(dst))

    def units_of(self, W):
        return W.rearrange("(u c p) n -> u p c n", c=UNIT, p=P)

    def run_steps(self, make, n, rest=(), **more):
        first = make(0) if n else rest
        self.split_first(first[0])
        tail = list(rest)
        if n > 1:
            per = {k: v for k, v in more.items()}
            for s in first:
                for u in range(s["slot0"], s["slot0"] + s["units"]):
                    for k in ("full", "ready", "used"):
                        per[f"{k}{u % SLOTS}"] = per.get(f"{k}{u % SLOTS}", 0) + 1
                per["act"] = per.get("act", 0) + s["units"]
                per["pe"] = per.get("pe", 0) + len(s["banks"]) - 1
                for b in s["banks"]:
                    per[f"emptied{b}"] = per.get(f"emptied{b}", 0) + 1
            with self.loop(n - 1, ("pe", "act", "dve", "sp"), **per) as i:
                steps = make(i)
                for s, after in zip(steps, steps[1:] + [make(i + 1)[0]]):
                    self.run_step(s, after)
        if n:
            tail = make(n - 1) + tail
        for s, after in zip(tail, tail[1:] + [None]):
            self.run_step(s, after)
        self.open += [self.emptied[b].now() for b in range(8)]

    def project_tokens(self, AT, W, rows, col0, n, dst):
        units, Wu = rows // (UNIT * P), self.units_of(W)
        whole, rest = n // TILE, n % TILE
        last = [self.tokens(AT, Wu, units, col0 + whole * TILE, rest, lambda t: dst[:, t, whole * TILE:n])] if rest else []
        k = 1 if units % SLOTS == 0 else 2
        assert whole % k == 0 and k * units % SLOTS == 0
        step = lambda i, s: self.tokens(AT, Wu, units, i * (k * TILE) + (col0 + s * TILE), TILE,
                                        lambda t: dst[:, t, ds(i * (k * TILE) + s * TILE, TILE)], s * units % SLOTS)
        self.run_steps(lambda i: [step(i, s) for s in range(k)], whole // k, last)
        return [self.emptied[t].now() for t in range(T)]

    def transpose_split(self, src, gain=None):
        nc, pe, act, dve = self.nc, self.pe, self.act, self.dve
        ident = self.c("ident")
        high, low = self.hT
        free = {}
        for k, c in enumerate(range(0, KC, 2)):
            b = 2 + k % 4
            if b in free:
                pe.wait(free[b])
            for j in range(2):
                for t in range(T):
                    ins = nc.tensor.transpose(self.ps[b][:, (j * T + t) * P:(j * T + t + 1) * P],
                                              src[:, t, (c + j) * P:(c + j + 1) * P], ident)
            act.wait(pe.did(ins))
            if gain is None:
                o, v = [a[:, c:c + 2, :] for a in (high, low)], self.ps[b][:, :].rearrange("p (c s) -> p c s", c=2)
                dve.wait(act.did(nc.scalar.activation(o[0], v, ACT.Copy)))
                free[b] = dve.did(nc.vector.tensor_tensor(o[1], v, o[0].bitcast(F32), ALU.subtract))
                continue
            for j in range(2):
                m = act.did(nc.scalar.activation(high[:, c + j, :], self.ps[b][:, j * S:(j + 1) * S], ACT.Copy,
                                                 scale=gain[:, c + j:c + j + 1]))
            dve.wait(m)
            for j in range(2):
                free[b] = dve.did(nc.vector.scalar_tensor_tensor(
                    low[:, c + j, :], self.ps[b][:, j * S:(j + 1) * S], gain[:, c + j:c + j + 1],
                    high[:, c + j, :].bitcast(F32), ALU.mult, ALU.subtract))

    def transpose_tokens(self, src, dst, gain=None):
        nc, pe, act, dve = self.nc, self.pe, self.act, self.dve
        n = src.shape[2] // P
        free = {}
        ident = self.c("ident")
        done = []
        for k, c in enumerate(range(0, n, 2)):
            b = 2 + k % 4
            cc = min(2, n - c)
            if b in free:
                pe.wait(free[b])
            for j in range(cc):
                for t in range(T):
                    ins = nc.tensor.transpose(self.ps[b][:, (j * T + t) * P:(j * T + t + 1) * P],
                                              src[:, t, (c + j) * P:(c + j + 1) * P], ident)
            m = pe.did(ins)
            q = act if k % 2 else dve
            q.wait(m)
            if gain is None:
                o, i_ = dst[:, c:c + cc, :], self.ps[b][:, 0:cc * S].rearrange("p (c s) -> p c s", c=cc)
                ins = nc.scalar.activation(o, i_, ACT.Copy) if q is act else nc.vector.tensor_copy(o, i_)
                free[b] = q.did(ins)
            else:
                for j in range(cc):
                    o, i_, g = dst[:, c + j, :], self.ps[b][:, j * S:(j + 1) * S], gain[:, c + j:c + j + 1]
                    ins = (nc.scalar.activation(o, i_, ACT.Copy, scale=g) if q is act
                           else nc.vector.tensor_scalar(o, i_, g, None, ALU.mult))
                    free[b] = q.did(ins)
            done.append(free[b])
        return done

    def inv_rms(self, ss, width, n, eps=EPS):
        nc, dve, pool = self.nc, self.dve, self.pool
        m = dve.did(nc.vector.tensor_scalar(ss, ss, 1.0 / n, eps, ALU.mult, ALU.add))
        pool.wait(m)
        mh = self.minus_half[0:ss.shape[0], 0:ss.shape[1]]
        m = pool.did(nc.gpsimd.tensor_tensor(ss, ss, mh, ALU.pow))
        dve.wait(m)

    def norm_to_hT(self, src, gain):
        nc, act, dve = self.nc, self.act, self.dve
        ss = self.rowstat[:, 0:T]
        for t in range(T):
            m = act.did(nc.scalar.activation(self.mixed[:, t, :], src[:, t, :], ACT.Square, accum_out=ss[:, t:t + 1]))
        dve.wait(m)
        self.inv_rms(ss, T, D)
        act.wait(self.pool.now())
        m = act.did(nc.scalar.activation(self.mixed[:, 0, :], src[:, 0, :], ACT.Copy, scale=ss[:, 0:1]))
        self.pe.wait(m, dve.did(nc.vector.tensor_scalar(self.mixed[:, 1, :], src[:, 1, :], ss[:, 1:2], None, ALU.mult)))
        self.transpose_split(self.mixed, gain)
        self.meet()

    def head_norm(self, src, tmp, heads, d, gain, rows=P):
        nc, dve = self.nc, self.dve
        ss = self.rowstat[0:rows, 4:4 + heads]
        dve.seq(nc.vector.tensor_tensor(tmp, src, src, ALU.mult))
        dve.seq(nc.vector.tensor_reduce(ss, tmp, AX.X, ALU.add))
        self.inv_rms(ss, heads, d)
        dve.seq(nc.vector.tensor_tensor(tmp, src, ss.unsqueeze(2).broadcast_to([rows, heads, d]), ALU.mult))
        if gain is not None:
            dve.seq(nc.vector.tensor_tensor(tmp, tmp, gain[0:rows].unsqueeze(1).broadcast_to([rows, heads, d]), ALU.mult))

    def rope(self, src, dst, heads, d, cos, sin, rows=P):
        nc, dve = self.nc, self.dve
        h = d // 2
        cb = cos.unsqueeze(1).broadcast_to([rows, heads, h])
        sb_ = sin.unsqueeze(1).broadcast_to([rows, heads, h])
        x1, x2, o1, o2 = src[:, :, 0:h], src[:, :, h:d], dst[:, :, 0:h], dst[:, :, h:d]
        tmp = self.rope_tmp[0:rows, 0:heads * h].rearrange("p (n d) -> p n d", n=heads)
        dve.did(nc.vector.tensor_tensor(o1, x1, cb, ALU.mult))
        dve.seq(nc.vector.tensor_tensor(tmp, x2, sb_, ALU.mult))
        dve.did(nc.vector.tensor_tensor(o1, o1, tmp, ALU.subtract))
        dve.seq(nc.vector.tensor_tensor(o2, x2, cb, ALU.mult))
        dve.seq(nc.vector.tensor_tensor(tmp, x1, sb_, ALU.mult))
        return dve.seq(nc.vector.tensor_tensor(o2, o2, tmp, ALU.add))

    def prep(self, groups):
        nc, act, dve, pool = self.nc, self.act, self.dve, self.pool
        room = self.mixed[:, :, :].rearrange("p t n -> p (t n)")
        width = max(heads * d for _, heads, d, _, _, _ in groups)
        by_head = lambda a, d: a.rearrange("p (n d) -> p n d", d=d)
        at, stats, read = 0, [], []
        for view, heads, d, gain, norm, rope in groups:
            for t in range(T):
                stats.append(None)
                if not norm:
                    continue
                n = len(read)
                buf = room[:, (n % 2) * width:(n % 2) * width + heads * d]
                if n >= 2:
                    act.wait(read[n - 2])
                dve.wait(act.did(nc.scalar.activation(by_head(buf, d), view(t), ACT.Square, scale=float(d) ** -0.5)))
                stats[-1] = self.prep_stats[:, at:at + heads]
                read.append(dve.did(nc.vector.tensor_reduce(stats[-1], by_head(buf, d), AX.X, ALU.add)))
                at += heads
        dve.wait(dve.now())
        step = self.minus_half.shape[1]
        for k in range(0, at, step):
            self.inv_rms(self.prep_stats[:, k:min(at, k + step)], min(at, k + step) - k, 1)
        for g, (view, heads, d, gain, norm, rope) in enumerate(groups):
            h = d // 2
            todo = []
            for t in range(T):
                x, ss = view(t), stats[g * T + t]
                x1, x2 = x[:, :, 0:h], x[:, :, h:d]
                t1, t2 = [by_head(room[:, i * width // 2:i * width // 2 + heads * h], h) for i in (2 * t, 2 * t + 1)]
                cos, sin = [self.c(f"{f}{d}")[:, t * h:(t + 1) * h].unsqueeze(1).broadcast_to([P, heads, h]) for f in ("cos", "sin")]
                steps = []
                if norm:
                    steps.append((x, x, ss.unsqueeze(2).broadcast_to([P, heads, d]), ALU.mult))
                if gain is not None:
                    steps.append((x, x, gain.unsqueeze(1).broadcast_to([P, heads, d]), ALU.mult))
                if rope:
                    steps += [(t1, x1, sin, ALU.mult), (t2, x2, sin, ALU.mult), (x1, x1, cos, ALU.mult), (x2, x2, cos, ALU.mult),
                              (x1, x1, t2, ALU.subtract), (x2, x2, t1, ALU.add)]
                todo.append(steps)
            marks = [dve.now()] * T
            for pairs in zip(*todo):
                for t, (o, a, b, op) in enumerate(pairs):
                    dve.wait(marks[t])
                    marks[t] = dve.did(nc.vector.tensor_tensor(o, a, b, op))
        dve.wait(dve.now())
        return dve.now()

    def attention(self, units):
        nc, pe, act, dve = self.nc, self.pe, self.act, self.dve
        R = 2
        n = len(units)
        st = [dict() for _ in units]

        def scores(i):
            u, s = units[i], st[i]
            bank = s["bank"] = self.ps[(1, 2, 3)[i % 3]]
            s["ps"] = bank[:, 0:u["keys"]]
            if i >= 3:
                pe.wait(st[i - 3]["masked"])
            s["scored"] = pe.did(nc.tensor.matmul(s["ps"], u["qT"], u["kT"], start=True, stop=True))
            if u.get("mlstm"):
                for c, g in enumerate(u["gates"]):
                    s["scored"] = pe.did(nc.tensor.matmul(bank[:, S + c * P:S + (c + 1) * P],
                                                          g.broadcast_to([P, P]), self.c("ident"), start=True, stop=True))

        def soften(i):
            u, s = units[i], st[i]
            k, j = u["keys"], i % DEPTH
            s["e"] = self.sm_e[:, j * S:j * S + k]
            stat = self.sm_stat[:, 4 * j:4 * j + 4]
            dve.wait(s["scored"])
            if i >= DEPTH:
                dve.wait(st[i - DEPTH]["exp"], st[i - DEPTH]["out"])
            if u.get("mlstm"):
                return weigh_mlstm(i, u, s, k, j)
            dve.hold(self.passed)
            s["masked"] = dve.did(nc.vector.tensor_tensor_reduce(
                out=self.sm_s[:, j * S:j * S + k], in0=s["ps"], in1=u["mask"], scale=1.0, scalar=3e38,
                op0=ALU.add, op1=ALU.min, accum_out=stat[:, 0:1]))
            act.wait(s["masked"])
            if i >= DEPTH:
                act.wait(st[i - DEPTH]["flipped"])
            s["exp"] = act.did(nc.scalar.activation(s["e"], self.sm_s[:, j * S:j * S + k], ACT.Exp,
                                                    bias=stat[:, 0:1], scale=-1.0, accum_out=stat[:, 1:2]))

        def finish(i):
            u, s = units[i], st[i]
            k, j = u["keys"], i % DEPTH
            dve.wait(s["exp"])
            if u.get("mlstm"):
                return finish_mlstm(i, u, s, k, j)
            stat = self.sm_stat[:, 4 * j:4 * j + 4]
            if u.get("keep") is not None:
                dve.hold(self.passed)
                s["exp"] = dve.seq(nc.vector.tensor_tensor_reduce(
                    out=s["e"], in0=s["e"], in1=u["keep"], scale=1.0, scalar=0.0,
                    op0=ALU.mult, op1=ALU.add, accum_out=stat[:, 1:2]))
                dve.seq(nc.vector.tensor_scalar(stat[:, 1:2], stat[:, 1:2], 1e-30, None, ALU.max))
            s["recip"] = dve.did(nc.vector.reciprocal(stat[:, 3:4], stat[:, 1:2]))
            s["r"] = stat[:, 3:4]

        def weigh_mlstm(i, u, s, k, j):
            G = s["bank"][:, S:S + k]
            stat = self.sm_stat[:, 8 * j:8 * j + 8]
            M, neg, m, floor = [stat[:, c:c + 1] for c in range(4)]
            buf = self.sm_s[:, j * S:j * S + k]
            dve.hold(self.passed)
            dve.seq(nc.vector.tensor_tensor_reduce(out=buf, in0=G, in1=u["mask"], scale=1.0, scalar=0.0,
                                                   op0=ALU.subtract, op1=ALU.max, accum_out=M))
            dve.did(nc.vector.tensor_scalar(neg, M, -1.0, None, ALU.mult))
            act.wait(dve.did(nc.vector.tensor_tensor(m, M, u["F"], ALU.add)))
            act.did(nc.scalar.activation(buf, buf, ACT.Exp, bias=neg))
            s["exp"] = act.did(nc.scalar.activation(floor, m, ACT.Exp, scale=-1.0))

        def finish_mlstm(i, u, s, k, j):
            stat = self.sm_stat[:, 8 * j:8 * j + 8]
            floor, den, recip = [stat[:, c:c + 1] for c in range(3, 6)]
            buf = self.sm_s[:, j * S:j * S + k]
            if i >= DEPTH:
                dve.wait(st[i - DEPTH]["flipped"])
            dve.hold(self.passed)
            s["masked"] = s["exp"] = dve.seq(nc.vector.tensor_tensor_reduce(
                out=s["e"], in0=s["ps"], in1=buf, scale=HD2 ** -0.5, scalar=0.0, op0=ALU.mult, op1=ALU.add, accum_out=den))
            dve.seq(nc.vector.scalar_tensor_tensor(floor, den, -1.0, floor, ALU.mult, ALU.max))
            dve.seq(nc.vector.tensor_tensor(den, den, floor, ALU.max))
            s["recip"] = dve.did(nc.vector.reciprocal(recip, den))
            s["r"] = recip

        def flip(i):
            u, s = units[i], st[i]
            k = u["keys"]
            kt = -(-k // P)
            bank = self.ps[4 + i % R]
            pe.wait(s["exp"])
            if i >= R:
                pe.wait(st[i - R]["eT"])
            for c in range(kt):
                w = min(P, k - c * P)
                ins = nc.tensor.transpose(bank[0:w, c * P:(c + 1) * P], s["e"][:, c * P:c * P + w], self.c("ident"))
            s["flipped"] = pe.did(ins)
            q = act if i % 2 else dve
            q.wait(s["flipped"])
            if i >= R:
                q.wait(st[i - R]["mixed"])
            w = min(P, k)
            s["eT_buf"] = self.sm_eT[0:w, (i % R) * S:(i % R) * S + kt * P]
            ins = (nc.scalar.activation(s["eT_buf"], bank[0:w, 0:kt * P], ACT.Copy) if q is act
                   else nc.vector.tensor_copy(s["eT_buf"], bank[0:w, 0:kt * P]))
            s["eT"] = q.did(ins)

        def mix(i):
            u, s = units[i], st[i]
            kt = -(-u["keys"] // P)
            o = self.ps[6 + i % R][:, 0:u["dv"]]
            pe.wait(s["eT"])
            if i >= R:
                pe.wait(st[i - R]["out"])
            for c in range(kt):
                ins = nc.tensor.matmul(o, s["eT_buf"][:, c * P:(c + 1) * P], u["v"][c], start=(c == 0), stop=(c == kt - 1))
            s["mixed"] = pe.did(ins)
            dve.wait(s["mixed"], s["recip"])
            s["out"] = u["out"](o, s["r"])

        for w in range(n + 3):
            if w < n:
                scores(w)
                soften(w)
            if 0 <= w - 1 < n:
                finish(w - 1)
            if 0 <= w - 2 < n:
                flip(w - 2)
            if 0 <= w - 3 < n:
                mix(w - 3)

    def stage_q(self, src, d, dst):
        nc, pe, act = self.nc, self.pe, self.act
        w = src.shape[2]
        q = self.q_stage[:, 0:T * w].rearrange("p (t d) -> p t d", t=T)
        m = act.did(nc.scalar.activation(q, src, ACT.Copy))
        pe.wait(m)
        pe.hold(self.passed)
        heads = w // d
        for k, h0 in enumerate(range(0, heads, 2)):
            n = min(2, heads - h0)
            bank = self.ps[(0, 4)[k]]
            for h in range(n):
                for t in range(T):
                    ins = nc.tensor.transpose(bank[0:d, (h * T + t) * P:(h * T + t + 1) * P],
                                              q[:, t, (h0 + h) * d:(h0 + h + 1) * d], self.c("ident"))
            m = pe.did(ins)
            act.wait(m)
            m = act.did(nc.scalar.activation(dst[:, h0 * S:(h0 + n) * S], bank[0:d, 0:n * S], ACT.Copy))
        pe.wait(m)

    def causal(self, t):
        return self.c("causal")[:, P:2 * P] if t == 0 else self.c("causal")

    def scaled(self, out, O, r):
        return self.dve.did(self.nc.vector.tensor_scalar(out, O, r, None, ALU.mult))

    def gate_with_silu(self, z, out):
        nc, act, dve = self.nc, self.act, self.dve
        for t in range(T):
            m = act.did(nc.scalar.activation(z[:, t, :], z[:, t, :], ACT.Silu))
            dve.wait(m)
            m = dve.did(nc.vector.tensor_tensor(out[:, t, :], out[:, t, :], z[:, t, :], ALU.mult))

    def project_out(self, W):
        nc, dve, pe = self.nc, self.dve, self.pe
        self.meet()
        self.transpose_split(self.mixed)
        self.meet()
        dve.wait(*self.project_tokens(self.hT, W, D, 0, D, self.mixed))
        for t in range(T):
            dve.did(nc.vector.tensor_tensor(self.x[:, t, :], self.x[:, t, :], self.mixed[:, t, :], ALU.add))
        self.meet()

    def load_params(self):
        nc, A = self.nc, self.A
        self.rowstat = self.take_fixed(64)
        self.minus_half = self.take_fixed(32)
        self.small.count(nc.scalar.dma_start(self.const[:, :], A["const_small"]))
        for t in range(T):
            self.small.count(nc.scalar.dma_start(self.x[:, t, :], A["x"][0, t * P:(t + 1) * P, :]))
        self.g_norm = [self.param_cols(A["norm_gain"][i], KC) for i in range(2)]
        self.g_mem = self.param_cols(A["mem_norm_gain"], KC)
        self.g_memqk = [[self.param(A["mem_qk_gain"][i, j], HD) for j in range(2)] for i in range(2)]
        self.g_nsa = [self.param(A["nsa_qk_gain"][0, j], HD) for j in range(4)]
        self.g_diff = [self.param(A["diff_qk_gain"][0, j], HD2) for j in range(2)]
        self.g_subln = self.param(A["diff_subln_gain"][0], HD)
        self.g_dsa = [self.param(A["dsa_qk_gain"][0, j], HD) for j in range(2)]
        self.lam = self.param(A["diff_lambda"][0].rearrange("a b -> (a b)"), 4 * HD2)
        self.second_params()
        nc.gpsimd.memset(self.minus_half[:, :], -0.5).then_inc(self.pool.sem, 1)
        self.pool.k += 1
        self.params_landed = self.small.now()
        for q in (self.pe, self.act, self.dve, self.pool):
            q.wait(self.params_landed)
        dve = self.dve
        for g, d in ((self.g_nsa[0], HD), (self.g_dsa[0], HD), (self.g_diff[0], HD2),
                     (self.g_memqk[0][0], HD), (self.g_memqk[1][0], HD)):
            dve.seq(nc.vector.tensor_scalar(g, g, -float(d) ** -0.5, None, ALU.mult))
        self.meet()

    def take_fixed(self, cols):
        self.fixed_at += cols
        assert self.fixed_at <= FIXED
        return self.fixed[:, self.fixed_at - cols:self.fixed_at]

    def fresh_work(self):
        self.meet()
        self.work_at, self.spare_at = self.work_fixed, 0

    def attention_buffers(self):
        self.prep_tmp = self.take(4 * HD)
        self.rope_tmp = self.take(HD)
        self.prep_stats = self.take(64)
        self.sm_s = self.take_spare(DEPTH * S)
        self.sm_e = self.take_spare(DEPTH * S)
        self.sm_eT = self.take_spare(2 * S)
        self.sm_stat = self.take_spare(4 * DEPTH)
        self.q_stage = self.take_spare(T * 3 * P)
        self.qT = self.take_spare(3 * S)
        self.q2 = self.take_spare(4 * S)

    def first_block(self):
        nc, A, pe, act, dve, pool = self.nc, self.A, self.pe, self.act, self.dve, self.pool
        self.mkv = [self.proj[:, 8192 * i:8192 * i + 2048].rearrange("p (t n) -> p t n", t=T) for i in range(2)]
        self.memkT = [self.proj[:, 14336 + i * 4 * S:14336 + (i + 1) * 4 * S] for i in range(2)]
        self.memv = [self.take(T * 512) for i in range(2)]
        self.work_fixed = self.work_at
        for t in range(T):
            m = self.work_ld.count(nc.scalar.dma_start(self.proj[:, t * D:(t + 1) * D], A["mem"][0, t * P:(t + 1) * P, :]))
        act.wait(m)
        dve.wait(m)
        self.norm_to_hT(self.proj[:, 0:T * D].rearrange("p (t n) -> p t n", t=T), self.g_mem)
        self.attention_buffers()
        for i in range(2):
            kv = self.mkv[i]
            dve.wait(*self.project_tokens(self.hT, A["mem_w_kv"][i], D, 0, 1024, kv))
            self.prep([(lambda t: kv[:, t, 0:512].rearrange("p (n d) -> p n d", d=HD), 4, HD, self.g_memqk[i][1], True, False)])
            for t in range(T):
                m = dve.did(nc.vector.tensor_copy(self.memv[i][:, t * 512:(t + 1) * 512], kv[:, t, 512:1024]))
            self.meet()
            self.transpose_tokens(kv[:, :, 0:512], self.memkT[i].rearrange("p (c s) -> p c s", c=4))
            self.meet()
        self.even_layer()
        self.odd_layer()
        self.meet()

    def memory_heads(self, i, pr, q_col, out_col):
        nc = self.nc
        mv = self.memv[i].rearrange("p (t n) -> p t n", t=T)
        kT = self.memkT[i].rearrange("p (h s) -> p h s", h=4)
        with self.loop(2, ("pe", "act", "dve", "pool"), **self.per["mem"]) as j:
            self.meet()
            self.stage_q(pr[:, :, ds(j * 2 * HD + q_col, 2 * HD)], HD, self.qT)
            self.attention([dict(qT=self.qT[:, (e * T + t) * P:(e * T + t + 1) * P], keys=S, dv=HD, mask=self.c("zeros"),
                                 kT=kT[:, ds(j * 2 + e, 1), :].rearrange("p a s -> p (a s)"),
                                 v=[mv[:, c, ds(j * 2 * HD + e * HD, HD)] for c in range(T)],
                                 out=lambda O, r, t=t, e=e: self.scaled(
                                     self.mixed[:, t, ds(j * 2 * HD + (e * HD + out_col), HD)], O, r))
                            for e in range(2) for t in range(T)])
        self.meet()

    per = dict(mem=dict(pe=13, act=8, dve=14),
               nsa=dict(pe=37, act=20, dve=62), diff=dict(pe=28, act=18, dve=32), dsa=dict(pe=20, act=12, dve=21),
               idx=dict(pe=10, act=11, dve=8), ret=dict(pe=8, act=6, dve=8), mlstm=dict(pe=36, act=22, dve=70), rwkv=dict(pe=141, act=69, dve=89, pool=8))

    def even_layer(self):
        nc, A, pe, act, dve, pool = self.nc, self.A, self.pe, self.act, self.dve, self.pool
        E = EVEN
        self.fresh_work()
        self.attention_buffers()
        self.norm_to_hT(self.x, self.g_norm[0])
        pr = self.proj[:, 0:T * EVEN_IN].rearrange("p (t n) -> p t n", t=T)
        kvT = self.take_spare(4 * S).rearrange("p (c s) -> p c s", c=4)
        rawT = self.take_spare(S)
        blkT = self.take_spare(CMP_LEN * 2 * NCMP).rearrange("p (l g c) -> p l g c", l=CMP_LEN, g=2)
        peT = self.take(CMP_LEN)
        pe_rows = self.take(HD)
        hid = self.take(CMP_HID)
        hidT = self.take(2 * 2 * NCMP)
        kc = self.take(HD)
        kcT = self.take(2 * NCMP)
        vc = self.take(HD)
        w2 = [self.take(2 * HD).rearrange("p (c n) -> p c n", c=2) for _ in range(2)]
        pos = [pe_rows, self.take(HD)]
        for j in range(2):
            m = self.work_ld.count(nc.scalar.dma_start(w2[j], A["nsa_cmp_w2"][0, j].rearrange("(c p) n -> p c n", p=P)))
            m = self.work_ld.count(nc.scalar.dma_start(pos[j][0:CMP_LEN, :], A["nsa_cmp_pos"][0, j]))
        pe.wait(m)

        dve.wait(*self.project_tokens(self.hT, A["even_w_in"][0], D, 0, EVEN_IN, pr))
        heads = lambda col, n, d: (lambda t: pr[:, t, col:col + n * d].rearrange("p (n d) -> p n d", d=d))
        self.meet()
        act.seq(nc.scalar.activation(pr[:, :, E["a_g"]:E["a_z"]], pr[:, :, E["a_g"]:E["a_z"]], ACT.Sigmoid))

        w1 = [A["nsa_cmp_w1"][0, j].rearrange("(u l p) n -> u p l n", l=4, p=P) for j in range(2)]
        slot_read = {}

        def compress(j):
            pe.seq(nc.tensor.transpose(self.ps[2][:, 0:CMP_LEN], pos[j][0:CMP_LEN, :], self.c("ident")[0:CMP_LEN, 0:CMP_LEN]))
            dve.wait(pe.now())
            dve.seq(nc.vector.tensor_copy(peT, self.ps[2][:, 0:CMP_LEN]))
            for g in range(2):
                col = E["a_kv"] + j * 256 + g * HD
                if g:
                    pe.wait(dve.now())
                for t in range(T):
                    ins = nc.tensor.transpose(self.ps[3][:, t * P:(t + 1) * P], pr[:, t, col:col + HD], self.c("ident"))
                dve.wait(pe.did(ins))
                dve.seq(nc.vector.tensor_copy(rawT, self.ps[3][:, 0:S]))
                win = bass.AP(rawT.tensor, rawT.offset, [rawT.ap[0], [1, CMP_LEN], [CMP_STRIDE, NCMP]])
                dve.seq(nc.vector.tensor_tensor(blkT[:, :, g, :], win, peT.unsqueeze(2).broadcast_to([P, CMP_LEN, NCMP]), ALU.add))
            pe.wait(dve.now())
            for u in range(8):
                i = u % SLOTS
                nc.sync.wait_ge(*self.ready[i].now())
                if u >= SLOTS:
                    nc.sync.wait_ge(*slot_read[i])
                wv = self.raw[i][:, :, :].rearrange("p c n -> p (c n)").rearrange("p (l n) -> p l n", l=4)
                self.full[i].count(nc.sync.dma_start(wv, w1[j][u]))
                pe.wait(self.full[i].now())
                for l in range(4):
                    k = u * 4 + l
                    ins = nc.tensor.matmul(self.ps[4][0:2 * NCMP, 0:CMP_HID], blkT[:, k, :, :].rearrange("p g c -> p (g c)"), wv[:, l, :],
                                           start=(k == 0), stop=(k == CMP_LEN - 1))
                slot_read[i] = released = pe.did(ins)
            nc.sync.wait_ge(*released)
            return released

        def compressed(j, released):
            act.wait(released)
            act.seq(nc.scalar.activation(hid[0:2 * NCMP, :], self.ps[4][0:2 * NCMP, 0:CMP_HID], ACT.Silu))
            pe.wait(act.now())
            for c in range(2):
                ins = nc.tensor.transpose(self.ps[5][:, c * 2 * NCMP:(c + 1) * 2 * NCMP], hid[0:2 * NCMP, c * P:(c + 1) * P],
                                          self.c("ident")[0:2 * NCMP, 0:2 * NCMP])
            dve.wait(pe.did(ins))
            dve.seq(nc.vector.tensor_copy(hidT, self.ps[5][:, 0:4 * NCMP]))
            pe.wait(dve.now())
            for c in range(2):
                ins = nc.tensor.matmul(self.ps[6][0:2 * NCMP, 0:HD], hidT[:, c * 2 * NCMP:(c + 1) * 2 * NCMP], w2[j][:, c, :],
                                       start=(c == 0), stop=(c == 1))
            dve.wait(pe.did(ins))
            if j == 1:
                dve.seq(nc.vector.tensor_copy(vc[0:2 * NCMP, :], self.ps[6][0:2 * NCMP, 0:HD]))
            else:
                R2 = 2 * NCMP
                three = lambda a: a[0:R2, :].rearrange("p (n d) -> p n d", n=1)
                dve.seq(nc.vector.tensor_copy(kc[0:R2, :], self.ps[6][0:R2, 0:HD]))
                tmp = self.prep_tmp[:, 0:HD]
                self.head_norm(three(kc), three(tmp), 1, HD, self.g_nsa[1], rows=R2)
                self.rope(three(tmp), three(kc), 1, HD, self.c("cos_cmp")[0:R2], self.c("sin_cmp")[0:R2], rows=R2)
                pe.wait(dve.now())
                pe.seq(nc.tensor.transpose(self.ps[7][:, 0:R2], kc[0:R2, :], self.c("ident")[0:R2, 0:R2]))
                dve.wait(pe.now())
                dve.seq(nc.vector.tensor_copy(kcT, self.ps[7][:, 0:R2]))
            self.meet()

        released = compress(0)
        self.prep([(heads(E["a_q"], 8, HD), 8, HD, self.g_nsa[0], True, True),
                   (heads(E["a_kv"] + 2 * 256, 2, HD), 2, HD, self.g_nsa[2], True, True),
                   (heads(E["a_kv"] + 4 * 256, 2, HD), 2, HD, self.g_nsa[3], True, True)])
        compressed(0, released)
        released = compress(1)
        self.prep([(heads(E["b_q"], 8, HD2), 8, HD2, self.g_diff[0], True, True),
                   (heads(E["b_k"], 8, HD2), 8, HD2, self.g_diff[1], True, True),
                   (heads(E["m_q"], 4, HD), 4, HD, self.g_memqk[0][0], True, False)])
        compressed(1, released)
        self.meet()

        self.transpose_tokens(pr[:, :, E["a_kv"] + 512:E["a_kv"] + 768], kvT[:, 0:2, :])
        self.meet()
        self.transpose_tokens(pr[:, :, E["a_kv"] + 1024:E["a_kv"] + 1280], kvT[:, 2:4, :])
        self.meet()
        gates = pr[:, :, E["a_g"]:E["a_z"]]
        for g in range(2):
            with self.loop(2, ("pe", "act", "dve", "pool"), **self.per["nsa"]) as j:
                self.meet()
                self.stage_q(pr[:, :, ds(j * 2 * HD + g * 4 * HD, 2 * HD)], HD, self.qT)
                units = []
                for e in range(2):
                    for t in range(T):
                        for b in range(3):
                            def out(O, rc, e=e, t=t, b=b):
                                dst = self.mixed[:, t, ds(j * 2 * HD + (g * 4 + e) * HD, HD)]
                                gate = gates[:, t, ds(j * 6 + (g * 12 + e * 3 + b), 1)]
                                dve.seq(nc.vector.tensor_tensor(self.coef, rc, gate, ALU.mult))
                                if b == 0:
                                    return dve.seq(nc.vector.tensor_scalar(dst, O, self.coef, None, ALU.mult))
                                return dve.seq(nc.vector.scalar_tensor_tensor(dst, O, self.coef, dst, ALU.mult, ALU.add))
                            u = dict(qT=self.qT[:, (e * T + t) * P:(e * T + t + 1) * P], dv=HD, out=out)
                            if b == 0:
                                u.update(kT=kcT, keys=2 * NCMP, mask=self.c(f"cmp_drop{g}{t}"), keep=self.c(f"cmp_keep{g}{t}"),
                                         v=[vc[0:2 * NCMP, :]])
                            else:
                                vcol = E["a_kv"] + (3 if b == 1 else 5) * 256 + g * HD
                                u.update(kT=kvT[:, 2 * (b - 1) + g, 0:(t + 1) * P], keys=(t + 1) * P, mask=self.causal(t),
                                         v=[pr[:, c, vcol:vcol + HD] for c in range(t + 1)])
                            units.append(u)
                self.attention(units)
            self.meet()

        lam, lt = self.rowstat[:, 20:24], self.prep_tmp
        for j in range(2):
            dve.seq(nc.vector.tensor_tensor(lt[:, 0:HD2], self.lam[:, 2 * j * HD2:(2 * j + 1) * HD2],
                                            self.lam[:, (2 * j + 1) * HD2:(2 * j + 2) * HD2], ALU.mult))
            dve.seq(nc.vector.tensor_reduce(lam[:, j:j + 1], lt[:, 0:HD2], AX.X, ALU.add))
        act.wait(dve.now())
        act.seq(nc.scalar.activation(lam[:, 0:2], lam[:, 0:2], ACT.Exp))
        dve.wait(act.now())
        dve.seq(nc.vector.tensor_tensor(lam[:, 2:3], lam[:, 1:2], lam[:, 0:1], ALU.subtract))
        dve.seq(nc.vector.tensor_scalar(lam[:, 2:3], lam[:, 2:3], LAMBDA_INIT, None, ALU.subtract))
        kT2 = kvT.rearrange("p c s -> p (c s)")
        self.meet()
        with self.loop(2, ("pe", "act", "dve", "pool"), **self.per["diff"]) as j:
            self.meet()
            self.stage_q(pr[:, :, ds(j * 2 * HD + E["b_q"], 2 * HD)], HD2, self.q2[0:HD2, :])
            self.stage_q(pr[:, :, ds(j * 2 * HD + E["b_k"], 2 * HD)], HD2, kT2[0:HD2, :])
            units = []
            for e in range(2):
                for t in range(T):
                    for c in range(2):
                        def out(O, rc, e=e, t=t, c=c):
                            dst = self.mixed[:, t, ds(j * 2 * HD + (e * HD + 1024), HD)]
                            if c == 0:
                                return dve.seq(nc.vector.tensor_scalar(dst, O, rc, None, ALU.mult))
                            dve.seq(nc.vector.tensor_tensor(self.coef, rc, lam[:, 2:3], ALU.mult))
                            return dve.seq(nc.vector.scalar_tensor_tensor(dst, O, self.coef, dst, ALU.mult, ALU.add))
                        at = (2 * e + c) * S
                        units.append(dict(qT=self.q2[0:HD2, at + t * P:at + (t + 1) * P], dv=HD, out=out,
                                          kT=kT2[0:HD2, at:at + (t + 1) * P], keys=(t + 1) * P, mask=self.causal(t),
                                          v=[pr[:, k, ds(j * 2 * HD + (e * HD + E["b_v"]), HD)] for k in range(t + 1)]))
            self.attention(units)
        self.meet()
        for t in range(T):
            o = self.mixed[:, t, 1024:1536].rearrange("p (n d) -> p n d", d=HD)
            tmp = self.prep_tmp[:, 0:512].rearrange("p (n d) -> p n d", d=HD)
            self.head_norm(o, tmp, 4, HD, self.g_subln)
            dve.seq(nc.vector.tensor_scalar(o, tmp, 1.0 - LAMBDA_INIT, None, ALU.mult))
        self.meet()
        self.memory_heads(0, pr, E["m_q"], 1536)
        self.gate_with_silu(pr[:, :, E["a_z"]:E["a_z"] + 1024], self.mixed[:, :, 0:1024])
        self.gate_with_silu(pr[:, :, E["b_z"]:E["b_z"] + 512], self.mixed[:, :, 1024:1536])
        self.gate_with_silu(pr[:, :, E["m_z"]:E["m_z"] + 512], self.mixed[:, :, 1536:2048])
        self.project_out(A["w_out"][0])

    def odd_layer(self):
        nc, A, pe, act, dve, pool = self.nc, self.A, self.pe, self.act, self.dve, self.pool
        O_ = ODD
        self.fresh_work()
        self.attention_buffers()
        self.norm_to_hT(self.x, self.g_norm[1])
        pr = self.proj[:, 0:T * ODD_IN].rearrange("p (t n) -> p t n", t=T)
        kT = self.take_spare(4 * S).rearrange("p (c s) -> p c s", c=4)
        kiT = self.take_spare(S)
        score = self.take_spare(T * S).rearrange("p (t s) -> p t s", t=T)
        drop = self.take_spare(T * S).rearrange("p (t s) -> p t s", t=T)
        rel = self.take_spare(T * S).rearrange("p (t s) -> p t s", t=T)
        best = self.take(8 * T)
        dve.wait(*self.project_tokens(self.hT, A["odd_w_in"][0], D, 0, ODD_IN, pr))
        heads = lambda col, n, d: (lambda t: pr[:, t, col:col + n * d].rearrange("p (n d) -> p n d", d=d))
        self.prep([(heads(O_["c_q"], 12, HD), 12, HD, self.g_dsa[0], True, True),
                   (heads(O_["c_k"], 4, HD), 4, HD, self.g_dsa[1], True, True),
                   (heads(O_["i_q"], 16, HD2), 16, HD2, None, False, True),
                   (heads(O_["i_k"], 1, HD2), 1, HD2, None, False, True),
                   (heads(O_["m_q"], 4, HD), 4, HD, self.g_memqk[1][0], True, False)])
        wi = pr[:, :, O_["i_w"]:O_["c_z"]]
        dve.seq(nc.vector.tensor_scalar(wi, wi, 16.0 ** -0.5 * 64.0 ** -0.5, None, ALU.mult))
        dve.seq(nc.vector.memset(score, 0.0))
        self.meet()
        self.transpose_tokens(pr[:, :, O_["c_k"]:O_["c_v"]], kT)
        self.meet()
        self.stage_q(pr[:, :, O_["i_k"]:O_["i_w"]], HD2, kiT[0:HD2, :])
        self.meet()
        with self.loop(4, ("pe", "act", "dve", "pool"), **self.per["idx"]) as j:
            self.meet()
            self.stage_q(pr[:, :, ds(j * 4 * HD2 + O_["i_q"], 4 * HD2)], HD2, self.q2[0:HD2, :])
            relued, added = [], []
            for h in range(4):
                for t in range(T):
                    k, n = (t + 1) * P, 2 * h + t
                    b = self.ps[(1, 2, 3, 5)[n % 4]]
                    buf = rel[:, n % 2, 0:k]
                    if n >= 4:
                        pe.wait(relued[n - 4])
                    act.wait(pe.did(nc.tensor.matmul(b[:, 0:k], self.q2[0:HD2, n * P:(n + 1) * P], kiT[0:HD2, 0:k],
                                                     start=True, stop=True)))
                    if n >= 2:
                        act.wait(added[n - 2])
                    relued.append(act.did(nc.scalar.activation(buf, b[:, 0:k], ACT.Relu)))
                    dve.wait(relued[n], *added[n - 2:n - 1])
                    added.append(dve.did(nc.vector.scalar_tensor_tensor(
                        score[:, t, 0:k], buf, pr[:, t, ds(j * 4 + (O_["i_w"] + h), 1)], score[:, t, 0:k], ALU.mult, ALU.add)))
        self.meet()
        TAKEN = -3e38
        for t in range(T):
            k = (t + 1) * P
            s_, m_ = score[:, t, 0:k], self.causal(t)
            dve.seq(nc.vector.tensor_tensor(s_, s_, m_, ALU.subtract))
        for rnd in range(TOPK // 8):
            for t in range(T):
                s_ = score[:, t, 0:(t + 1) * P]
                dve.did(nc.vector.max(best[:, 8 * t:8 * t + 8], s_))
            dve.wait(dve.now())
            for t in range(T):
                s_ = score[:, t, 0:(t + 1) * P]
                dve.did(nc.vector.match_replace(s_, best[:, 8 * t:8 * t + 8], s_, TAKEN))
            dve.wait(dve.now())
        for t in range(T):
            k = (t + 1) * P
            dve.seq(nc.vector.tensor_scalar(drop[:, t, 0:k], score[:, t, 0:k], -2e38, BIG, ALU.is_gt, ALU.mult))
            dve.seq(nc.vector.tensor_tensor(drop[:, t, 0:k], drop[:, t, 0:k], self.causal(t), ALU.add))
        with self.loop(4, ("pe", "act", "dve", "pool"), **self.per["dsa"]) as g:
            self.meet()
            self.stage_q(pr[:, :, ds(g * 3 * HD, 3 * HD)], HD, self.qT)
            self.attention([dict(qT=self.qT[:, (r * T + t) * P:(r * T + t + 1) * P], dv=HD, keys=(t + 1) * P,
                                 kT=kT[:, ds(g, 1), 0:(t + 1) * P].rearrange("p a s -> p (a s)"), mask=drop[:, t, 0:(t + 1) * P],
                                 v=[pr[:, c, ds(g * HD + O_["c_v"], HD)] for c in range(t + 1)],
                                 out=lambda O, rc, r=r, t=t: self.scaled(
                                     self.mixed[:, t, ds(g * 3 * HD + r * HD, HD)], O, rc))
                            for r in range(3) for t in range(T)])
        self.meet()
        self.memory_heads(1, pr, O_["m_q"], 1536)
        self.gate_with_silu(pr[:, :, O_["c_z"]:O_["c_z"] + 1536], self.mixed[:, :, 0:1536])
        self.gate_with_silu(pr[:, :, O_["m_z"]:O_["m_z"] + 512], self.mixed[:, :, 1536:2048])
        self.project_out(A["w_out"][1])

    def main(self):
        self.coef = self.take_fixed(1)
        self.first_block()
        self.second_block()

    def second_params(self):
        A = self.A
        self.b2 = []
        for l in range(2):
            q = {}
            for name, n in (("norm_pre_mix_2", KC), ("norm_pre_ffn_2", KC), ("rwkv_mu_2", 14), ("rwkv_w0_2", 4),
                            ("rwkv_a0_2", 4), ("rwkv_k_k_2", 4), ("rwkv_k_a_2", 4), ("rwkv_r_k_2", 4),
                            ("mlstm_conv_b_2", 8)):
                q[name] = self.param_cols(A[name][l], n)
            q["conv"] = [self.param_cols(A["mlstm_conv_w_2"][l, j], 8) for j in range(4)]
            q["lb"] = self.param_cols(A["hgrn_lb_logits_2"][l], 4)
            q["ib"] = self.param(A["mlstm_i_bias_2"][l], H2)
            q["fb"] = self.param(A["mlstm_f_bias_2"][l], H2)
            self.b2.append(q)
        self.b2[1]["v0"] = self.param_cols(A["rwkv_v0_2"][0], 4)

    def load_row(self, dram_row, width):
        dst = self.take(width)
        self.work_ld.count(self.nc.scalar.dma_start(dst, dram_row.partition_broadcast(P)))
        return dst

    def load_work(self, dst, src):
        self.work_ld.count(self.nc.scalar.dma_start(dst, src))

    def work_landed(self):
        for q in (self.pe, self.act, self.dve, self.pool):
            q.wait(self.work_ld.now())

    def second_block(self):
        self.v_first = self.take_fixed(4 * S)
        for l in range(2):
            self.second_layer(l)

    def second_layer(self, l):
        nc, A, pe, act, dve, pool = self.nc, self.A, self.pe, self.act, self.dve, self.pool
        self.meet()
        self.work_at = self.work_fixed = self.spare_at = 0
        q = self.b2[l]
        self.norm_to_hT(self.x, q["norm_pre_mix_2"])
        NT = 8 * GW + 2 * H2
        pt = self.proj[:, 0:T * NT].rearrange("p (t n) -> p t n", t=T)
        pf = self.proj[:, T * NT:T * NT + 30 * S].rearrange("p (c s) -> p c s", c=30)
        W = A["w_in_2"][l]
        Wu = self.units_of(W)
        self.run_steps(lambda i: [self.tokens(self.hT, Wu, 8, i * GW, GW, lambda t: pt[:, t, ds(i * GW, GW)])], 4)
        fm = lambda c0, i, w: (lambda j: pf[:, ds(i * w + (c0 + j), 1), :].rearrange("p a s -> p (a s)"))
        c0, rw = 4 * GW, 12 * GW + 2 * H2
        self.run_steps(lambda i: [
            self.features(self.hT, Wu, 8, i * 4 * GW + c0, 4, fm(0, i, 8)),
            self.features(self.hT, Wu, 8, i * 4 * GW + (c0 + GW), 4, fm(4, i, 8)),
            self.tokens(self.hT, Wu, 8, i * 4 * GW + (c0 + 2 * GW), GW, lambda t: pt[:, t, ds(i * 2 * GW + 4 * GW, GW)]),
            self.tokens(self.hT, Wu, 8, i * 4 * GW + (c0 + 3 * GW), GW, lambda t: pt[:, t, ds(i * 2 * GW + 5 * GW, GW)])], 2)
        self.run_steps(lambda i: [self.features(self.hT, Wu, 8, i * GW + rw, 4, fm(16, i, 4))], 3, [
            self.tokens(self.hT, Wu, 8, 12 * GW, 2 * H2, lambda t: pt[:, t, 8 * GW:NT]),
            self.features(self.hT, Wu, 8, rw + 3 * GW, 2, lambda j: pf[:, 28 + j, :])])
        self.meet()
        self.retention(l, pt)
        self.hgrn(l, pt, pf)
        self.mlstm(l, pt, pf)
        self.rwkv(l, pt, pf)
        self.work_at = self.work_fixed
        self.meet()
        self.transpose_split(self.mixed)
        self.meet()
        gain = self.load_row(A["norm_post_mix_2"][l], D)
        self.project_tokens(self.hT, A["w_out_2"][l], D, 0, D, self.mixed)
        self.meet()
        self.add_normed(self.mixed, gain)
        self.norm_to_hT(self.x, q["norm_pre_ffn_2"])
        gain = self.ff_small[:, 0:D]
        self.load_work(gain, A["norm_post_ffn_2"][l].partition_broadcast(P))
        gate = self.ff_small[:, D:D + 4 * S].rearrange("p (c s) -> p c s", c=4)
        prod = self.ff_small[:, D + 4 * S:D + 8 * S].rearrange("p (c s) -> p c s", c=4)
        Gu, Uu = self.units_of(A["w_ffn_gate_2"][l]), self.units_of(A["w_ffn_up_2"][l])

        def gate_and_up(i):

            def silu(j, b, mark):
                act.wait(mark, self.emptied[4 + j].now())
                self.emptied[b].count(nc.scalar.activation(gate[:, j, :], self.ps[b][:, 0:S], ACT.Silu))

            def times(j, b, mark):
                dve.wait(mark, self.emptied[j].now())
                self.emptied[b].count(nc.vector.tensor_tensor(prod[:, j, :], gate[:, j, :], self.ps[b][:, 0:S], ALU.mult))
                if j < 3:
                    return
                dst = [a[:, ds(i * 4, 4), :] for a in self.actT]
                act.wait(self.emptied[b].now())
                dve.wait(act.did(nc.scalar.activation(dst[0], prod, ACT.Copy)))
                dve.did(nc.vector.tensor_tensor(dst[1], prod, dst[0].bitcast(F32), ALU.subtract))
            return [self.features(self.hT, Gu, 8, i * TILE, 4, None, 0, silu),
                    self.features(self.hT, Uu, 8, i * TILE, 4, None, 4, times)]
        self.run_steps(gate_and_up, D_FF // TILE, act=1, dve=1)
        self.meet()
        down = self.spare[:, 0:T * D].rearrange("p (t n) -> p t n", t=T)
        self.project_tokens(self.actT, A["w_ffn_down_2"][l], D_FF, 0, D, down)
        self.meet()
        self.add_normed(down, gain)

    def add_normed(self, y, gain):
        nc, act, dve = self.nc, self.act, self.dve
        ss = self.rowstat[:, 0:T]
        for t in range(T):
            m = act.did(nc.scalar.activation(self.spare[:, T * D + t * D:T * D + (t + 1) * D], y[:, t, :], ACT.Square, accum_out=ss[:, t:t + 1]))
        dve.wait(m)
        self.inv_rms(ss, T, D)
        dve.wait(self.work_ld.now())
        for t in range(T):
            dve.seq(nc.vector.scalar_tensor_tensor(y[:, t, :], y[:, t, :], ss[:, t:t + 1], gain, ALU.mult, ALU.mult))
            dve.seq(nc.vector.tensor_tensor(self.x[:, t, :], self.x[:, t, :], y[:, t, :], ALU.add))
        self.meet()

    def head_rms_gate(self, col, z, func, gain):
        nc, act, dve = self.nc, self.act, self.dve
        tmp = [self.take(GW) for t in range(T)]
        heads = lambda a: a.rearrange("p (n d) -> p n d", d=HD2)
        ss = self.rowstat[:, 4:4 + T * H2]
        squared = [act.did(nc.scalar.activation(tmp[t], self.mixed[:, t, col:col + GW], ACT.Square)) for t in range(T)]
        gated = [act.did(nc.scalar.activation(z[:, t, :], z[:, t, :], func)) for t in range(T)]
        for t in range(T):
            dve.wait(squared[t])
            dve.did(nc.vector.tensor_reduce(ss[:, t * H2:(t + 1) * H2], heads(tmp[t]), AX.X, ALU.add))
        dve.wait(dve.now())
        self.inv_rms(ss, T * H2, HD2)
        marks = []
        for t in range(T):
            marks.append(dve.did(nc.vector.tensor_tensor(
                heads(tmp[t]), heads(self.mixed[:, t, col:col + GW]),
                ss[:, t * H2:(t + 1) * H2].unsqueeze(2).broadcast_to([P, H2, HD2]), ALU.mult)))
        if gain is not None:
            for t in range(T):
                dve.wait(marks[t])
                marks[t] = dve.did(nc.vector.tensor_tensor(tmp[t], tmp[t], gain, ALU.mult))
        for t in range(T):
            dve.wait(marks[t], gated[t])
            dve.did(nc.vector.tensor_tensor(self.mixed[:, t, col:col + GW], tmp[t], z[:, t, :], ALU.mult))
        dve.wait(dve.now())

    def pair(self, fm, j):
        return fm[:, ds(j, 1), :].rearrange("p a s -> p (a s)")

    def retention(self, l, pt):
        nc, pe, act, dve, pool = self.nc, self.pe, self.act, self.dve, self.pool
        self.fresh_work()
        decay = self.take(H2 * 2 * P)
        self.load_work(decay, self.A["const_decay"])
        qT, kT = [self.take(4 * S).rearrange("p (c s) -> p c s", c=4) for _ in range(2)]
        qs, ks = [self.take(2 * S).rearrange("p (c s) -> p c s", c=2) for _ in range(2)]
        sT = [self.take(3 * P) for _ in range(4)]
        self.prep([(lambda t, c=c: pt[:, t, c * GW:(c + 1) * GW].rearrange("p (n d) -> p n d", d=HD2), H2, HD2, None, False, True)
                   for c in range(2)])
        self.meet()
        self.transpose_tokens(pt[:, :, 0:GW], qT)
        self.meet()
        self.transpose_tokens(pt[:, :, GW:2 * GW], kT)
        self.meet()
        self.work_landed()
        dv = decay.rearrange("p (h n) -> p h n", h=H2)
        with self.loop(2, ("pe", "act", "dve", "pool"), **self.per["ret"]) as j:
            self.meet()
            act.did(nc.scalar.activation(qs, qT[:, ds(j * 2, 2), :], ACT.Copy))
            pe.wait(act.did(nc.scalar.activation(ks, kT[:, ds(j * 2, 2), :], ACT.Copy)))
            weighed = []
            for n in range(4):
                h, c, b = slice(n % 2 * HD2, (n % 2 + 1) * HD2), n // 2, self.ps[n]
                nc.tensor.matmul(b[:, 0:S], ks[h, c, 0:P], qs[h, c, 0:S], start=True, stop=True)
                dve.wait(pe.did(nc.tensor.matmul(b[:, S:S + P], ks[h, c, P:S], qs[h, c, P:S], start=True, stop=True)))
                d = dv[:, ds(j * 4 + n, 1), :].rearrange("p a n -> p (a n)")
                dve.did(nc.vector.tensor_tensor(sT[n][:, 0:S], b[:, 0:S], d, ALU.mult))
                weighed.append(dve.did(nc.vector.tensor_tensor(
                    sT[n][:, S:S + P], b[:, S:S + P], dv[:, ds(j * 4 + n, 1), 0:P].rearrange("p a n -> p (a n)"), ALU.mult)))
            for n in range(4):
                pe.wait(weighed[n])
                v = [pt[:, t, ds(j * 4 * HD2 + (2 * GW + n * HD2), HD2)] for t in range(T)]
                o = self.ps[4 + n]
                nc.tensor.matmul(o[:, 0:HD2], sT[n][:, 0:P], v[0], start=True, stop=True)
                nc.tensor.matmul(o[:, HD2:2 * HD2], sT[n][:, P:S], v[0], start=True, stop=False)
                act.wait(pe.did(nc.tensor.matmul(o[:, HD2:2 * HD2], sT[n][:, S:S + P], v[1], start=False, stop=True)))
                act.did(nc.scalar.activation(self.mixed[:, :, ds(j * 4 * HD2 + n * HD2, HD2)],
                                             o[:, 0:2 * HD2].rearrange("p (t d) -> p t d", t=T), ACT.Copy))
        self.meet()
        self.head_rms_gate(0, pt[:, :, 3 * GW:4 * GW], ACT.Silu, None)

    def cumulate(self, out, src, width):
        nc, dve = self.nc, self.dve
        n = src.shape[1]
        one = self.c("ones")[:, 0:1].broadcast_to([P, width])
        for k in range(0, n, width):
            dve.did(nc.vector.tensor_tensor_scan(out[:, k:k + width], one, src[:, k:k + width], 0.0, ALU.mult, ALU.add))
        dve.wait(dve.now())

    def hgrn(self, l, pt, pf):
        nc, pe, act, dve, pool = self.nc, self.pe, self.act, self.dve, self.pool
        self.fresh_work()
        flat = lambda a: a.rearrange("p c s -> p (c s)")
        q, f = flat(pf[:, 0:4, :]), flat(pf[:, 4:8, :])
        n, NT = 4 * S, 8 * GW + 2 * H2
        masks = self.take(LEVELS * P)
        self.load_work(masks, self.A["const_halves_T"])
        gain = self.load_row(self.A["hgrn_norm_w_2"][l], GW)
        lb, keep = self.rowstat[:, 24:28], self.rowstat[:, 28:32]
        E, cum, k, qd, kd = [self.take(n) for _ in range(5)]
        acc = self.take(16 * P)
        cross = self.take(H2 * P)
        if l == 1:
            dve.seq(nc.vector.tensor_tensor(lb, self.b2[1]["lb"], self.b2[0]["lb"], ALU.subtract))
            act.wait(dve.now())
            act.seq(nc.scalar.activation(lb, lb, ACT.Sigmoid))
            dve.wait(act.now())
            dve.seq(nc.vector.tensor_scalar(keep, lb, -1.0, 1.0, ALU.mult, ALU.add))
        over = lambda a: a.unsqueeze(2).broadcast_to([P, 4, S])
        v3 = lambda a: a.rearrange("p (c s) -> p c s", c=4)
        act.did(nc.scalar.activation(k, f, ACT.Sigmoid, scale=-1.0))
        act.seq(nc.scalar.activation(q, q, ACT.Silu))
        act.seq(nc.scalar.activation(E, f, ACT.Abs))
        act.seq(nc.scalar.activation(E, E, ACT.Exp, scale=-1.0))
        act.seq(nc.scalar.activation(E, E, ACT.Ln, bias=1.0))
        dve.wait(act.now())
        dve.did(nc.vector.tensor_scalar(q, q, HD2 ** -0.5, None, ALU.mult))
        if l == 0:
            dve.seq(nc.vector.scalar_tensor_tensor(f, f, 0.0, E, ALU.min, ALU.subtract))
        else:
            dve.did(nc.vector.tensor_scalar(qd, f, 0.0, None, ALU.min))
            dve.did(nc.vector.tensor_scalar(kd, f, 0.0, None, ALU.max))
            dve.seq(nc.vector.tensor_tensor(v3(k), v3(k), over(keep), ALU.mult))
            act.wait(dve.now())
            act.did(nc.scalar.activation(qd, qd, ACT.Exp))
            act.did(nc.scalar.activation(kd, kd, ACT.Exp, scale=-1.0))
            dve.wait(act.now())
            dve.seq(nc.vector.tensor_tensor(v3(kd), v3(kd), over(lb), ALU.mult))
            dve.seq(nc.vector.tensor_tensor(qd, qd, kd, ALU.add))
            dve.seq(nc.vector.tensor_scalar(qd, qd, 2.0 ** -60, None, ALU.max))
            act.wait(dve.now())
            act.seq(nc.scalar.activation(qd, qd, ACT.Ln))
            dve.wait(act.now())
            dve.seq(nc.vector.tensor_tensor(f, qd, E, ALU.subtract))
        self.cumulate(cum, f, P)
        dve.seq(nc.vector.memset(acc, 0.0))
        self.work_landed()
        self.meet()
        heads = [(h // 2, slice((h % 2) * HD2, (h % 2 + 1) * HD2)) for h in range(H2)]

        free_pt = [self.proj[:, 0:2048], self.proj[:, NT:NT + 2048]]
        bufs = [(E, qd, kd), (free_pt[0][:, 0:n], free_pt[0][:, n:2 * n], free_pt[1][:, 0:n])]
        exps, scaled, multiplied, merged = {}, {}, {}, {}

        def exponents(lev):
            B = 1 << lev
            Eb = bufs[lev % 2][0]
            blk = lambda a: a.rearrange("p (n b) -> p n b", b=2 * B)
            if lev >= 2:
                pool.wait(scaled[lev - 2])
            m = pool.did(nc.gpsimd.tensor_tensor(blk(Eb), blk(cum), blk(cum)[:, :, B - 1:B].broadcast_to([P, n // (2 * B), 2 * B]),
                                                 ALU.subtract))
            act.wait(m)
            act.seq(nc.scalar.activation(Eb, Eb, ACT.Abs))
            exps[lev] = act.did(nc.scalar.activation(Eb, Eb, ACT.Exp, scale=-1.0))

        def scale(lev):
            Eb, qb, kb = bufs[lev % 2]
            dve.wait(exps[lev])
            if lev >= 1:
                dve.wait(multiplied[lev - 2])
            dve.did(nc.vector.tensor_tensor(qb, q, Eb, ALU.mult))
            scaled[lev] = dve.did(nc.vector.tensor_tensor(kb, k, Eb, ALU.mult))

        def multiply(lev, kk, qq):
            k3, q3 = v3(kk), v3(qq)
            for g in range(4):
                b = self.ps[4 * (lev % 2) + g]
                if lev >= 1:
                    pe.wait(merged[lev - 2, g])
                for i in range(4):
                    c, h = heads[4 * (g // 2) + g % 2 + 2 * (i // 2)]
                    t = i % 2
                    ins = nc.tensor.matmul(b[:, i * P:(i + 1) * P], k3[h, c, t * P:(t + 1) * P], q3[h, c, t * P:(t + 1) * P],
                                           start=True, stop=True)
                multiplied[lev, g] = multiplied[lev] = pe.did(ins)

        def merge(lev, mask):
            m = mask.bitcast(mybir.dt.uint32).unsqueeze(1).broadcast_to([P, 4, P])
            for g in range(4):
                dve.wait(multiplied[lev, g], *([merged[lev - 1, g]] if lev >= 0 else []))
                merged[lev, g] = dve.did(nc.vector.copy_predicated(
                    acc[:, g * 512:(g + 1) * 512].rearrange("p (i s) -> p i s", i=4), m,
                    self.ps[4 * (lev % 2) + g][:, :].rearrange("p (i s) -> p i s", i=4)))

        multiply(-1, k, q)
        for w in range(LEVELS + 2):
            if w < LEVELS:
                exponents(w)
            if 0 <= w - 1 < LEVELS:
                scale(w - 1)
                pe.wait(scaled[w - 1])
                multiply(w - 1, bufs[(w - 1) % 2][2], bufs[(w - 1) % 2][1])
            if w == 0:
                merge(-1, self.c("ident"))
            if 0 <= w - 2 < LEVELS:
                merge(w - 2, masks[:, (w - 2) * P:(w - 1) * P])
        dve.wait(act.now())
        c3, E3, qd3, kd3 = v3(cum), v3(E), v3(qd), v3(kd)
        dve.seq(nc.vector.tensor_tensor(E3[:, :, 0:P], c3[:, :, P - 1:P].broadcast_to([P, 4, P]), c3[:, :, 0:P], ALU.subtract))
        dve.seq(nc.vector.tensor_copy(E3[:, :, P:S], c3[:, :, P:S]))
        act.wait(dve.now())
        act.seq(nc.scalar.activation(E, E, ACT.Exp))
        dve.wait(act.now(), pe.now())
        dve.did(nc.vector.tensor_tensor(kd3[:, :, 0:P], v3(k)[:, :, 0:P], E3[:, :, 0:P], ALU.mult))
        dve.seq(nc.vector.tensor_tensor(qd3[:, :, P:S], v3(q)[:, :, P:S], E3[:, :, P:S], ALU.mult))
        pe.wait(dve.now())
        for g in range(2):
            for i in range(4):
                c, h = heads[g + 2 * i]
                ins = nc.tensor.matmul(self.ps[6 + g][:, i * P:(i + 1) * P], kd3[h, c, 0:P], qd3[h, c, P:S], start=True, stop=True)
            act.wait(pe.did(ins))
            pe.wait(act.did(nc.scalar.activation(cross[:, g * 512:(g + 1) * 512], self.ps[6 + g][:, :], ACT.Copy)))
        i0 = 4 * GW
        for t in range(T):
            o = self.ps[t]
            for h in range(H2):
                v = [pt[:, c, i0 + h * HD2:i0 + (h + 1) * HD2] for c in range(T)]
                at = 4 * (2 * (h // 4) + h % 2) + 2 * ((h % 4) // 2) + t
                a = acc[:, at * P:(at + 1) * P]
                x = cross[:, (4 * (h % 2) + h // 2) * P:(4 * (h % 2) + h // 2 + 1) * P]
                ins = nc.tensor.matmul(o[:, h * HD2:(h + 1) * HD2], a, v[t], start=True, stop=(t == 0))
                if t:
                    ins = nc.tensor.matmul(o[:, h * HD2:(h + 1) * HD2], x, v[0], start=False, stop=True)
            act.wait(pe.did(ins))
            act.did(nc.scalar.activation(self.mixed[:, t, GW:2 * GW], o[:, :], ACT.Copy))
        self.meet()
        self.head_rms_gate(GW, pt[:, :, 5 * GW:6 * GW], ACT.Sigmoid, gain)

    def mlstm(self, l, pt, pf):
        nc, pe, act, dve, pool = self.nc, self.pe, self.act, self.dve, self.pool
        q_ = self.b2[l]
        self.fresh_work()
        gain = self.load_row(self.A["mlstm_norm_w_2"][l], GW)
        self.sm_s, self.sm_e, self.sm_eT, self.sm_stat = self.take(DEPTH * S), self.take(DEPTH * S), self.take(2 * S), self.take(8 * DEPTH)
        gates = self.take(4 * T * H2).rearrange("p (k t h) -> p k t h", k=4, t=T)
        li, lf, cum, G = [gates[:, k, :, :] for k in range(4)]
        qs, ks = [self.take(2 * S).rearrange("p (c s) -> p c s", c=2) for _ in range(2)]
        gs, fs = self.take(T * 4), self.take(T * 4)
        for c in range(8):
            src, dst = pf[:, 8 + c, :], pf[:, c, :]
            w = [x[:, c:c + 1] for x in q_["conv"]]
            dve.seq(nc.vector.tensor_scalar(dst, src, w[3], q_["mlstm_conv_b_2"][:, c:c + 1], ALU.mult, ALU.add))
            for d in range(1, 4):
                dve.seq(nc.vector.scalar_tensor_tensor(dst[:, d:S], src[:, 0:S - d], w[3 - d], dst[:, d:S], ALU.mult, ALU.add))
        act.wait(dve.now())
        qk = pf[:, 0:8, :].rearrange("p c s -> p (c s)")
        act.seq(nc.scalar.activation(qk, qk, ACT.Silu))
        raw = pt[:, :, 8 * GW:8 * GW + 2 * H2]
        row = lambda a: a.unsqueeze(1).broadcast_to([P, T, H2])
        dve.did(nc.vector.tensor_tensor(li, raw[:, :, 0:H2], row(q_["ib"]), ALU.add))
        dve.seq(nc.vector.tensor_tensor(lf, raw[:, :, H2:2 * H2], row(q_["fb"]), ALU.add))
        act.wait(dve.now())
        act.seq(nc.scalar.activation(G, lf, ACT.Abs))
        act.seq(nc.scalar.activation(G, G, ACT.Exp, scale=-1.0))
        act.seq(nc.scalar.activation(G, G, ACT.Ln, bias=1.0))
        dve.wait(act.now())
        dve.seq(nc.vector.scalar_tensor_tensor(lf, lf, 0.0, G, ALU.min, ALU.subtract))
        pe.wait(dve.now())
        nc.tensor.matmul(self.ps[2][:, 0:H2], self.c("upto_T"), lf[:, 0, :], start=True, stop=True)
        nc.tensor.matmul(self.ps[2][:, H2:2 * H2], self.c("ones"), lf[:, 0, :], start=True, stop=False)
        dve.wait(pe.did(nc.tensor.matmul(self.ps[2][:, H2:2 * H2], self.c("upto_T"), lf[:, 1, :], start=False, stop=True)))
        dve.seq(nc.vector.tensor_copy(cum, self.ps[2][:, 0:2 * H2].rearrange("p (t h) -> p t h", t=T)))
        dve.seq(nc.vector.tensor_tensor(G, li, cum, ALU.subtract))
        self.meet()
        st3 = lambda a: a.rearrange("p (t e) -> p t e", t=T)
        with self.loop(2, ("pe", "act", "dve", "pool"), **self.per["mlstm"]) as j:
            self.meet()
            act.did(nc.scalar.activation(qs, pf[:, ds(j * 2, 2), :], ACT.Copy))
            act.did(nc.scalar.activation(ks, pf[:, ds(j * 2 + 4, 2), :], ACT.Copy))
            dve.did(nc.vector.tensor_copy(st3(gs), G[:, :, ds(j * 4, 4)]))
            dve.seq(nc.vector.tensor_copy(st3(fs), cum[:, :, ds(j * 4, 4)]))
            pe.wait(act.now(), dve.now())
            units = []
            for c in range(2):
                for e in range(2):
                    h, n = slice(e * HD2, (e + 1) * HD2), 2 * c + e
                    for t in range(T):
                        units.append(dict(
                            mlstm=True, qT=qs[h, c, t * P:(t + 1) * P], kT=ks[h, c, 0:(t + 1) * P], keys=(t + 1) * P,
                            mask=self.causal(t), gates=[st3(gs)[:, i, n:n + 1] for i in range(t + 1)],
                            F=st3(fs)[:, t, n:n + 1], dv=HD2,
                            v=[pt[:, i, ds(j * 4 * HD2 + (6 * GW + n * HD2), HD2)] for i in range(t + 1)],
                            out=lambda O, r, t=t, n=n: self.scaled(
                                self.mixed[:, t, ds(j * 4 * HD2 + (2 * GW + n * HD2), HD2)], O, r)))
            self.attention(units)
        self.meet()
        self.work_landed()
        self.head_rms_gate(2 * GW, pt[:, :, 7 * GW:8 * GW], ACT.Sigmoid, gain)

    def rwkv(self, l, pt, pf):
        nc, pe, act, dve, pool = self.nc, self.pe, self.act, self.dve, self.pool
        q_, A = self.b2[l], self.A
        self.fresh_work()
        lora_gup = self.take(2 * GW)
        lora, g_up = lora_gup[:, 0:GW], lora_gup[:, GW:2 * GW]
        self.load_work(lora[0:64, :], A["rwkv_w_up_2"][l])
        self.load_work(lora[64:128, :], A["rwkv_a_up_2"][l])
        self.load_work(g_up, A["rwkv_g_up_2"][l])
        masks = self.take(2 * LEVELS * P).rearrange("p (k n) -> p k n", k=2)
        self.load_work(masks[:, 0, :], A["const_halves"])
        self.load_work(masks[:, 1, :], A["const_halves_T"])
        vt = self.take(T * GW).rearrange("p (t n) -> p t n", t=T)
        gt = self.take(T * GW).rearrange("p (t n) -> p t n", t=T)
        col = lambda a, c: a[:, c:c + 1]
        over = lambda a: a.unsqueeze(2).broadcast_to([P, 4, S])
        p, d = pf[:, 16:30, :], pf[:, 0:14, :]
        dve.did(nc.vector.tensor_tensor(d[:, :, 1:S], p[:, :, 0:S - 1], p[:, :, 1:S], ALU.subtract))
        dve.seq(nc.vector.tensor_scalar(d[:, :, 0:1], p[:, :, 0:1], -1.0, None, ALU.mult))
        for c in range(14):
            dve.did(nc.vector.scalar_tensor_tensor(p[:, c, :], d[:, c, :], col(q_["rwkv_mu_2"], c), p[:, c, :], ALU.mult, ALU.add))
        dve.wait(dve.now())
        r, k, v, wa, gd = pf[:, 16:20, :], pf[:, 20:24, :], pf[:, 24:28, :], pf[:, 28, :], pf[:, 29, :]
        lw, a, kk, L = pf[:, 0:4, :], pf[:, 4:8, :], pf[:, 8:12, :], pf[:, 12:16, :]
        act.wait(dve.now())
        act.did(nc.scalar.activation(wa[0:64, :], wa[0:64, :], ACT.Tanh))
        act.seq(nc.scalar.activation(gd, gd, ACT.Sigmoid))
        self.work_landed()
        self.meet()
        if l == 1:
            vd = self.take(4 * 32).rearrange("p (c n) -> p c n", c=4)
            vu, low_v, mix = self.take(GW), self.take(S), self.take(S)
            self.load_work(vd, A["rwkv_v_down_2"][0].rearrange("(c p) n -> p c n", p=P))
            self.load_work(vu[0:32, :], A["rwkv_v_up_2"][0])
            self.work_landed()
            for c in range(4):
                ins = nc.tensor.matmul(self.ps[2][0:32, 0:S], vd[:, c, :], v[:, c, :], start=(c == 0), stop=(c == 3))
            act.wait(pe.did(ins))
            pe.wait(act.did(nc.scalar.activation(low_v[0:32, :], self.ps[2][0:32, 0:S], ACT.Copy)))
            for c in range(4):
                pe.wait(act.now())
                act.wait(pe.did(nc.tensor.matmul(self.ps[3][:, 0:S], vu[0:32, c * P:(c + 1) * P], low_v[0:32, :], start=True, stop=True)))
                act.wait(dve.now())
                dve.wait(act.did(nc.scalar.activation(mix, self.ps[3][:, 0:S], ACT.Sigmoid, bias=col(q_["v0"], c))))
                vf = self.v_first[:, c * S:(c + 1) * S]
                dve.seq(nc.vector.tensor_tensor(vf, vf, v[:, c, :], ALU.subtract))
                dve.seq(nc.vector.tensor_tensor(vf, vf, mix, ALU.mult))
                dve.seq(nc.vector.tensor_tensor(v[:, c, :], v[:, c, :], vf, ALU.add))
        else:
            dve.seq(nc.vector.tensor_copy(self.v_first, v.rearrange("p c s -> p (c s)")))
        pe.wait(act.now())
        for c in range(4):
            b = self.ps[4 + c]
            b2 = self.ps[c]
            nc.tensor.matmul(b[:, 0:S], lora[0:64, c * P:(c + 1) * P], wa[0:64, :], start=True, stop=True)
            act.wait(pe.did(nc.tensor.matmul(b2[:, 0:S], lora[64:128, c * P:(c + 1) * P], wa[64:128, :], start=True, stop=True)))
            act.did(nc.scalar.activation(lw[:, c, :], b[:, 0:S], ACT.Sigmoid, bias=col(q_["rwkv_w0_2"], c)))
            act.did(nc.scalar.activation(a[:, c, :], b2[:, 0:S], ACT.Sigmoid, bias=col(q_["rwkv_a0_2"], c)))
            dve.did(nc.vector.tensor_scalar(kk[:, c, :], k[:, c, :], col(q_["rwkv_k_k_2"], c), None, ALU.mult))
        pe.wait(act.now())
        for t in range(T):
            act.wait(pe.did(nc.tensor.matmul(self.ps[t][:, :], gd[:, t * P:(t + 1) * P], g_up, start=True, stop=True)))
            act.did(nc.scalar.activation(gt[:, t, :], self.ps[t][:, :], ACT.Copy))
        self.meet()
        f3 = lambda x: x.rearrange("p c s -> p (c s)")
        dve.did(nc.vector.tensor_scalar(lw, lw, -DECAY_SCALE, None, ALU.mult))
        before_sq = self.work_at, self.spare_at
        sq = self.take(4 * S)
        act.seq(nc.scalar.activation(sq, f3(kk), ACT.Square))
        pe.wait(act.now())
        for g in range(2):
            m = pe.did(nc.tensor.matmul(self.ps[2 + g][:, :], self.c("pair_ones"), sq[:, g * 512:(g + 1) * 512], start=True, stop=True))
            act.wait(m)
        for g in range(2):
            act.did(nc.scalar.activation(sq[:, g * 512:(g + 1) * 512], self.ps[2 + g][:, :], ACT.Sqrt))
        dve.wait(act.now())
        dve.seq(nc.vector.tensor_scalar(sq, sq, 1e-12, None, ALU.max))
        dve.seq(nc.vector.reciprocal(sq, sq))
        dve.seq(nc.vector.tensor_tensor(f3(kk), f3(kk), sq, ALU.mult))
        for c in range(4):
            dve.did(nc.vector.tensor_scalar(sq[:, c * S:(c + 1) * S], a[:, c, :], 1.0, col(q_["rwkv_k_a_2"], c), ALU.subtract, ALU.mult))
        dve.wait(dve.now())
        dve.seq(nc.vector.scalar_tensor_tensor(f3(k), sq, 1.0, f3(k), ALU.add, ALU.mult))
        dve.seq(nc.vector.tensor_tensor(sq, f3(r), f3(k), ALU.mult))
        for c in range(4):
            dve.did(nc.vector.tensor_scalar(sq[:, c * S:(c + 1) * S], sq[:, c * S:(c + 1) * S], col(q_["rwkv_r_k_2"], c), None, ALU.mult))
        bonus = self.take(T * H2).rearrange("p (t h) -> p t h", t=T)
        pe.wait(dve.now())
        for t in range(T):
            for c in range(4):
                ins = nc.tensor.matmul(self.ps[2][:, t * H2 + 2 * c:t * H2 + 2 * c + 2], sq[:, c * S + t * P:c * S + (t + 1) * P],
                                       self.c("pair_pick"), start=True, stop=True)
        dve.wait(pe.did(ins))
        dve.seq(nc.vector.tensor_copy(bonus, self.ps[2][:, 0:T * H2].rearrange("p (t h) -> p t h", t=T)))
        dve.seq(nc.vector.tensor_tensor(f3(a), f3(a), f3(kk), ALU.mult))
        self.cumulate(f3(L), f3(lw), P)
        L4 = f3(L).rearrange("p (n s) -> p n s", s=P)
        ends = self.rowstat[:, 32:64].rearrange("p (k n) -> p k n", k=4)
        dve.did(nc.vector.tensor_copy(ends[:, 0, :].unsqueeze(2), L4[:, :, P // 2 - 1:P // 2]))
        dve.seq(nc.vector.tensor_copy(ends[:, 1, :].unsqueeze(2), L4[:, :, P - 1:P]))
        dve.seq(nc.vector.tensor_tensor(L4, L4, ends[:, 0, :].unsqueeze(2).broadcast_to([P, 8, P]), ALU.subtract))
        mid = ends[:, 0, :].rearrange("p (c t) -> p c t", t=T)
        end = ends[:, 1, :].rearrange("p (c t) -> p c t", t=T)
        fac = ends[:, 2, 0:4].unsqueeze(2)
        dve.seq(nc.vector.tensor_tensor(fac, end[:, :, 0:1], mid[:, :, 0:1], ALU.subtract))
        dve.seq(nc.vector.tensor_tensor(fac, fac, mid[:, :, 1:2], ALU.add))
        act.wait(dve.now())
        act.seq(nc.scalar.activation(ends[:, 2, 0:4], ends[:, 2, 0:4], ACT.Exp))
        self.meet()
        for t in range(T):
            for c in range(4):
                ins = nc.tensor.transpose(self.ps[2 + t][:, c * P:(c + 1) * P], v[:, c, t * P:(t + 1) * P], self.c("ident"))
            act.wait(pe.did(ins))
            act.did(nc.scalar.activation(vt[:, t, :], self.ps[2 + t][:, :], ACT.Copy))
        self.meet()
        self.work_at, self.spare_at = before_sq
        bonus2 = self.take(T * H2).rearrange("p (t h) -> p t h", t=T)
        dve.seq(nc.vector.tensor_copy(bonus2, bonus))
        units = [(t, c, e) for t in range(T) for c in range(2) for e in range(2)]
        N = len(units)
        free_at = [0]

        def over_pt(cols):
            free_at[0] += cols
            assert free_at[0] <= T * (8 * GW + 2 * H2)
            return self.proj[:, free_at[0] - cols:free_at[0]]
        M4 = [over_pt(4 * P) for _ in units]
        TT = [over_pt(2 * P) for _ in units]
        Y_all = over_pt(N * P)
        Y = [Y_all[:, n * P:(n + 1) * P] for n in range(N)]
        RU = [over_pt(2 * HD2) for _ in units]
        kr = lora_gup.rearrange("p (c t k s) -> p c t k s", c=2, t=T, k=2)
        bt, kt = [self.take(2 * S).rearrange("p (c s) -> p c s", c=2) for _ in range(2)]
        eP, eN, shifted = self.take(2 * S), self.take(2 * S), Y_all[:, 0:2 * S]
        bk = self.take(4 * P)
        S1 = self.take(2 * HD2)
        vs = self.take(T * 2 * P).rearrange("p (t n) -> p t n", t=T)
        uint = mybir.dt.uint32
        before_upto = self.take(2 * P)
        dve.did(nc.vector.tensor_copy(before_upto[:, 0:P], self.c("before_T")))
        dve.did(nc.vector.tensor_copy(before_upto[:, P:2 * P], self.c("upto_T")))
        both_masks = before_upto.unsqueeze(1).broadcast_to([P, 2, 2 * P])
        with self.loop(2, ("pe", "act", "dve", "pool"), **self.per["rwkv"]) as j:
            self.meet()
            two = lambda fm: fm[:, ds(j * 2, 2), :]
            v3 = lambda x: x.rearrange("p (c s) -> p c s", c=2)
            v4 = lambda x: x.rearrange("p c (t s) -> p c t s", t=T)
            pool.hold(self.passed)
            eyes = [pool.did(nc.gpsimd.tensor_copy(TT[n].rearrange("p (k s) -> p k s", k=2),
                                                   self.c("ident").unsqueeze(1).broadcast_to([P, 2, P]))) for n in range(N)]
            grown = act.did(nc.scalar.activation(v3(eP), two(L), ACT.Exp))
            shrunk = act.did(nc.scalar.activation(v3(eN), two(L), ACT.Exp, scale=-1.0))
            act.wait(dve.did(nc.vector.tensor_tensor(v3(shifted), two(L), two(lw), ALU.subtract)))
            before = act.did(nc.scalar.activation(shifted, shifted, ACT.Exp))
            act.did(nc.scalar.activation(vs, vt[:, :, ds(j * 2 * P, 2 * P)], ACT.Copy))
            dve.wait(grown)
            dve.did(nc.vector.tensor_tensor(kr[:, :, :, 1, :], v4(v3(eP)), v4(two(r)), ALU.mult))
            dve.wait(shrunk)
            dve.did(nc.vector.tensor_tensor(bt, v3(eN), two(a), ALU.mult))
            pe.wait(dve.did(nc.vector.tensor_tensor(kt, v3(eN), two(k), ALU.mult)))
            for c in range(2):
                nc.tensor.transpose(self.ps[7][:, 2 * c * P:(2 * c + 1) * P], bt[:, c, 0:P], self.c("ident"))
                ins = nc.tensor.transpose(self.ps[7][:, (2 * c + 1) * P:(2 * c + 2) * P], kt[:, c, 0:P], self.c("ident"))
            act.wait(pe.did(ins))
            turned = act.did(nc.scalar.activation(bk, self.ps[7][:, :], ACT.Copy))
            dve.wait(before)
            pe.wait(dve.did(nc.vector.scalar_tensor_tensor(kr[:, :, :, 0, :], v4(v3(shifted)), -1.0, v4(two(kk)), ALU.mult, ALU.mult)))
            head = lambda e: slice(e * HD2, (e + 1) * HD2)
            masked = []
            for n, (t, c, e) in enumerate(units):
                h, tok = head(e), slice(t * P, (t + 1) * P)
                b = self.ps[n]
                rhs = kr[h, c, t, :, :].rearrange("p k s -> p (k s)")
                if n == N - 1:
                    pe.wait(turned)
                nc.tensor.matmul(b[:, 0:S], bt[h, c, tok], rhs, start=True, stop=True)
                dve.wait(pe.did(nc.tensor.matmul(b[:, S:2 * S], kt[h, c, tok], rhs, start=True, stop=True)), eyes[n])
                dve.did(nc.vector.tensor_tensor(M4[n].rearrange("p (g n) -> p g n", g=2), b[:, :].rearrange("p (g n) -> p g n", g=2),
                                                both_masks, ALU.mult))
                dve.hold(self.passed)
                masked.append(dve.did(nc.vector.copy_predicated(TT[n][:, P:2 * P], masks[:, 1, 0:P].bitcast(uint), b[:, 0:P])))
            grown = []
            for n, (t, c, e) in enumerate(units):
                pe.wait(masked[n])
                dve.wait(pe.did(nc.tensor.matmul(self.ps[n][:, 0:P], kr[head(e), c, t, 0, :], bt[head(e), c, t * P:(t + 1) * P],
                                                 start=True, stop=True)))
                dve.hold(self.passed)
                grown.append(dve.did(nc.vector.copy_predicated(TT[n][:, 0:P], masks[:, 0, 0:P].bitcast(uint), self.ps[n][:, 0:P])))
            for lev in range(1, LEVELS):
                lo = P if lev == LEVELS - 1 else 0
                copied = []
                for n in range(N):
                    pe.wait(grown[n])
                    act.wait(pe.did(nc.tensor.matmul(self.ps[n][:, 0:P], M4[n][:, 0:P], TT[n][:, 0:P], start=True, stop=True)))
                    copied.append(act.did(nc.scalar.activation(Y[n], self.ps[n][:, 0:P], ACT.Copy)))
                for n in range(N):
                    b = self.ps[n]
                    pe.wait(copied[n])
                    if not lo:
                        nc.tensor.matmul(b[:, P:2 * P], TT[n][:, P:2 * P], Y[n], start=True, stop=True)
                    dve.wait(pe.did(nc.tensor.matmul(b[:, 2 * P:3 * P], Y[n], TT[n][:, P:2 * P], start=True, stop=True)))
                    half = lambda x: x.rearrange("p (k s) -> p k s", s=P)
                    dve.hold(self.passed)
                    grown[n] = dve.did(nc.vector.copy_predicated(
                        half(TT[n][:, lo:2 * P]), masks[:, lo // P:2, lev * P:(lev + 1) * P].bitcast(uint),
                        half(b[:, P + lo:3 * P])))
            for t in range(T):
                these = [(n, c, e) for n, (tt, c, e) in enumerate(units) if tt == t]
                values = lambda c, e: vs[:, t, c * P + e * HD2:c * P + (e + 1) * HD2]
                marks = {}
                for n, c, e in these:
                    b = self.ps[n]
                    pe.wait(grown[n])
                    ins = nc.tensor.matmul(b[:, 0:HD2], M4[n][:, S:S + P], values(c, e), start=True, stop=(t == 0))
                    if t:
                        pe.wait(stated[c, e])
                        ins = nc.tensor.matmul(b[:, 0:HD2], kr[head(e), c, 1, 0, :], S1[head(e), c * HD2:(c + 1) * HD2], start=False, stop=True)
                    dve.wait(pe.did(ins))
                    marks[n] = dve.did(nc.vector.tensor_copy(RU[n][:, 0:HD2], b[:, 0:HD2]))
                for n, c, e in these:
                    b = self.ps[n]
                    pe.wait(marks[n])
                    act.wait(pe.did(nc.tensor.matmul(b[:, HD2:2 * HD2], TT[n][:, P:2 * P], RU[n][:, 0:HD2], start=True, stop=True)))
                    marks[n] = act.did(nc.scalar.activation(RU[n][:, HD2:2 * HD2], b[:, HD2:2 * HD2], ACT.Copy))
                if t == 0:
                    stated = {}
                for n, c, e in these:
                    b, h, U = self.ps[n], head(e), RU[n][:, HD2:2 * HD2]
                    pe.wait(marks[n])
                    if t == 0:
                        s_ = b[h, 3 * HD2:4 * HD2]
                        nc.tensor.matmul(s_, bk[:, 2 * c * P + e * HD2:2 * c * P + (e + 1) * HD2], U, start=True, stop=False)
                        dve.wait(pe.did(nc.tensor.matmul(s_, bk[:, (2 * c + 1) * P + e * HD2:(2 * c + 1) * P + (e + 1) * HD2],
                                                         values(c, e), start=False, stop=True)))
                        stated[c, e] = dve.did(nc.vector.tensor_scalar(S1[h, c * HD2:(c + 1) * HD2], s_,
                                                                       ends[h, 2, ds(j * 2 + c, 1)], None, ALU.mult))
                        pe.wait(stated[c, e])
                for n, c, e in these:
                    y, h, U = self.ps[n][:, 2 * HD2:3 * HD2], head(e), RU[n][:, HD2:2 * HD2]
                    nc.tensor.matmul(y, M4[n][:, S + P:2 * S], values(c, e), start=True, stop=False)
                    if t:
                        nc.tensor.matmul(y, kr[h, c, 1, 1, :], S1[h, c * HD2:(c + 1) * HD2], start=False, stop=False)
                    act.wait(pe.did(nc.tensor.matmul(y, M4[n][:, P:2 * P], U, start=False, stop=True)))
                    act.did(nc.scalar.activation(self.mixed[:, t, ds(j * 4 * HD2 + (3 * GW + (2 * c + e) * HD2), HD2)], y, ACT.Copy))
        self.meet()
        row_w, row_b = M4[0], M4[1]
        self.work_ld.count(nc.scalar.dma_start(row_w, A["rwkv_ln_w_2"][l].partition_broadcast(P)))
        self.work_ld.count(nc.scalar.dma_start(row_b, A["rwkv_ln_b_2"][l].partition_broadcast(P)))
        self.work_landed()
        tmp = M4[2].rearrange("p (n d) -> p n d", d=HD2)
        st = self.rowstat[:, 4:4 + H2]
        over = lambda x: x.unsqueeze(2).broadcast_to([P, H2, HD2])
        for t in range(T):
            y2 = self.mixed[:, t, 3 * GW:4 * GW]
            y = y2.rearrange("p (n d) -> p n d", d=HD2)
            v8 = vt[:, t, :].rearrange("p (n d) -> p n d", d=HD2)
            dve.seq(nc.vector.tensor_reduce(st, y, AX.X, ALU.add))
            dve.seq(nc.vector.tensor_scalar(st, st, 1.0 / HD2, None, ALU.mult))
            dve.seq(nc.vector.tensor_tensor(y, y, over(st), ALU.subtract))
            dve.seq(nc.vector.tensor_tensor(tmp, y, y, ALU.mult))
            dve.seq(nc.vector.tensor_reduce(st, tmp, AX.X, ALU.add))
            self.inv_rms(st, H2, HD2, LN_EPS)
            dve.seq(nc.vector.tensor_tensor(y, y, over(st), ALU.mult))
            dve.seq(nc.vector.tensor_tensor(y2, y2, row_w, ALU.mult))
            dve.seq(nc.vector.tensor_tensor(y2, y2, row_b, ALU.add))
            dve.seq(nc.vector.tensor_tensor(tmp, v8, over(bonus2[:, t, :]), ALU.mult))
            dve.seq(nc.vector.tensor_tensor(y, y, tmp, ALU.add))
            dve.seq(nc.vector.tensor_tensor(y2, y2, gt[:, t, :], ALU.mult))
        self.meet()

    def finish(self):
        nc = self.nc
        for q in (self.pe, self.act, self.dve, self.pool):
            nc.sync.wait_ge(*q.now())
        for t in range(T):
            self.outs.count(nc.sync.dma_start(self.out_dram[0, t * P:(t + 1) * P, :], self.x[:, t, :]))
        nc.sync.wait_ge(*self.outs.now())


def build(nc, A, consts, out):
    Program(nc, A, consts, out).build()


_INS = ['x', 'mem', 'norm_gain', 'mem_norm_gain', 'mem_w_kv', 'mem_qk_gain', 'w_out', 'even_w_in', 'nsa_qk_gain',
        'nsa_cmp_pos', 'nsa_cmp_w1', 'nsa_cmp_w2', 'diff_qk_gain', 'diff_lambda', 'diff_subln_gain', 'odd_w_in',
        'dsa_qk_gain', 'w_in_2', 'w_out_2', 'norm_pre_mix_2', 'norm_post_mix_2', 'norm_pre_ffn_2', 'norm_post_ffn_2',
        'w_ffn_gate_2', 'w_ffn_up_2', 'w_ffn_down_2', 'hgrn_lb_logits_2', 'hgrn_norm_w_2', 'mlstm_conv_w_2',
        'mlstm_conv_b_2', 'mlstm_i_bias_2', 'mlstm_f_bias_2', 'mlstm_norm_w_2', 'rwkv_mu_2', 'rwkv_w0_2',
        'rwkv_w_up_2', 'rwkv_a0_2', 'rwkv_a_up_2', 'rwkv_g_up_2', 'rwkv_k_k_2', 'rwkv_k_a_2', 'rwkv_r_k_2',
        'rwkv_ln_w_2', 'rwkv_ln_b_2', 'rwkv_v0_2', 'rwkv_v_down_2', 'rwkv_v_up_2']


def kernel(**inputs):
    import numpy as _np
    import concourse.bacc as _bacc
    from concourse import mybir as _mybir
    from concourse.bass_utils import run_bass_kernel_spmd as _run

    nc = _bacc.Bacc("TRN2", target_bir_lowering=False, num_devices=1, dynamic_dma_scratch_size=1024)
    small, offs, halves_T, halves, decay = shape_constants()
    arrays, A = {}, {}
    tables = dict(const_small=small, const_halves_T=halves_T, const_halves=halves, const_decay=decay)
    for name, a in [(n, inputs[n]) for n in _INS] + list(tables.items()):
        a = _np.ascontiguousarray(a)
        arrays[f"in_{name}_dram"] = a
        A[name] = nc.dram_tensor(f"in_{name}_dram", a.shape, _mybir.dt.from_np(a.dtype), kind="ExternalInput").ap()
    out = nc.dram_tensor("out_0_dram", (1, S, D), _mybir.dt.float32, kind="ExternalOutput").ap()
    build(nc, A, dict(small=small, offs=offs), out)
    r = _run(nc, [arrays], core_ids=[0])
    return r.results[0]["out_0_dram"]
```
